# Optimizing a Trainium2 kernel written in Bass

```python
import math
import jax, jax.numpy as jnp
from jax import lax
import numpy as np

D_MODEL = 1024
BATCH = 1
SEQ = 1024
DEPTH = 1
DEC_BATCH = 8
DEC_SEQ = 4
PAST_LEN = 2048
PAGE_SIZE = 128

EXPAND = 2
D_MIX = EXPAND * D_MODEL
D_ATTN = D_MIX // 2
D_CONV = D_MIX - D_ATTN
HEAD_DIM = 64
N_HEADS = D_ATTN // HEAD_DIM
N_KV = 2
HPG = N_HEADS // N_KV
D_KV = N_KV * HEAD_DIM
BLK = 64
N_SEL = 16
WINDOW = 512
CMP_HID = 2 * HEAD_DIM
CONV_W = 3
N_BUCKETS = 32
MAX_DIST = 128
Q_BLOCK = 128
EPS = 1e-6
NEG = -1e30
PROJ_SIZES = (D_ATTN, D_KV, D_KV, D_KV, D_KV, D_KV, D_KV, 3 * N_HEADS, D_CONV, D_CONV, D_CONV, D_MIX)
D_IN = sum(PROJ_SIZES)

kernel_name = "hymba_nsa_shortconv_adaln_step"

def rmsnorm(x, g):
    xf = x.astype(jnp.float32)
    y = xf * lax.rsqrt(jnp.mean(xf * xf, axis=-1, keepdims=True) + EPS)
    return (y * g.astype(jnp.float32)).astype(x.dtype)

def t5_bucket(dist):
    n = jnp.maximum(dist, 0)
    max_exact = N_BUCKETS // 2
    nf = jnp.maximum(n, max_exact).astype(jnp.float32)
    large = max_exact + (jnp.log(nf / max_exact) / math.log(MAX_DIST / max_exact)
                         * (N_BUCKETS - max_exact)).astype(jnp.int32)
    return jnp.where(n < max_exact, n, jnp.minimum(large, N_BUCKETS - 1))

def masked_softmax(logits, mask):
    p = jax.nn.softmax(jnp.where(mask, logits.astype(jnp.float32), NEG), axis=-1)
    return p * jnp.any(mask, axis=-1, keepdims=True)

def split_proj(u):
    offs = np.cumsum((0,) + PROJ_SIZES)
    return [u[..., int(offs[i]):int(offs[i + 1])] for i in range(len(PROJ_SIZES))]

def modulate_project(x, c, ada_w, ada_b, norm_g, w_in):
    shift, scale, gate = jnp.split(c @ ada_w + ada_b, 3, axis=-1)
    h = rmsnorm(x, norm_g) * (1 + scale[:, None, :]) + shift[:, None, :]
    return split_proj(h @ w_in), gate

def kv_heads(t):
    return t.reshape(t.shape[0], t.shape[1], N_KV, HEAD_DIM)

def compress(kv, pe, w1, w2):
    b, l, g, d = kv.shape
    blocks = kv.reshape(b, l // BLK, BLK, g, d) + pe[None, None, :, None, :]
    flat = blocks.transpose(0, 1, 3, 2, 4).reshape(b, l // BLK, g, BLK * d)
    return jax.nn.silu(flat @ w1) @ w2

def to_blocks(k):
    b, l, g, d = k.shape
    return k.reshape(b, l // BLK, BLK, g, d).transpose(0, 3, 1, 2, 4)

def nsa_attend(q, gts, q_pos, k_cmp, v_cmp, k_sel, v_sel, k_win, v_win, win_pos, rel_bias):
    qs = q * (HEAD_DIM ** -0.5)
    nb = k_cmp.shape[1]
    blk_start = jnp.arange(nb, dtype=jnp.int32) * BLK
    blk_end = blk_start + BLK - 1
    tab = rel_bias.reshape(N_BUCKETS, N_KV, HPG)
    d_cmp = q_pos[:, None] - blk_end[None, :]
    m_cmp = d_cmp >= 0
    lg = jnp.einsum('bqghd,bngd->bghqn', qs, k_cmp) + tab[t5_bucket(d_cmp)].transpose(2, 3, 0, 1)
    p_cmp = masked_softmax(lg, m_cmp)
    o_cmp = jnp.einsum('bghqn,bngd->bqghd', p_cmp.astype(v_cmp.dtype), v_cmp)
    imp = p_cmp.sum(axis=2)
    score = jnp.where(m_cmp, imp, jnp.where(blk_start[None, :] <= q_pos[:, None], 2.0, -1.0))
    top_s, idx = lax.top_k(score, min(N_SEL, nb))
    gather = jax.vmap(jax.vmap(lambda kb, ix: kb[ix]))
    ks = gather(k_sel, idx)
    vs = gather(v_sel, idx)
    s_pos = idx[..., None] * BLK + jnp.arange(BLK, dtype=jnp.int32)
    d_sel = q_pos[None, None, :, None, None] - s_pos
    m_sel = (d_sel >= 0) & (top_s[..., None] >= 0)
    b_sel = jax.vmap(lambda tb, bk: tb[bk], in_axes=(1, 1), out_axes=1)(tab, t5_bucket(d_sel))
    lg = jnp.einsum('bqghd,bgqnkd->bghqnk', qs, ks) + b_sel.transpose(0, 1, 5, 2, 3, 4)
    shp = lg.shape
    p_sel = masked_softmax(lg.reshape(shp[:4] + (-1,)), m_sel.reshape(m_sel.shape[:3] + (-1,))[:, :, None])
    o_sel = jnp.einsum('bghqnk,bgqnkd->bqghd', p_sel.reshape(shp).astype(vs.dtype), vs)
    d_win = q_pos[:, None] - win_pos[None, :]
    m_win = (d_win >= 0) & (d_win <= WINDOW) & (win_pos[None, :] >= 0)
    lg = jnp.einsum('bqghd,bwgd->bghqw', qs, k_win) + tab[t5_bucket(d_win)].transpose(2, 3, 0, 1)
    p_win = masked_softmax(lg, m_win)
    o_win = jnp.einsum('bghqw,bwgd->bqghd', p_win.astype(v_win.dtype), v_win)
    g = jax.nn.sigmoid(gts.astype(jnp.float32)).astype(q.dtype)[..., None]
    return g[:, :, 0] * o_cmp + g[:, :, 1] * o_sel + g[:, :, 2] * o_win

def nsa_prompt(q, gts, kc, vc, ksl, vsl, kw, vw, cmpw, rel_bias):
    b, s = q.shape[:2]
    k_cmp, v_cmp = compress(kc, *cmpw[:3]), compress(vc, *cmpw[3:])
    k_sel, v_sel = to_blocks(ksl), to_blocks(vsl)
    pad = ((0, 0), (WINDOW, 0), (0, 0), (0, 0))
    kw_pad, vw_pad = jnp.pad(kw, pad), jnp.pad(vw, pad)

    def q_block(i):
        s0 = i * Q_BLOCK
        qb = lax.dynamic_slice_in_dim(q, s0, Q_BLOCK, axis=1)
        gb = lax.dynamic_slice_in_dim(gts, s0, Q_BLOCK, axis=1)
        kwb = lax.dynamic_slice_in_dim(kw_pad, s0, WINDOW + Q_BLOCK, axis=1)
        vwb = lax.dynamic_slice_in_dim(vw_pad, s0, WINDOW + Q_BLOCK, axis=1)
        q_pos = s0 + jnp.arange(Q_BLOCK, dtype=jnp.int32)
        w_pos = s0 - WINDOW + jnp.arange(WINDOW + Q_BLOCK, dtype=jnp.int32)
        return nsa_attend(qb, gb, q_pos, k_cmp, v_cmp, k_sel, v_sel, kwb, vwb, w_pos, rel_bias)

    o = lax.map(q_block, jnp.arange(s // Q_BLOCK, dtype=jnp.int32))
    return jnp.moveaxis(o, 0, 1).reshape(b, s, D_ATTN)

def nsa_sample(q, gts, kc, vc, ksl, vsl, kw, vw, past_kc, past_vc, past_ks, past_vs,
               buf_kw, buf_vw, cmpw, rel_bias):
    b, t = q.shape[:2]
    past = past_kc.shape[1]
    pad_len = (-(past + t)) % BLK

    def full(p, n):
        return jnp.pad(jnp.concatenate([p, n], axis=1), ((0, 0), (0, pad_len), (0, 0), (0, 0)))

    k_cmp, v_cmp = compress(full(past_kc, kc), *cmpw[:3]), compress(full(past_vc, vc), *cmpw[3:])
    k_sel, v_sel = to_blocks(full(past_ks, ksl)), to_blocks(full(past_vs, vsl))
    k_win = jnp.concatenate([buf_kw, kw], axis=1)
    v_win = jnp.concatenate([buf_vw, vw], axis=1)
    q_pos = past + jnp.arange(t, dtype=jnp.int32)
    w_pos = past - buf_kw.shape[1] + jnp.arange(buf_kw.shape[1] + t, dtype=jnp.int32)
    o = nsa_attend(q, gts, q_pos, k_cmp, v_cmp, k_sel, v_sel, k_win, v_win, w_pos, rel_bias)
    return o.reshape(b, t, D_ATTN)

def short_conv(u_pad, w):
    t = u_pad.shape[1] - (CONV_W - 1)
    return sum(w[k] * u_pad[:, k:k + t] for k in range(CONV_W))

def merge_output(x, gate, o_attn, y_conv, z, w_out):
    z_a, z_c = z[..., :D_ATTN], z[..., D_ATTN:]
    o = jnp.concatenate([o_attn * jax.nn.silu(z_a), y_conv * jax.nn.silu(z_c)], axis=-1) @ w_out
    return x + gate[:, None, :] * o

def gather_pages(cache, page_table):
    g = cache[page_table]
    return g.reshape(g.shape[0], g.shape[1] * g.shape[2], g.shape[3], g.shape[4])

def setup_inputs(seed: int = 0) -> dict:
    key = jax.random.key(seed)
    ks = jax.random.split(key, 32)
    n_pages = PAST_LEN // PAGE_SIZE
    n_used = DEC_BATCH * n_pages
    n_pool = n_used + n_used // 4
    win_buf = min(WINDOW, PAST_LEN)

    def nrm(k, shape, s=1.0):
        return s * jax.random.normal(k, shape, jnp.float32)

    page_table = jax.random.permutation(ks[0], n_pool)[:n_used].reshape(DEC_BATCH, n_pages).astype(jnp.int32)
    kv_page = (DEPTH, n_pool, PAGE_SIZE, N_KV, HEAD_DIM)
    kv_win = (DEPTH, DEC_BATCH, win_buf, N_KV, HEAD_DIM)
    return {
        "x_prompt": nrm(ks[1], (BATCH, SEQ, D_MODEL)),
        "x_sample": nrm(ks[2], (DEC_BATCH, DEC_SEQ, D_MODEL)),
        "cache_k_cmp": nrm(ks[3], kv_page),
        "cache_v_cmp": nrm(ks[4], kv_page),
        "cache_k_slc": nrm(ks[5], kv_page),
        "cache_v_slc": nrm(ks[6], kv_page),
        "cache_k_win": nrm(ks[7], kv_win),
        "cache_v_win": nrm(ks[8], kv_win),
        "state_conv": nrm(ks[9], (DEPTH, DEC_BATCH, CONV_W - 1, D_CONV)),
        "page_table": page_table,
        "c_prompt": nrm(ks[10], (BATCH, D_MODEL)),
        "c_sample": nrm(ks[11], (DEC_BATCH, D_MODEL)),
        "ada_w": nrm(ks[12], (DEPTH, D_MODEL, 3 * D_MODEL), 0.5 * D_MODEL ** -0.5),
        "ada_b": nrm(ks[13], (DEPTH, 3 * D_MODEL), 0.02),
        "norm_g": 1.0 + nrm(ks[14], (DEPTH, D_MODEL), 0.02),
        "w_in": nrm(ks[15], (DEPTH, D_MODEL, D_IN), D_MODEL ** -0.5),
        "cmp_pe_k": nrm(ks[16], (DEPTH, BLK, HEAD_DIM), 0.1),
        "cmp_w1_k": nrm(ks[17], (DEPTH, BLK * HEAD_DIM, CMP_HID), (BLK * HEAD_DIM) ** -0.5),
        "cmp_w2_k": nrm(ks[18], (DEPTH, CMP_HID, HEAD_DIM), CMP_HID ** -0.5),
        "cmp_pe_v": nrm(ks[19], (DEPTH, BLK, HEAD_DIM), 0.1),
        "cmp_w1_v": nrm(ks[20], (DEPTH, BLK * HEAD_DIM, CMP_HID), (BLK * HEAD_DIM) ** -0.5),
        "cmp_w2_v": nrm(ks[21], (DEPTH, CMP_HID, HEAD_DIM), CMP_HID ** -0.5),
        "conv_w": nrm(ks[22], (DEPTH, CONV_W, D_CONV), 0.5),
        "w_out": nrm(ks[23], (DEPTH, D_MIX, D_MODEL), D_MIX ** -0.5),
        "rel_bias": nrm(ks[24], (N_BUCKETS, N_HEADS), 0.5),
        "final_g": 1.0 + nrm(ks[25], (D_MODEL,), 0.02),
    }

def reference(x_prompt, x_sample, cache_k_cmp, cache_v_cmp, cache_k_slc, cache_v_slc,
              cache_k_win, cache_v_win, state_conv, page_table, c_prompt, c_sample,
              ada_w, ada_b, norm_g, w_in, cmp_pe_k, cmp_w1_k, cmp_w2_k, cmp_pe_v, cmp_w1_v,
              cmp_w2_v, conv_w, w_out, rel_bias, final_g):
    xp, xs = x_prompt, x_sample
    prompt_states, sample_states = [], []
    for l in range(DEPTH):
        cmpw = (cmp_pe_k[l], cmp_w1_k[l], cmp_w2_k[l], cmp_pe_v[l], cmp_w1_v[l], cmp_w2_v[l])
        (q, kc, vc, ksl, vsl, kw, vw, gts, hc, bc, cc, z), gate = modulate_project(
            xp, c_prompt, ada_w[l], ada_b[l], norm_g[l], w_in[l])
        b, s = q.shape[:2]
        q = q.reshape(b, s, N_KV, HPG, HEAD_DIM)
        gts = gts.reshape(b, s, 3, N_KV, HPG)
        kc, vc, ksl, vsl, kw, vw = (kv_heads(t) for t in (kc, vc, ksl, vsl, kw, vw))
        o_attn = nsa_prompt(q, gts, kc, vc, ksl, vsl, kw, vw, cmpw, rel_bias)
        u = cc * hc
        y_conv = bc * short_conv(jnp.pad(u, ((0, 0), (CONV_W - 1, 0), (0, 0))), conv_w[l])
        xp = merge_output(xp, gate, o_attn, y_conv, z, w_out[l])
        w_keep = min(WINDOW, s)
        prompt_states.append((kc, vc, ksl, vsl, kw[:, -w_keep:], vw[:, -w_keep:], u[:, -(CONV_W - 1):]))
        (q, kc, vc, ksl, vsl, kw, vw, gts, hc, bc, cc, z), gate = modulate_project(
            xs, c_sample, ada_w[l], ada_b[l], norm_g[l], w_in[l])
        b, t = q.shape[:2]
        q = q.reshape(b, t, N_KV, HPG, HEAD_DIM)
        gts = gts.reshape(b, t, 3, N_KV, HPG)
        kc, vc, ksl, vsl, kw, vw = (kv_heads(a) for a in (kc, vc, ksl, vsl, kw, vw))
        buf_kw, buf_vw = cache_k_win[l], cache_v_win[l]
        o_attn = nsa_sample(q, gts, kc, vc, ksl, vsl, kw, vw,
                            gather_pages(cache_k_cmp[l], page_table), gather_pages(cache_v_cmp[l], page_table),
                            gather_pages(cache_k_slc[l], page_table), gather_pages(cache_v_slc[l], page_table),
                            buf_kw, buf_vw, cmpw, rel_bias)
        u = cc * hc
        u_pad = jnp.concatenate([state_conv[l].astype(u.dtype), u], axis=1)
        y_conv = bc * short_conv(u_pad, conv_w[l])
        xs = merge_output(xs, gate, o_attn, y_conv, z, w_out[l])
        nbuf = buf_kw.shape[1]
        new_kw = jnp.concatenate([buf_kw, kw], axis=1)[:, -nbuf:]
        new_vw = jnp.concatenate([buf_vw, vw], axis=1)[:, -nbuf:]
        sample_states.append((kc, vc, ksl, vsl, new_kw, new_vw, u_pad[:, -(CONV_W - 1):]))
    y_prompt = rmsnorm(xp, final_g)
    y_sample = rmsnorm(xs, final_g)
    p_kc, p_vc, p_ks, p_vs, p_kw, p_vw, p_cv = (jnp.stack(a) for a in zip(*prompt_states))
    s_kc, s_vc, s_ks, s_vs, s_kw, s_vw, s_cv = (jnp.stack(a) for a in zip(*sample_states))
    return (y_prompt, y_sample, p_kc, p_vc, p_ks, p_vs, p_kw, p_vw, p_cv,
            s_kc, s_vc, s_ks, s_vs, s_kw, s_vw, s_cv)


_drawn_inputs = setup_inputs


def setup_inputs(seed=0):
    import zlib

    import numpy as np

    out = dict(_drawn_inputs(seed))
    spreads = {}
    factors = {'cache_k_cmp': 4.714,
     'cache_v_cmp': 3.38,
     'cache_k_slc': 7.066,
     'cache_v_slc': 6.008,
     'cmp_pe_k': 8.0,
     'cmp_pe_v': 8.0,
     'rel_bias': 3.376,
     'final_g': 2.803}
    for name, (base, spread) in spreads.items():
        noise = np.random.default_rng([zlib.crc32(name.encode()), seed]).standard_normal(out[name].shape)
        drawn = base * np.exp(spread * noise) if base else spread * noise
        out[name] = __import__('jax').numpy.asarray(drawn.astype(out[name].dtype))
    for name, factor in factors.items():
        out[name] = (out[name] * factor).astype(out[name].dtype)
    return out
```

```python
from contextlib import ExitStack

import concourse.bass as bass
from concourse import mybir

ALU = mybir.AluOpType
ACT = mybir.ActivationFunctionType
AX = mybir.AxisListType
F32 = mybir.dt.float32
F32R = mybir.dt.float32r
I32 = mybir.dt.int32

P = 128
D = 1024
S = 1024
NB, TS = 8, 4
SAMP = NB * TS
TOK = S + SAMP
KC = D // P
NTT = S // P + 1
CH = TOK // 3
PAST, PAGE, WIN, BLK = 2048, 128, 512, 64
NH, NG, HD = 16, 2, 64
HPG = NH // NG
DKV = NG * HD
NPT = 16
NPB = S // BLK
NSB = PAST // BLK
EPS = 1e-6
NEG = -1e30
O_KV = 1024
KV0, KV1 = 3 * DKV, 3 * DKV + 3 * NH
KVW = KV0 + KV1
O_H = O_KV + KVW
O_B, O_C, O_Z = O_H + D, O_H + 2 * D, O_H + 3 * D
C_KC, C_VC, C_KS, C_VS, C_KW, C_VW, C_G = (i * DKV for i in range(7))
CC, HC, BC, ZC, ZA, QQ = range(6)
NK = 6
XR, XW = 255, 384
CB = 2 * P + NPB + 1


ACT_A, ACT_B = {0}, {0}


def build(nc: "bass.Bass", x_prompt, x_sample, cache_k_cmp, cache_v_cmp, cache_k_slc, cache_v_slc, cache_k_win,
          cache_v_win, state_conv, page_table, c_prompt, c_sample, ada_w, ada_b, norm_g, w_in,
          cmp_pe_k, cmp_w1_k, cmp_w2_k, cmp_pe_v, cmp_w1_v, cmp_w2_v, conv_w, w_out, rel_bias,
          final_g, k_ident, k_stack2, k_group, k_before, k_row, k_cmpd, k_edge, k_wedge, k_any,
          y_prompt, y_sample, p_kc, p_vc, p_ks, p_vs, p_kw, p_vw, p_cv,
          s_kc, s_vc, s_ks, s_vs, s_kw, s_vw, s_cv):
    ctx = ExitStack()

    def scope():
        return ctx.enter_context(ExitStack())

    def sb(name, shape, dt=F32, cx=None):
        return (cx or ctx).enter_context(nc.sbuf_tensor(name, shape, dt))

    def sem(name):
        return ctx.enter_context(nc.semaphore(name))

    def ext(ap, *dims):
        return bass.AP(ap.tensor, ap.offset, [*[list(x) for x in ap.ap], *[list(x) for x in dims]])

    def flat(ap, off, dims):
        return bass.AP(ap.tensor, off, [list(x) for x in dims])

    def f32(ap):
        return ap.bitcast(F32)

    with ctx:
        PS = ctx.enter_context(nc.psum_tensor("PS", [P, 8, 512], F32))
        qst = nc.dram_tensor("q_stacked", [NH, P, S], F32R, kind="Internal").ap()
        zad = nc.dram_tensor("z_attn_silu", [8, P, TOK], F32, kind="Internal").ap()
        mixd = nc.dram_tensor("mixed", [16, P, TOK], F32, kind="Internal").ap()
        rowd = nc.dram_tensor("bias_rows", [NH, P, XW], F32, kind="Internal").ap()
        gbd = nc.dram_tensor("gate_rows", [9, D], F32, kind="Internal").ap()
        gated = nc.dram_tensor("gates_sample", [SAMP, 3 * NH], F32, kind="Internal").ap()

        ident = sb("ident", [P, P])
        gate = sb("gate", [9, D])
        qs = sb("qs", [P, 8, SAMP])
        vcol = sb("vcol", [P, 8, 29])
        tcmp = sb("tcmp", [P, 4, NH])
        sc = sb("sc", [P, 4])

        idxc = sb("idxc", [P, 2], I32)
        idxs = sb("idxs", [P, NB], I32)
        pidx = sb("pidx", [P, 2], I32)
        pgc = sb("pgc", [P, 2], I32)
        pgs = sb("pgs", [P, NB], I32)
        sg = sb("sg", [P, NTT, 3 * NH])
        kcs = sb("kcs", [P, NB * NSB])
        vcs = sb("vcs", [NSB, NB, DKV])
        kcp = sb("kcp", [P, NG, 2 * NPB], F32R)
        vcp = sb("vcp", [P, NG, P], F32R)
        pebias = sb("pebias", [P, 2])

        cK = ExitStack()
        kvs = sb("kvs", [P, KVW], cx=cK)
        cN = ExitStack()
        nearl = sb("nearl", [P, NH, 2 * P], F32R, cN)
        cN.close()
        kvt = sb("kvt", [P, NTT - 1, KVW], cx=cK)
        krow = kvt[0:33, 7, 0:XW]
        kcmpd = kvs[0:33, 0:4 * P].rearrange("p (m q) -> p m q", m=4)

        cA = ExitStack()
        hhi = sb("hhi", [P, KC, TOK], F32R, cA)
        hlo = sb("hlo", [P, KC, TOK], F32R, cA)
        c0 = ExitStack()
        vrow = sb("vrow", [29, D], cx=c0)
        relx = sb("relx", [33, NH], cx=c0)
        rel31 = sb("rel31", [32, NH], cx=c0)
        rows = sb("rows", [NH, XW], cx=c0)
        wkr = [sb(f"wkr{i}", [P, KC, w], cx=c0) for i, w in enumerate((KV0, KV1))]
        xb = [sb(f"xb{i}", [P, D], cx=c0) for i in range(2)]
        h32 = sb("h32", [P, KC, P], cx=c0)
        scA = sb("scA", [P, KC, 9], cx=c0)
        scB = sb("scB", [P, KC, 9], cx=c0)
        ssq = sb("ssq", [P, NTT], cx=c0)
        ms = sb("ms", [P, NTT], cx=c0)
        rms = sb("rms", [P, NTT], cx=c0)
        rstd = sb("rstd", [P, NTT], cx=c0)
        cS = ExitStack()
        adaw = [sb(f"adaw{i}", [P, KC, 512], cx=cS) for i in range(2)]
        adar = sb("adar", [9, 2 * D], cx=cS)
        adab = sb("adab", [9, 3 * D], cx=cS)
        cS.close()
        wkh = [sb(f"wkh{i}", [P, KC, w], F32R, c0) for i, w in enumerate((KV0, KV1))]
        wkl = [sb(f"wkl{i}", [P, KC, w], F32R, c0) for i, w in enumerate((KV0, KV1))]
        c0.close()
        c2 = ExitStack()
        wr = [sb(f"wr{i}", [P, KC, P], cx=c2) for i in range(2)]
        wh = [sb(f"wh{i}", [P, KC, P], F32R, c2) for i in range(2)]
        wl = [sb(f"wl{i}", [P, KC, P], F32R, c2) for i in range(2)]
        cct = sb("cct", [P, TOK], cx=c2)
        uu = sb("uu", [P, 2 + TOK], cx=c2)
        us = sb("us", [P, NB, 6], cx=c2)
        yy = sb("yy", [P, TOK], cx=c2)
        zt = sb("zt", [P, TOK], cx=c2)
        ych = sb("ych", [P, TOK], cx=c2)
        zab = sb("zab", [P, TOK], cx=c2)
        qhi = sb("qhi", [P, TOK], F32R, c2)
        qlo = sb("qlo", [P, TOK], F32R, c2)
        tail = sb("tail", [P, 18], cx=c2)
        tailr = sb("tailr", [18, D], cx=c2)
        c2.close()
        cA.close()
        c3 = ExitStack()
        xbl = [sb(f"xbl{i}", [P, BLK * DKV], cx=c3) for i in range(2)]
        xpl = sb("xpl", [NPB + 1, BLK * DKV], cx=c3)
        w1 = sb("w1", [P, 32, P], cx=c3)
        w2 = sb("w2", [P, P], cx=c3)
        xt = [sb(f"xt{i}", [P, NG, CB], cx=c3) for i in range(2)]
        hs3 = sb("hs3", [P, NG, CB], cx=c3)
        c3.close()
        c4 = ExitStack()
        ksh, ksl, kwh, kwl = (sb(n, [P, NG, S], F32R, c4) for n in ("ksh", "ksl", "kwh", "kwl"))
        vsx, vwx = (sb(n, [P, 8, NG, P], F32R, c4) for n in ("vsx", "vwx"))
        near = sb("near", [P, NH, 2 * P], F32R, c4)
        edge = sb("edge", [P, P], cx=c4)
        edger = sb("edger", [P, P], F32R, c4)
        identr = sb("identr", [P, P], F32R, c4)
        stack2 = sb("stack2", [P, 64], cx=c4)
        anyc = sb("anyc", [P, 1], cx=c4)
        pr = [sb(f"pr{i}", [P, 4, S], cx=c4) for i in range(3)]
        prc = [sb(f"prc{i}", [P, 4, P], cx=c4) for i in range(3)]
        nearr = pr[2][:, :, :].rearrange("p a (b c) -> p (a b) c", c=2 * P)
        cs = sb("cs", [P, 4, NPB], cx=c4)
        nm = sb("nm", [P, 3, 8], cx=c4)
        rsum = sb("rsum", [P, 3, 8], cx=c4)
        rrec = sb("rrec", [P, 3, 8], cx=c4)
        rg = sb("rg", [P, 3, 8], cx=c4)
        qb = [sb(f"qb{i}", [P, 4, P], F32R, c4) for i in range(4)]
        pth = [sb(f"pth{i}", [P, 512], F32R, c4) for i in range(2)]
        ptl = [sb(f"ptl{i}", [P, 512], F32R, c4) for i in range(2)]
        osb = sb("osb", [P, 512], cx=c4)
        zau = [sb(f"zau{i}", [P, 4, P], cx=c4) for i in range(2)]
        mixs = [sb(f"mixs{i}", [P, 4, P], cx=c4) for i in range(2)]
        c4.close()
        c5 = ExitStack()
        NSEL, NWIN = PAST // P, WIN // P
        grp = sb("grp", [P, P], cx=c5)
        before = sb("before", [P, NSB, NSB], cx=c5)
        wedge = sb("wedge", [P, TS], cx=c5)
        nb = sb("nb", [P, P], cx=c5)
        nbnew = sb("nbnew", [P, 4, SAMP], cx=c5)
        nbc = sb("nbc", [P, 2], cx=c5)
        gr = sb("gr", [P, 4, 3], cx=c5)
        zas = sb("zas", [P, 8, SAMP], cx=c5)
        qbd = sb("qbd", [P, NB, 64], cx=c5)
        kb = [sb(f"kb{i}", [P, NSEL, DKV], cx=c5) for i in range(2)]
        vb = [sb(f"vb{i}", [P, NSEL, DKV], cx=c5) for i in range(4)]
        kwb = [sb(f"kwb{i}", [P, NWIN, DKV], cx=c5) for i in range(2)]
        vwb = [sb(f"vwb{i}", [P, NWIN, DKV], cx=c5) for i in range(4)]
        kt5 = [sb(f"kt5{i}", [P, NSEL + NWIN, P], cx=c5) for i in range(2)]
        knt = sb("knt", [P, 2, SAMP], cx=c5)
        SEL, WN = PAST + SAMP, WIN + SAMP
        s5 = [sb(f"s5{i}", [P, SEL + WN], cx=c5) for i in range(2)]
        cm = sb("cm", [P, NSB], cx=c5)
        pn = sb("pn", [P, NSB], cx=c5)
        cmg = sb("cmg", [P, NSB], cx=c5)
        imp = sb("imp", [P, NSB], cx=c5)
        gt = sb("gt", [P, NSB, NSB], cx=c5)
        eq = sb("eq", [P, NSB, NSB], cx=c5)
        rank = sb("rank", [P, NSB], cx=c5)
        bmask = sb("bmask", [P, NSB], cx=c5)
        n5 = sb("n5", [P, 4], cx=c5)
        r5 = sb("r5", [P, 4], cx=c5)
        i5 = sb("i5", [P, 4], cx=c5)
        pt5 = sb("pt5", [P, NSEL + NWIN + 3, P], cx=c5)
        o5 = sb("o5", [P, P], cx=c5)
        mix5 = sb("mix5", [P, 8, SAMP], cx=c5)
        c5.close()
        cK.close()
        c6 = ExitStack()
        woh = sb("woh", [P, 16, D], F32R, c6)
        wol = sb("wol", [P, 16, D], F32R, c6)
        wor = [sb(f"wor{i}", [P, D], cx=c6) for i in range(2)]
        mr = [sb(f"mr{i}", [P, 16, P], cx=c6) for i in range(2)]
        mh = sb("mh", [P, 16, P], F32R, c6)
        ml = sb("ml", [P, 16, P], F32R, c6)
        gbc = sb("gbc", [P, D], cx=c6)
        fgb = sb("fgb", [P, D], cx=c6)
        xf = [sb(f"xf{i}", [P, D], cx=c6) for i in range(2)]
        yf = sb("yf", [P, D], cx=c6)
        yo = sb("yo", [P, D], cx=c6)
        s6 = sb("s6", [P, 4], cx=c6)
        c6.close()

        const_ld, c_ld, row_st, rel_ld = sem("const_ld"), sem("c_ld"), sem("row_st"), sem("rel_ld")
        adaw_ld = [sem(f"adaw_ld{i}") for i in range(2)]
        ct_pe, ct_dve, ada_mm, ada_ev, ada_t, ada_col = (sem(n) for n in
            ("ct_pe", "ct_dve", "ada_mm", "ada_ev", "ada_t", "ada_col"))
        x_ld = [sem(f"x_ld{i}") for i in range(2)]
        x_ms, x_rms, x_sq, x_n, x_t, h_ev, h_hi, h_lo = (sem(n) for n in ("x_ms", "x_rms", "x_sq", "x_n", "x_t", "h_ev", "h_hi", "h_lo"))
        wk_ld, wk_hi, wk_lo, kv_mm, kv_ev = (sem(n) for n in ("wk_ld", "wk_hi", "wk_lo", "kv_mm", "kv_ev"))
        dch, pch = sem("dch"), sem("pch")
        wr_ld = [sem(f"wr_ld{i}") for i in range(2)]
        w_hi, w_lo, p2_mm = sem("w_hi"), sem("w_lo"), sem("p2_mm")
        p2_ev = [sem(f"p2_ev{i}") for i in range(2)]
        q_hi, y_rdy, tail_rdy, tail_t, tail_ev = (sem(n) for n in
            ("q_hi", "y_rdy", "tail_rdy", "tail_t", "tail_ev"))
        ych_st, zab_st, q_st = sem("ych_st"), sem("zab_st"), sem("q_st")
        tb_mm, tb_ev, tb_rel = sem("tb_mm"), sem("tb_ev"), sem("tb_rel")
        out_st, tail_st = sem("out_st"), sem("tail_st")
        nout = [0]
        idx_ld, idx_a, idx_b, kc_st = sem("idx_ld"), sem("idx_a"), sem("idx_b"), sem("kc_st")
        xbl_ld = [sem(f"xbl_ld{i}") for i in range(2)]
        xpl_ld, w12_ld, x3_t, x3_mm, pe_rdy, hs_rdy, k3_mm, v3_mm, k3_hi, k3_ev, v3_ev, v3_hi = (sem(n) for n in
            ("xpl_ld", "w12_ld", "x3_t", "x3_mm", "pe_rdy", "hs_rdy", "k3_mm", "v3_mm", "k3_hi", "k3_ev", "v3_ev", "v3_hi"))
        xe = [sem(f"xe{i}") for i in range(2)]
        c4_ld, kt_t, kt_hi, kt_lo, vb_hi, vb_lo, sg_rdy, pad0 = (sem(n) for n in
            ("c4_ld", "kt_t", "kt_hi", "kt_lo", "vb_hi", "vb_lo", "sg_rdy", "pad0"))
        s_mm, m_rdy, mc_rdy, e_done, ec_done, r_rdy, n_act, n_dve, t_mm, pt_hi, pt_lo, pv_mm, o_ev, r_mm, r_ev = (sem(n) for n in
            ("s_mm", "m_rdy", "mc_rdy", "e_done", "ec_done", "r_rdy", "n_act", "n_dve", "t_mm", "pt_hi", "pt_lo", "pv_mm", "o_ev", "r_mm", "r_ev"))
        q_ld = [sem(f"q_ld{i}") for i in range(4)]
        za_ld = [sem(f"za_ld{i}") for i in range(2)]
        mix_st = [sem(f"mix_st{i}") for i in range(2)]

        c5_ld, g_st, gr_ld = sem("c5_ld"), sem("g_st"), sem("gr_ld")
        kg_ld = [sem(f"kg_ld{i}") for i in range(2)]
        vg_ld = [sem(f"vg_ld{i}") for i in range(4)]
        kw_ld = [sem(f"kw_ld{i}") for i in range(2)]
        vw_ld = [sem(f"vw_ld{i}") for i in range(4)]
        q5_rdy, nbn_rdy, t5, ev5, s5c_mm, m5c, e5c, pn_rdy, imp_mm, s5_mm, s5_ev, m5, e5, p5, b5_rd, o5_mm, o5_cp, ot_t, mix5_rdy, mix5_st, kn_t, kn_ev = (
            sem(n) for n in ("q5_rdy nbn_rdy t5 ev5 s5c_mm m5c e5c pn_rdy imp_mm s5_mm s5_ev m5 e5 p5 b5_rd o5_mm o5_cp ot_t mix5_rdy mix5_st kn_t kn_ev".split()))
        wo_ld = [sem(f"wo_ld{i}") for i in range(2)]
        mr_ld = [sem(f"mr_ld{i}") for i in range(2)]
        xf_ld = [sem(f"xf_ld{i}") for i in range(2)]
        c6_ld, wo_hi, wo_lo, m_hi, m_lo, y_mm, y_ev, y_sum, y_sq, y_ms, y_rms, y_out, y_st = (
            sem(n) for n in "c6_ld wo_hi wo_lo m_hi m_lo y_mm y_ev y_sum y_sq y_ms y_rms y_out y_st".split())

        NU = 32
        NI = 2 * NU

        def unit(u):
            return u // 16, u // 8 % 2, u % 8

        def tiles_of(w):
            i = w // 2 % 8
            return i + 1 if w % 2 == 0 else min(i + 1, 5) + 1

        def keys_of(w):
            k = (tiles_of(w) - w % 2) * P
            return k, ([k] if k <= 512 else [k // 2, k // 2])

        ON_ACT = {0: ACT_A, 1: ACT_B}

        tile0 = [0]
        for w in range(NI):
            tile0.append(tile0[-1] + tiles_of(w))

        def slots(w):
            n = tiles_of(w)
            cuts = [(n * q + 3) // 4 for q in range(5)]
            return [range(cuts[q], cuts[q + 1]) for q in range(4)]

        class Chain:
            def __init__(self, eng, s):
                self.eng, self.s, self.n = eng, s, 0

            def link(self, ins):
                self.n += 1
                ins.then_inc(self.s, 1)
                self.eng.wait_ge(self.s, self.n)

        w3 = w_in.rearrange("l (k p) c -> p (l k) c", p=P)
        ada3 = ada_w.rearrange("l (k p) c -> p (l k) c", p=P)
        xp = x_prompt.rearrange("b (t p) c -> p (b t) c", p=P)
        xs = x_sample.rearrange("b t c -> (b t) c")

        def wcol(j, kind):
            if kind == QQ:
                return [(64 * j, 64), (512 + 64 * j, 64)]
            if kind == ZA:
                return [(O_Z + 64 * j, 64), (O_Z + 512 + 64 * j, 64)]
            return [({CC: O_C, HC: O_H, BC: O_B, ZC: O_Z + D}[kind] + P * j, P)]

        def rows_of(tt):
            return P if tt < NTT - 1 else SAMP

        KVB = [0, 7, 1, 2]

        block = ctx.enter_context(nc.Block())

        @block.sync
        def _(sp):
            sp.dma_start(vrow[0:1, :], c_prompt).then_inc(c_ld, 16)
            sp.dma_start(vrow[1:9, :], c_sample).then_inc(c_ld, 16)
            sp.dma_start(adab[:, :], flat(ada_b, 0, [(0, 9), (1, 3 * D)])).then_inc(c_ld, 16)
            for ch in range(6):
                if ch >= 2:
                    sp.wait_ge(ada_mm, ch - 1)
                sp.dma_start(adaw[ch % 2][:, :, :], ada3[:, :, 512 * ch:512 * ch + 512]).then_inc(adaw_ld[ch % 2], 16)
                if ch == 1:
                    sp.dma_start(wkr[0][:, :, :], w3[:, :, O_KV:O_KV + KV0]).then_inc(wk_ld, 16)
                    sp.dma_start(wkr[1][:, :, :], w3[:, :, O_KV + KV0:O_H]).then_inc(wk_ld, 16)
            sp.wait_ge(h_lo, NTT)
            sp.wait_ge(h_hi, NTT)
            sp.wait_ge(kv_mm, 2 * NTT)
            sp.wait_ge(row_st, 16)
            sp.wait_ge(tb_ev, 2)

            def load_w(j, kind, first):
                n = NK * j + kind
                if not first:
                    sp.wait_ge(w_lo, n - 1)
                for at, (c0_, w) in zip((0, 64), wcol(j, kind)):
                    sp.dma_start(wr[kind % 2][:, :, at:at + w], w3[:, :, c0_:c0_ + w]).then_inc(wr_ld[kind % 2], 16 if kind in (QQ, ZA) else 16)

            for j in range(8):
                for kind in range(NK):
                    load_w(j, kind, j == 0 and kind < 2)
            for e in (0, 1):
                sp.wait_ge(p2_ev[e], 24)
            sp.wait_ge(y_rdy, 8)
            sp.wait_ge(tail_ev, 8)
            sp.wait_ge(ych_st, 16 * 8)
            sp.wait_ge(zab_st, 16 * 8)
            sp.wait_ge(q_st, 16 * 32)
            for c, (pe_, w1_, w2_, rows_) in enumerate(((cmp_pe_k, cmp_w1_k, cmp_w2_k, p_kc), (cmp_pe_v, cmp_w1_v, cmp_w2_v, p_vc))):
                if c == 0:
                    sp.wait_ge(kc_st, 32)
                    sp.wait_ge(tail_st, 32)
                else:
                    sp.wait_ge(x3_t, 64)
                sp.dma_start(xpl[0:NPB, :], rows_.rearrange("l b (n t) g d -> (l b n) (t g d)", t=BLK)).then_inc(xpl_ld, 16)
                for g in range(NG):
                    sp.dma_start(xpl[NPB:NPB + 1, :].rearrange("p (t c) -> p t c", c=DKV)[:, :, 64 * g:64 * g + 64], pe_).then_inc(xpl_ld, 16)
                if c:
                    sp.wait_ge(x3_mm, 32)
                sp.dma_start(w1[:, :, :], w1_.rearrange("l (t p) c -> p (l t) c", p=P)).then_inc(w12_ld, 16)
                if c:
                    sp.wait_ge(k3_mm, 1)
                for a in range(2):
                    sp.dma_start(w2[:, 64 * a:64 * a + 64], w2_.rearrange("l p c -> (l p) c")).then_inc(w12_ld, 16)
            sp.wait_ge(v3_mm, 1)
            sp.wait_ge(row_st, 16)
            sp.dma_start(nearr, flat(rowd, P - 1, [(XW - 1, P), (P * XW, NH), (1, 2 * P)])).then_inc(c4_ld, 16)
            sp.dma_start(edge[:, :], k_edge).then_inc(c4_ld, 16)
            sp.dma_start(stack2[:, :], k_stack2).then_inc(c4_ld, 16)
            sp.dma_start(anyc[:, :], k_any).then_inc(c4_ld, 16)

            def load_q(u):
                g, hs, i = unit(u)
                if u >= 4:
                    sp.wait_ge(s_mm, 8 * (u - 3))
                h0 = HPG * g + 4 * hs
                sp.dma_start(f32(qb[u % 4][:, :, :]), f32(qst[h0:h0 + 4, :, i * P:(i + 1) * P]).rearrange("h p c -> p h c")).then_inc(q_ld[u % 4], 16)

            def load_za(u):
                g, hs, i = unit(u)
                half = slice(64 * g, 64 * g + 64)
                if u >= 2:
                    sp.wait_ge(r_ev, u - 1)
                sp.dma_start(zau[u % 2][half, :, :], zad[4 * hs:4 * hs + 4, half, i * P:(i + 1) * P].rearrange("j p c -> p j c")).then_inc(za_ld[u % 2], 16)

            for u in range(3):
                load_q(u)
            load_za(0)
            for u in range(NU):
                g, hs, i = unit(u)
                half = slice(64 * g, 64 * g + 64)
                if u + 3 < NU:
                    load_q(u + 3)
                if u + 1 < NU:
                    load_za(u + 1)
                sp.wait_ge(r_ev, u + 1)
                sp.dma_start(mixd[4 * hs:4 * hs + 4, half, i * P:(i + 1) * P].rearrange("j p c -> p j c"), mixs[u % 2][half, :, :]).then_inc(mix_st[u % 2], 16)
            sp.wait_ge(mix_st[0], 16 * NU // 2)
            sp.wait_ge(mix_st[1], 16 * NU // 2)
            sp.wait_ge(r_ev, NU)
            sp.wait_ge(pv_mm, tile0[NI])
            sp.wait_ge(g_st, 32)
            sp.dma_start(grp[:, :], k_group).then_inc(c5_ld, 16)
            sp.dma_start(before[:, :, :], flat(k_before, 0, [(0, P), (1, NSB * NSB)])).then_inc(c5_ld, 16)
            sp.dma_start(wedge[:, :], k_wedge).then_inc(c5_ld, 16)
            sp.dma_start(zas[:, :, :], zad[:, :, S:TOK].rearrange("j p c -> p j c")).then_inc(c5_ld, 16)
            for b2 in range(2):
                half = slice(64 * b2, 64 * b2 + 64)
                sp.dma_start(nb[half, :], flat(rowd, P - 1, [(P * XW, NH), (XW - 1, TS), (1, P)])).then_inc(c5_ld, 16)
                for a in range(2):
                    sp.dma_start(nbc[half, a:a + 1], flat(rowd, XR - 65 + 64 * a, [(P * XW, NH), (XW - 1, TS), (1, 1)]), allow_slow_non_contiguous=True).then_inc(c5_ld, 16)
            for b in range(NB):
                half = slice(64 * (b % 2), 64 * (b % 2) + 64)
                for a in range(3):
                    sp.dma_start(gr[half, b // 2, a:a + 1], flat(gated, TS * b * 3 * NH + NH * a, [(1, NH), (3 * NH, TS), (1, 1)]), allow_slow_non_contiguous=True).then_inc(gr_ld, 16)
            sp.wait_ge(nbn_rdy, 1)
            for b in range(NB):
                half = slice(64 * (b % 2), 64 * (b % 2) + 64)
                sp.dma_start(nbnew[half, b // 2, TS * b:TS * b + TS], flat(rowd, XR, [(P * XW, NH), (XW - 1, TS), (1, TS)])).then_inc(gr_ld, 16)
            for b in range(NB):
                if b >= 2:
                    sp.wait_ge(s5_mm, b // 2)
                sp.dma_start(kwb[b % 2][:, :, :], cache_k_win[0, b].rearrange("(p i) g d -> p (i g d)", i=NWIN)).then_inc(kw_ld[b % 2], 16)
                if b >= 4:
                    sp.wait_ge(o5_mm, b // 2 - 1)
                sp.dma_start(vwb[b % 4][:, :, :], cache_v_win[0, b].rearrange("(p i) g d -> p (i g d)", i=NWIN)).then_inc(vw_ld[b % 4], 16)
            sp.wait_ge(mix5_rdy, 4)
            sp.dma_start(mixd[0:8, :, S:TOK].rearrange("j p c -> p j c"), mix5[:, :, :]).then_inc(mix5_st, 16)
            sp.wait_ge(mix5_st, 16)
            sp.wait_ge(o5_mm, 4)
            sp.dma_start(gbc[:, :], flat(gbd, 0, [(0, P), (1, D)])).then_inc(c6_ld, 16)
            sp.dma_start(fgb[:, :], flat(final_g, 0, [(0, P), (1, D)])).then_inc(c6_ld, 16)
            wo = w_out.rearrange("l r c -> (l r) c")

            def load_wo(j):
                if j >= 2:
                    sp.wait_ge(wo_lo, j - 1)
                if j < 8:
                    sp.dma_start(wor[j % 2][0:64, :], wo[64 * j:64 * j + 64, :]).then_inc(wo_ld[j % 2], 16)
                    sp.dma_start(wor[j % 2][64:128, :], wo[512 + 64 * j:576 + 64 * j, :]).then_inc(wo_ld[j % 2], 16)
                else:
                    sp.dma_start(wor[j % 2][:, :], wo[P * j:P * j + P, :]).then_inc(wo_ld[j % 2], 16)

            def load_mix(tt):
                n = rows_of(tt)
                if tt >= 2:
                    sp.wait_ge(m_lo, tt - 1)
                    sp.wait_ge(y_sum, tt - 1)
                sp.dma_start(mr[tt % 2][:, :, 0:n], mixd[:, :, tt * P:tt * P + n].rearrange("j p c -> p j c")).then_inc(mr_ld[tt % 2], 16)
                sp.dma_start(xf[tt % 2][0:n, :], xp[:, tt, :] if tt < NTT - 1 else xs).then_inc(xf_ld[tt % 2], 16)

            load_mix(0)
            for j in range(16):
                load_wo(j)
            for tt in range(1, NTT):
                load_mix(tt)
            sp.wait_ge(y_ev, NTT - 1)
            sp.dma_start(gbc[0:SAMP, :], flat(gbd, D, [(D, NB), (0, TS), (1, D)])).then_inc(c6_ld, 16)

        def wr_count(j, kind):
            return 16 * (4 * j + (1, 1, 2, 2, 4, 4)[kind])

        @block.gpsimd
        def _(po):
            chain = Chain(po, pch)
            chain.link(po.memset(relx[32:33, :], NEG))
            for T in range(2):
                po.dma_start(pgc[:, T:T + 1], flat(page_table, 64 * T, [(1, 64), (0, 2), (1, 1)])).then_inc(idx_ld, 16)
            for b in range(NB):
                po.dma_start(pgs[:, b:b + 1], flat(page_table, NPT * b, [(1, NPT), (0, 8), (1, 1)])).then_inc(idx_ld, 16)
            po.iota(pidx[:, :], [[0, 2]], base=0, channel_multiplier=1).then_inc(idx_a, 1)
            po.dma_start(ident[:, :], k_ident).then_inc(const_ld, 16)
            po.dma_start(vrow[9:10, :], norm_g).then_inc(const_ld, 16)
            po.dma_start(vrow[10:13, :], conv_w.rearrange("l r c -> (l r) c")).then_inc(const_ld, 16)
            po.dma_start(vrow[13:29, :], state_conv.rearrange("l b r c -> (l b r) c")).then_inc(const_ld, 16)
            po.dma_start(relx[0:32, :], rel_bias).then_inc(rel_ld, 16)
            po.dma_start(rel31[:, :], flat(rel_bias, 31 * NH, [(0, 32), (1, NH)])).then_inc(rel_ld, 16)
            po.dma_start(krow, k_row).then_inc(rel_ld, 16)
            po.dma_start(kcmpd, k_cmpd).then_inc(rel_ld, 16)
            for tt in range(NTT):
                if tt >= 2:
                    po.wait_ge(x_t, tt - 1)
                src = xp[:, tt, :] if tt < NTT - 1 else xs
                po.dma_start(xb[tt % 2][0:rows_of(tt), :], src).then_inc(x_ld[tt % 2], 16)
            po.wait_ge(tb_ev, 1)
            rv = rows[:, :]
            po.dma_start(rowd, bass.AP(rv.tensor, rv.offset, [list(rv.ap[0]), [0, P], [1, XW]])).then_inc(row_st, 16)
            po.wait_ge(kv_ev, 2 * NTT)
            for which, (dst, col, t0) in enumerate(((p_kc, C_KC, 0), (p_vc, C_VC, 0), (p_ks, C_KS, 0), (p_vs, C_VS, 0),
                                 (p_kw, C_KW, 4), (p_vw, C_VW, 4))):
                po.dma_start(dst.rearrange("l b (t p) g d -> p (l b t) (g d)", p=P), kvt[:, t0:8, col:col + DKV]).then_inc(kc_st if which < 2 else out_st, 16)
                nout[0] += 0 if which < 2 else 16
            for dst, col in ((s_kc, C_KC), (s_vc, C_VC), (s_ks, C_KS), (s_vs, C_VS)):
                po.dma_start(dst.rearrange("l b t g d -> (l b t) (g d)"), kvs[0:SAMP, col:col + DKV]).then_inc(out_st, 16)
                nout[0] += 16
            for dst, buf, col in ((s_kw, cache_k_win, C_KW), (s_vw, cache_v_win, C_VW)):
                po.dma_start(dst[0, :, 0:WIN - TS, :, :].rearrange("b t g d -> b (t g d)"),
                             buf[0, :, TS:WIN, :, :].rearrange("b t g d -> b (t g d)")).then_inc(out_st, 16)
                for b in range(NB):
                    po.dma_start(dst[0, b, WIN - TS:WIN, :, :].rearrange("t g d -> t (g d)"),
                                 kvs[TS * b:TS * b + TS, col:col + DKV]).then_inc(out_st, 16)
                nout[0] += 16 * 9
            for j in range(8):
                po.wait_ge(y_rdy, j + 1)
                po.dma_start(mixd[8 + j], ych[:, :]).then_inc(ych_st, 16)
                po.wait_ge(p2_ev[0], 3 * j + 3)
                po.dma_start(zad[j], zab[:, :]).then_inc(zab_st, 16)
                po.wait_ge(p2_ev[1], 3 * j + 3)
                for g in range(2):
                    half = slice(64 * g, 64 * g + 64)
                    po.dma_start(f32(qst[8 * g + j, 0:64, :]), f32(qhi[half, 0:S])).then_inc(q_st, 16)
                    po.dma_start(f32(qst[8 * g + j, 64:128, :]), f32(qlo[half, 0:S])).then_inc(q_st, 16)
            po.wait_ge(tail_ev, 8)
            po.dma_start(p_cv.rearrange("l b r c -> (l b r) c"), tailr[0:2, :]).then_inc(tail_st, 16)
            po.dma_start(s_cv.rearrange("l b r c -> (l b r) c"), tailr[2:18, :]).then_inc(tail_st, 16)
            po.wait_ge(out_st, nout[0])
            po.wait_ge(ych_st, 16 * 8)
            po.wait_ge(zab_st, 16 * 8)
            po.wait_ge(q_st, 16 * 32)
            po.wait_ge(row_st, 16)
            po.wait_ge(tail_st, 32)
            for e in (0, 1):
                po.wait_ge(p2_ev[e], 24)
            po.wait_ge(idx_b, 2)
            for c, cache in enumerate((cache_k_cmp, cache_v_cmp)):
                src = cache.rearrange("l n (h t) g d -> (l n h) (t g d)", h=2)
                for T in range(2):
                    if c:
                        po.wait_ge(x3_t, 64)
                    po.indirect_dma_start(xbl[T][:, :], None, src, bass.IndirectOffsetOnAxis(idxc[:, T:T + 1], 0)).then_inc(xbl_ld[T], 16)
            po.wait_ge(xbl_ld[0], 32)
            po.wait_ge(xbl_ld[1], 32)
            po.memset(f32(vcp[:, :, :]), 0.0).then_inc(pad0, 1)
            po.wait_ge(v3_mm, 1)
            for r in range(3):
                ins = po.memset(prc[r][:, :, :], 0.0)
            ins.then_inc(pad0, 1)
            po.wait_ge(sg_rdy, 2)
            po.dma_start(gated, sg[0:SAMP, 8, :]).then_inc(g_st, 16)
            po.dma_start(gbd, gate[:, :]).then_inc(g_st, 16)
            po.wait_ge(g_st, 32)
            po.wait_ge(r_ev, NU)
            po.wait_ge(pv_mm, tile0[NI])
            ksrc = cache_k_slc.rearrange("l n (e t) g d -> (l n e) (t g d)", e=8)
            vsrc = cache_v_slc.rearrange("l n (e t) g d -> (l n e) (t g d)", e=8)
            flat2 = lambda t: t[:, :, :].rearrange("p i c -> p (i c)")
            for b in range(NB):
                if b == 1:
                    po.memset(nbnew[:, :, :], NEG).then_inc(nbn_rdy, 1)
                if b >= 2:
                    po.wait_ge(s5_mm, b // 2)
                po.indirect_dma_start(flat2(kb[b % 2]), None, ksrc, bass.IndirectOffsetOnAxis(idxs[:, b:b + 1], 0)).then_inc(kg_ld[b % 2], 16)
                if b >= 4:
                    po.wait_ge(o5_mm, b // 2 - 1)
                po.indirect_dma_start(flat2(vb[b % 4]), None, vsrc, bass.IndirectOffsetOnAxis(idxs[:, b:b + 1], 0)).then_inc(vg_ld[b % 4], 16)
            for q in range(4):
                po.wait_ge(vg_ld[q], 32)
            for q in range(2):
                po.wait_ge(kg_ld[q], 64)
            for tt in range(NTT):
                n = rows_of(tt)
                po.wait_ge(y_out, tt + 1)
                dst = y_prompt[0, tt * P:tt * P + n, :] if tt < NTT - 1 else y_sample.rearrange("b t c -> (b t) c")
                po.dma_start(dst, yo[0:n, :]).then_inc(y_st, 16)
            po.wait_ge(y_st, 16 * NTT)

        @block.tensor
        def _(pe):
            pe.wait_ge(const_ld, 16 * 4)
            pe.wait_ge(c_ld, 48)
            for k in range(KC):
                ins = pe.transpose(PS[:, 7, 29 * k:29 * k + 29], vrow[:, k * P:(k + 1) * P], ident[0:29, 0:29])
            ins.then_inc(ct_pe, 1)
            pe.wait_ge(ct_dve, 1)
            for ch in range(6):
                pe.wait_ge(adaw_ld[ch % 2], 16 * (ch // 2 + 1))
                if ch >= 2:
                    pe.wait_ge(ada_ev, ch - 1)
                for k in range(KC):
                    ins = pe.matmul(PS[0:9, 1 + ch % 2, :], vcol[:, k, 0:9], adaw[ch % 2][:, k, :], start=(k == 0), stop=(k == KC - 1))
                ins.then_inc(ada_mm, 1)
            pe.wait_ge(ada_ev, 4)
            for c in range(16):
                ins = pe.transpose(PS[:, 0, 9 * c:9 * c + 9], adar[:, c * P:(c + 1) * P], ident[0:9, 0:9])
            ins.then_inc(ada_t, 1)
            pe.wait_ge(rel_ld, 64)
            pe.wait_ge(tb_rel, 1)
            pe.wait_ge(pch, 1)
            pe.matmul(PS[0:NH, 7, 0:XW], relx[:, :], krow, start=True, stop=True)
            for m in range(4):
                ins = pe.matmul(PS[:, 7, XW + NH * m:XW + NH * m + NH], kcmpd[:, m, :], relx[:, :], start=True, stop=True)
            ins.then_inc(tb_mm, 1)

            def transpose_x(tt):
                n, bank = rows_of(tt), 3 + 2 * (tt % 2)
                pe.wait_ge(x_n, tt + 1)
                if tt >= 2:
                    pe.wait_ge(h_ev, tt - 1)
                for k in range(KC):
                    ins = pe.transpose(PS[:, bank + k // 4, P * (k % 4):P * (k % 4) + n], xb[tt % 2][0:n, k * P:(k + 1) * P], ident[0:n, 0:n])
                ins.then_inc(x_t, 1)

            def kv(tt):
                n = rows_of(tt)
                pe.wait_ge(h_hi, tt + 1)
                pe.wait_ge(h_lo, tt + 1)
                for c in range(2):
                    m = 2 * tt + c
                    pe.wait_ge(wk_hi, c + 1)
                    pe.wait_ge(wk_lo, c + 1)
                    if m >= 4:
                        pe.wait_ge(kv_ev, m - 3)
                    out = PS[0:n, KVB[m % 4], 0:(KV0, KV1)[c]]
                    for k in range(KC):
                        a, b = hhi[:, k, tt * P:tt * P + n], hlo[:, k, tt * P:tt * P + n]
                        pe.matmul(out, a, wkh[c][:, k, :], start=(k == 0), stop=False)
                        pe.matmul(out, a, wkl[c][:, k, :], start=False, stop=False)
                        ins = pe.matmul(out, b, wkh[c][:, k, :], start=False, stop=(k == KC - 1))
                    ins.then_inc(kv_mm, 1)

            transpose_x(0)
            pe.wait_ge(ada_col, 1)
            pe.wait_ge(ada_ev, 6)
            pe.wait_ge(tb_ev, 2)
            for tt in range(NTT):
                if tt + 1 < NTT:
                    transpose_x(tt + 1)
                kv(tt)
            pe.wait_ge(kv_ev, 2 * NTT)
            pe.wait_ge(h_ev, NTT)

            def project(j, kind, first):
                n = NK * j + kind
                pe.wait_ge(w_hi, n + 1)
                pe.wait_ge(w_lo, n + 1)
                if not first:
                    pe.wait_ge(p2_ev[kind % 2], NK // 2 * j + kind // 2)
                bank = 3 * (kind % 2)
                for k in range(KC):
                    for a, b in ((wh, hhi), (wh, hlo), (wl, hhi)):
                        for c in range(3):
                            ins = pe.matmul(PS[:, bank + c, 0:CH], a[kind % 2][:, k, :], b[:, k, c * CH:(c + 1) * CH],
                                            start=(k == 0 and b is hhi and a is wh), stop=(k == KC - 1 and a is wl))
                ins.then_inc(p2_mm, 1)

            def tails(j):
                pe.wait_ge(tail_rdy, j + 1)
                if j >= 1:
                    pe.wait_ge(tail_ev, j)
                pe.transpose(PS[0:18, 6, 0:P], tail[:, :], ident[:, :]).then_inc(tail_t, 1)

            for j in range(8):
                for kind in range(NK):
                    project(j, kind, j == 0 and kind < 2)
                    if kind == ZC:
                        tails(j)
            for e in (0, 1):
                pe.wait_ge(p2_ev[e], 24)
            pe.wait_ge(tail_ev, 8)
            for c in range(2):
                def turn(t):
                    if t == 0:
                        pe.wait_ge(xbl_ld[0], 16 * (c + 1))
                        pe.wait_ge(xbl_ld[1], 16 * (c + 1))
                        pe.wait_ge(xpl_ld, 48 * (c + 1))
                    n = 64 * c + t
                    if n >= 4:
                        pe.wait_ge(xe[t % 2], n // 2 - 1)
                    col = slice(t * DKV, (t + 1) * DKV)
                    pe.transpose(PS[:, t % 4, 0:P], xbl[0][:, col], ident[:, :])
                    pe.transpose(PS[:, t % 4, P:2 * P], xbl[1][:, col], ident[:, :])
                    pe.transpose(PS[:, t % 4, 2 * P:CB], xpl[:, col], ident[0:NPB + 1, 0:NPB + 1]).then_inc(x3_t, 1)

                def pair(m):
                    if m == 0:
                        pe.wait_ge(w12_ld, 48 * (c + 1))
                    for e in (0, 1):
                        pe.wait_ge(xe[e], 32 * c + m + 1)
                    for g in range(NG):
                        ins = pe.matmul(PS[:, 4 + g, 0:CB], w1[:, m, :], xt[m % 2][:, g, :], start=(m == 0), stop=(m == 31))
                    ins.then_inc(x3_mm, 1)

                turn(0)
                turn(1)
                for m in range(32):
                    if m < 31:
                        turn(2 * m + 2)
                        turn(2 * m + 3)
                    pair(m)
                pe.wait_ge(hs_rdy, c + 1)
                if c == 0:
                    for g in range(NG):
                        pe.matmul(PS[64 * g:64 * g + 64, 6, 0:2 * P], w2[:, 0:64], hs3[:, g, 0:2 * P], start=True, stop=True)
                    for g in range(NG):
                        ins = pe.matmul(PS[:, 7, NPB * g:NPB * g + NPB], w2[:, :], hs3[:, g, 2 * P:2 * P + NPB], start=True, stop=True)
                    ins.then_inc(k3_mm, 1)
                else:
                    pe.wait_ge(k3_ev, 2)
                    for b in range(NB):
                        for g in range(NG):
                            pe.matmul(PS[0:NSB, 6 + b // 4, (b % 4) * P + 64 * g:(b % 4) * P + 64 * g + 64], hs3[:, g, NSB * b:NSB * b + NSB], w2[:, 0:64], start=True, stop=True)
                    for g in range(NG):
                        ins = pe.matmul(PS[0:NPB, 4, 64 * g:64 * g + 64], hs3[:, g, 2 * P:2 * P + NPB], w2[:, 0:64], start=True, stop=True)
                    ins.then_inc(v3_mm, 1)
            pe.wait_ge(xe[0], 64)
            pe.wait_ge(xe[1], 64)
            for a, col in enumerate((C_KS, C_KW)):
                for half in range(2):
                    for q in range(4):
                        ins = pe.transpose(PS[:, 2 * a + half, q * P:(q + 1) * P], kvt[:, 4 * half + q, col:col + DKV], ident[:, :])
                    ins.then_inc(kt_t, 1)
            pe.wait_ge(kt_hi, 4)
            pe.wait_ge(kt_lo, 4)
            pe.wait_ge(vb_hi, 2)
            pe.wait_ge(vb_lo, 2)
            pe.wait_ge(v3_ev, 3)
            pe.wait_ge(k3_ev, 2)

            def scores(w, h):
                u, n = w // 2, 4 * w + h
                g, hs, i = unit(u)
                if h == 0:
                    pe.wait_ge(q_ld[u % 4], 16 * (u // 4 + 1))
                if n >= 2:
                    pe.wait_ge(e_done, n - 1)
                b0 = 2 * (n % 2)
                q = qb[u % 4][:, h, :]
                kh, kl = (ksh, ksl) if w % 2 == 0 else (kwh, kwl)
                k, parts = keys_of(w)
                a = (i + 1) * P - k
                for c, m in enumerate(parts):
                    last, masked = c == len(parts) - 1, w % 2 and i >= 4 and c == 0
                    pe.matmul(PS[:, b0 + c, 0:m], q, kh[:, g, a:a + m], start=True, stop=False)
                    ins = pe.matmul(PS[:, b0 + c, 0:m], q, kl[:, g, a:a + m], start=False, stop=not (last or masked))
                    if masked:
                        ins = pe.matmul(PS[:, b0 + c, 0:P], identr[:, :], edger[:, :], start=False, stop=not last)
                    if last:
                        r = min(2 * P, k)
                        head = HPG * g + 4 * hs + h
                        pe.matmul(PS[:, b0 + c, m - r:m], identr[:, :], near[:, head, 2 * P - r:2 * P], start=False, stop=False)
                        ins = pe.matmul(PS[:, b0 + c, m - r:m], identr[:, :], nearl[:, head, 2 * P - r:2 * P], start=False, stop=True)
                    a += m
                if w % 2 and h == 3:
                    for hh in range(4):
                        c0_ = 384 + 2 * NPB * hh
                        ins = pe.matmul(PS[:, b0 + 1, c0_:c0_ + 2 * NPB], qb[u % 4][:, hh, :], kcp[:, g, :], start=True, stop=True)
                ins.then_inc(s_mm, 1)

            def turn_p(w, t):
                tc = tile0[w] + t
                if t == 0:
                    if ON_ACT[w % 2]:
                        pe.wait_ge(n_act, (w + 1) if ACT_A and ACT_B else w // 2 + 1)
                    pe.wait_ge(n_dve, w + 1)
                if tc >= 2:
                    pe.wait_ge(pt_hi, tc - 1)
                    pe.wait_ge(pt_lo, tc - 1)
                for h in range(4):
                    cmp_ = w % 2 and t == tiles_of(w) - 1
                    src = prc[w % 3][:, h, :] if cmp_ else pr[w % 3][:, h, t * P:(t + 1) * P]
                    ins = pe.transpose(PS[:, 4 + tc % 2, h * P:(h + 1) * P], src, ident[:, :])
                ins.then_inc(t_mm, 1)

            def values(w, t):
                tc, u = tile0[w] + t, w // 2
                g, hs, i = unit(u)
                pe.wait_ge(pt_hi, tc + 1)
                pe.wait_ge(pt_lo, tc + 1)
                first, last = w % 2 == 0 and t == 0, w % 2 == 1 and t == tiles_of(w) - 1
                if first and u:
                    pe.wait_ge(o_ev, u)
                v = vsx[:, t, g, :] if w % 2 == 0 else vcp[:, g, :] if last else vwx[:, max(0, i - 4) + t, g, :]
                pe.matmul(PS[:, 6, :], v, pth[tc % 2][:, :], start=first, stop=False)
                pe.matmul(PS[:, 6, :], v, ptl[tc % 2][:, :], start=False, stop=last).then_inc(pv_mm, 1)

            def reduce_o(u):
                g = unit(u)[0]
                pe.wait_ge(o_ev, u + 1)
                if u:
                    pe.wait_ge(r_ev, u)
                pe.matmul(PS[64 * g:64 * g + 64, 7, :], stack2[:, :], osb[:, :], start=True, stop=True).then_inc(r_mm, 1)

            pe.wait_ge(vb_hi, 5)
            pe.wait_ge(vb_lo, 3)
            for w in range(2):
                for h in range(4):
                    scores(w, h)
            behind = None
            for w in range(NI):
                for h, part in enumerate(slots(w)):
                    for t in part or [None]:
                        if t is not None:
                            turn_p(w, t)
                        if t in (None, part.start) and w + 2 < NI:
                            scores(w + 2, h)
                        if t is not None:
                            if behind:
                                values(*behind)
                            behind = (w, t)
                    if h == 2 and w % 2 == 0 and w:
                        reduce_o(w // 2 - 1)
            values(*behind)
            reduce_o(NU - 1)
            pe.wait_ge(r_ev, NU)
            pe.wait_ge(pt_lo, tile0[NI])
            pe.wait_ge(c5_ld, 16 * 10)
            gi = [0]

            def group(ops):
                n = gi[0]
                if n >= 2:
                    pe.wait_ge(ev5, n - 1)
                for q, (k, src) in enumerate(ops):
                    ins = pe.transpose(PS[0:k, 6 + n % 2, q * P:(q + 1) * P], src, ident[:, :])
                ins.then_inc(t5, 1)
                gi[0] += 1

            for a, col in enumerate((C_KS, C_KW)):
                ins = pe.transpose(PS[:, 5, 256 + SAMP * a:256 + SAMP * a + SAMP], kvs[0:SAMP, col:col + DKV], ident[0:SAMP, 0:SAMP])
            ins.then_inc(kn_t, 1)
            pe.wait_ge(kn_ev, 1)
            pe.wait_ge(q5_rdy, 1)

            turns5 = [0]

            def bank5():
                if turns5[0]:
                    pe.wait_ge(b5_rd, turns5[0])
                turns5[0] += 1

            def first_scores(pq):
                bank5()
                for b2 in range(2):
                    ins = pe.matmul(PS[64 * b2:64 * b2 + 64, 5, 64:96], qbd[:, 2 * pq + b2, :], kcs[:, NSB * (2 * pq + b2):NSB * (2 * pq + b2 + 1)], start=True, stop=True)
                ins.then_inc(s5c_mm, 1)

            def key_turns(pq):
                for b2 in range(2):
                    pe.wait_ge(kg_ld[b2], 16 * (pq + 1))
                    pe.wait_ge(kw_ld[b2], 16 * (pq + 1))
                    for q in range(NSEL // 4):
                        group([(P, kb[b2][:, 4 * q + r, :]) for r in range(4)])
                    group([(P, kwb[b2][:, r, :]) for r in range(4)])

            def pair_scores(pq):
                pe.wait_ge(ev5, 16 * pq + 10 - 6 * (pq > 0))
                if pq:
                    pe.wait_ge(s5_ev, pq)
                for b2 in range(2):
                    q = qbd[:, 2 * pq + b2, :]
                    half = slice(64 * b2, 64 * b2 + 64)
                    kt = kt5[b2][:, :, :].rearrange("p i c -> p (i c)")
                    for c in range(5):
                        pe.matmul(PS[half, c, :], q, kt[:, 512 * c:512 * c + 512], start=True, stop=True)
                bank5()
                for b2 in range(2):
                    q = qbd[:, 2 * pq + b2, :]
                    half = slice(64 * b2, 64 * b2 + 64)
                    for a in range(2):
                        ins = pe.matmul(PS[half, 5, SAMP * a:SAMP * a + SAMP], q, knt[:, a, :], start=True, stop=True)
                ins.then_inc(s5_mm, 1)

            def importance(pq):
                pe.wait_ge(pn_rdy, pq + 1)
                bank5()
                pe.matmul(PS[:, 5, 96:128], grp[:, :], pn[:, :], start=True, stop=True).then_inc(imp_mm, 1)

            def pair_values(pq):
                pe.wait_ge(p5, pq + 1)
                s = s5[pq % 2]
                pos = [P * r for r in range(NSEL)] + [SEL + P * r for r in range(NWIN)]
                for q in range(5):
                    group([(P, s[:, a:a + P]) for a in pos[4 * q:4 * q + 4]])
                group([(SAMP, s[:, PAST:SEL]), (SAMP, s[:, SEL + WIN:SEL + WN]), (NSB, cmg[:, :])])
                pe.wait_ge(ev5, gi[0])
                bank5()
                for b2 in range(2):
                    b = 2 * pq + b2
                    pe.wait_ge(vg_ld[b % 4], 16 * (b // 4 + 1))
                    pe.wait_ge(vw_ld[b % 4], 16 * (b // 4 + 1))
                    half = slice(64 * b2, 64 * b2 + 64)
                    ops = [(pt5[:, r, half], vb[b % 4][:, r, :]) for r in range(NSEL)]
                    ops += [(pt5[:, NSEL + r, half], vwb[b % 4][:, r, :]) for r in range(NWIN)]
                    ops += [(pt5[0:SAMP, 20, half], kvs[0:SAMP, C_VS:C_VS + DKV]), (pt5[0:SAMP, 21, half], kvs[0:SAMP, C_VW:C_VW + DKV]),
                            (pt5[0:NSB, 22, half], vcs[:, b, :])]
                    for n, (a, v) in enumerate(ops):
                        ins = pe.matmul(PS[half, 5, P:2 * P], a, v, start=(n == 0), stop=(n == len(ops) - 1))
                ins.then_inc(o5_mm, 1)
                bank5()
                pe.wait_ge(o5_cp, pq + 1)
                pe.transpose(PS[:, 5, 256:384], o5[:, :], ident[:, :]).then_inc(ot_t, 1)

            first_scores(0)
            key_turns(0)
            pair_scores(0)
            importance(0)
            for pq in range(4):
                if pq < 3:
                    first_scores(pq + 1)
                    key_turns(pq + 1)
                    pair_scores(pq + 1)
                    importance(pq + 1)
                pair_values(pq)
            pe.wait_ge(mix5_rdy, 4)
            pe.wait_ge(s5_ev, 4)
            pe.wait_ge(ev5, gi[0])
            for tt in range(NTT):
                n, b0 = rows_of(tt), 2 * (tt % 4)
                pe.wait_ge(m_hi, tt + 1)
                pe.wait_ge(m_lo, tt + 1)
                if tt >= 4:
                    pe.wait_ge(y_ev, tt - 3)
                for k in range(16):
                    if tt == 0:
                        pe.wait_ge(wo_hi, k + 1)
                        pe.wait_ge(wo_lo, k + 1)
                    for a, b in ((mh, woh), (mh, wol), (ml, woh)):
                        for c in range(2):
                            ins = pe.matmul(PS[0:n, b0 + c, :], a[:, k, 0:n], b[:, k, 512 * c:512 * c + 512],
                                            start=(k == 0 and a is mh and b is woh), stop=(k == 15 and a is ml))
                ins.then_inc(y_mm, 1)

        @block.scalar
        def _(act):
            def hi(tt):
                n = rows_of(tt)
                act.wait_ge(h_ev, tt + 1)
                act.activation(hhi[:, :, tt * P:tt * P + n], h32[:, :, 0:n], ACT.Copy).then_inc(h_hi, 1)

            def kv_evac(tt, c):
                m, n = 2 * tt + c, rows_of(tt)
                act.wait_ge(kv_mm, m + 1)
                cols = slice(c * KV0, c * KV0 + (KV0, KV1)[c])
                act.activation(kvt[:, tt, cols] if tt < NTT - 1 else kvs[0:n, cols], PS[0:n, KVB[m % 4], 0:(KV0, KV1)[c]], ACT.Copy).then_inc(kv_ev, 1)

            for tt in range(NTT):
                n = rows_of(tt)
                act.wait_ge(x_ld[tt % 2], 16 * (tt // 2 + 1))
                if tt:
                    act.wait_ge(h_lo, tt)
                    act.wait_ge(h_hi, tt)
                act.activation(h32[0:n, :, :].rearrange("p a b -> p (a b)"), xb[tt % 2][0:n, :], ACT.Square,
                               accum_out=ssq[0:n, tt:tt + 1]).then_inc(x_sq, 1)
                act.wait_ge(x_ms, tt + 1)
                act.activation(rms[0:n, tt:tt + 1], ms[0:n, tt:tt + 1], ACT.Sqrt).then_inc(x_rms, 1)
                if tt == 0:
                    act.wait_ge(ada_t, 1)
                    act.wait_ge(ada_mm, 6)
                    act.wait_ge(ada_ev, 6)
                    act.wait_ge(wk_ld, 32)
                    for c in range(2):
                        act.activation(wkh[c][:, :, :], wkr[c][:, :, :], ACT.Copy).then_inc(wk_hi, 1)
                hi(tt)
                if tt:
                    kv_evac(tt - 1, 0)
                    kv_evac(tt - 1, 1)
            kv_evac(NTT - 1, 0)
            kv_evac(NTT - 1, 1)

            act.wait_ge(kv_mm, 2 * NTT)
            act.wait_ge(h_lo, NTT)

            def split(j, kind, first):
                n = NK * j + kind
                act.wait_ge(wr_ld[kind % 2], wr_count(j, kind))
                if not first:
                    act.wait_ge(p2_mm, n - 1)
                act.activation(wh[kind % 2][:, :, :], wr[kind % 2][:, :, :], ACT.Copy).then_inc(w_hi, 1)

            def ev(j, kind):
                n = NK * j + kind
                src = PS[:, 3 * (kind % 2):3 * (kind % 2) + 3, 0:CH]
                act.wait_ge(p2_mm, n + 1)
                v = lambda t: t[:, 0:TOK].rearrange("p (a b) -> p a b", a=3)
                if kind == CC:
                    if j:
                        act.wait_ge(p2_ev[1], 3 * j - 2)
                    act.activation(v(cct), src, ACT.Copy).then_inc(p2_ev[0], 1)
                elif kind == ZC:
                    if j:
                        act.wait_ge(y_rdy, j)
                    act.activation(v(zt), src, ACT.Silu).then_inc(p2_ev[1], 1)
                elif kind == ZA:
                    if j:
                        act.wait_ge(zab_st, 16 * j)
                    act.activation(v(zab), src, ACT.Silu).then_inc(p2_ev[0], 1)
                elif kind == QQ:
                    if j:
                        act.wait_ge(q_st, 64 * j)
                    act.activation(v(qhi), src, ACT.Copy, scale=0.125).then_inc(q_hi, 1)

            split(0, 0, True)
            for j in range(8):
                for kind in range(NK):
                    if not (j == 7 and kind == NK - 1):
                        jn, kn = (j, kind + 1) if kind + 1 < NK else (j + 1, 0)
                        split(jn, kn, j == 0 and kind == 0)
                    ev(j, kind)
            act.activation(sg[:, 0:8, :], kvt[:, 0:8, C_G:C_G + 3 * NH], ACT.Sigmoid).then_inc(sg_rdy, 1)
            act.activation(sg[0:SAMP, 8, :], kvs[0:SAMP, C_G:C_G + 3 * NH], ACT.Sigmoid).then_inc(sg_rdy, 1)
            for c in range(2):
                for m in range(32):
                    act.wait_ge(x3_t, 64 * c + 2 * m + 2)
                    if 32 * c + m >= 2:
                        act.wait_ge(x3_mm, 32 * c + m - 1)
                    bank = (2 * m + 1) % 4
                    for g in range(NG):
                        ins = act.activation(xt[m % 2][64:128, g, :], PS[64 * g:64 * g + 64, bank, 0:CB], ACT.Copy)
                    ins.then_inc(xe[1], 1)
                act.wait_ge(pe_rdy, c + 1)
                act.wait_ge(x3_mm, 32 * (c + 1))
                if c:
                    act.wait_ge(k3_mm, 1)
                for g in range(NG):
                    ins = act.activation(hs3[:, g, :], PS[:, 4 + g, 0:CB], ACT.Silu, bias=pebias[:, c:c + 1])
                ins.then_inc(hs_rdy, 1)
                if c == 0:
                    act.wait_ge(k3_mm, 1)
                    act.activation(kcp[:, :, 0:NPB], PS[:, 7, 0:2 * NPB].rearrange("p (g n) -> p g n", g=NG), ACT.Copy).then_inc(k3_hi, 1)
                else:
                    act.wait_ge(v3_mm, 1)
                    act.wait_ge(pad0, 1)
                    act.activation(vcp[0:NPB, :, 0:64], PS[0:NPB, 4, 0:P].rearrange("p (g d) -> p g d", g=NG), ACT.Copy).then_inc(v3_hi, 1)
            act.wait_ge(v3_mm, 1)
            for a, kh in enumerate((ksh, kwh)):
                for half in range(2):
                    act.wait_ge(kt_t, 2 * a + half + 1)
                    for g in range(NG):
                        for r in range(2):
                            ins = act.activation(kh[64 * r:64 * r + 64, g, 512 * half:512 * half + 512], PS[64 * g:64 * g + 64, 2 * a + half, :], ACT.Copy)
                    ins.then_inc(kt_hi, 1)
            for v, col in ((vsx, C_VS), (vwx, C_VW)):
                act.activation(v[:, :, :, 0:64], kvt[:, 0:8, col:col + DKV].rearrange("p t (g d) -> p t g d", g=NG), ACT.Copy).then_inc(vb_hi, 1)

            act.wait_ge(c4_ld, 64)
            act.activation(identr[:, :], ident[:, :], ACT.Copy).then_inc(vb_hi, 1)
            act.activation(edger[:, :], edge[:, :], ACT.Copy).then_inc(vb_hi, 1)
            act.activation(near[:, :, :], nearr, ACT.Copy).then_inc(vb_hi, 1)

            def exps(w, h):
                n, u = 4 * w + h, w // 2
                g, hs, i = unit(u)
                act.wait_ge(m_rdy, n + 1)
                if h == 0 and w >= 3:
                    act.wait_ge(t_mm, tile0[w - 2])
                k, parts = keys_of(w)
                b0, r = 2 * (n % 2), w % 3
                out = pr[r][:, h, 0:k].rearrange("p (a b) -> p a b", a=len(parts))
                act.activation(out, PS[:, b0:b0 + len(parts), 0:parts[0]], ACT.Exp, bias=nm[:, r, h:h + 1], accum_out=rsum[:, r, h:h + 1]).then_inc(e_done, 1)
                if w % 2 and h == 3:
                    act.wait_ge(mc_rdy, u + 1)
                    act.activation(prc[r][:, :, 0:2 * i + 2], cs[:, :, 0:2 * i + 2], ACT.Exp).then_inc(ec_done, 1)

            def scale(w):
                act.wait_ge(r_rdy, w + 1)
                for h in sorted(ON_ACT[w % 2]):
                    k, r = keys_of(w)[0], w % 3
                    ins = act.activation(pr[r][:, h, 0:k], pr[r][:, h, 0:k], ACT.Copy, scale=rg[:, r, h:h + 1])
                ins.then_inc(n_act, 1)

            def high(w, t):
                tc = tile0[w] + t
                act.wait_ge(t_mm, tc + 1)
                if tc >= 2:
                    act.wait_ge(pv_mm, tc - 1)
                act.activation(pth[tc % 2][:, :], PS[:, 4 + tc % 2, :], ACT.Copy).then_inc(pt_hi, 1)

            def sums(u):
                act.wait_ge(pv_mm, tile0[2 * u + 2])
                if u:
                    act.wait_ge(r_mm, u)
                act.activation(osb[:, :], PS[:, 6, :], ACT.Copy).then_inc(o_ev, 1)

            for w in range(2):
                for h in range(4):
                    exps(w, h)
            scale(0)
            behind, ahead = None, None
            for w in range(NI):
                for h, part in enumerate(slots(w)):
                    for t in part or [None]:
                        if t is not None:
                            high(w, t)
                            if behind is not None:
                                sums(behind)
                                behind = None
                        if t in (None, part.start):
                            if ahead:
                                exps(*ahead)
                            ahead = (w + 2, h) if w + 2 < NI else None
                    if w + 1 < NI and h == 2:
                        scale(w + 1)
                if w % 2:
                    behind = w // 2
            sums(NU - 1)
            act.wait_ge(r_mm, NU)
            act.wait_ge(kn_t, 1)
            act.activation(knt[:, :, :], PS[:, 5, 256:256 + 2 * SAMP].rearrange("p (a c) -> p a c", a=2), ACT.Copy).then_inc(kn_ev, 1)
            gi = [0]

            def copy_group(dst, k=P, m=4):
                n = gi[0]
                act.wait_ge(t5, n + 1)
                act.activation(dst, PS[0:k, 6 + n % 2, 0:m * P].rearrange("p (a c) -> p a c", a=m), ACT.Copy).then_inc(ev5, 1)
                gi[0] += 1

            def key_copies(pq):
                if pq:
                    act.wait_ge(s5_mm, pq)
                for b2 in range(2):
                    for q in range(5):
                        copy_group(kt5[b2][:, 4 * q:4 * q + 4, :])

            def exp_cmp(pq):
                act.wait_ge(m5c, pq + 1)
                act.activation(cm[:, :], cm[:, :], ACT.Exp, bias=n5[:, 2:3], accum_out=r5[:, 2:3]).then_inc(e5c, 1)

            def exp_rest(pq):
                act.wait_ge(m5, pq + 1)
                s = s5[pq % 2]
                act.activation(s[:, 0:SEL], s[:, 0:SEL], ACT.Exp, bias=n5[:, 0:1], accum_out=r5[:, 0:1])
                act.activation(s[:, SEL:SEL + WN], s[:, SEL:SEL + WN], ACT.Exp, bias=n5[:, 1:2], accum_out=r5[:, 1:2]).then_inc(e5, 1)

            exp_cmp(0)
            key_copies(0)
            exp_rest(0)
            for pq in range(4):
                if pq < 3:
                    exp_cmp(pq + 1)
                    key_copies(pq + 1)
                if pq:
                    act.wait_ge(o5_mm, pq)
                for q in range(5):
                    copy_group(pt5[:, 4 * q:4 * q + 4, :])
                copy_group(pt5[0:SAMP, 20:23, :], SAMP, 3)
                act.wait_ge(o5_mm, pq + 1)
                act.activation(o5[:, :], PS[:, 5, P:2 * P], ACT.Copy).then_inc(o5_cp, 1)
                act.wait_ge(o5_cp, pq + 1)
                act.sem_inc(b5_rd, 1)
                if pq < 3:
                    exp_rest(pq + 1)
            act.wait_ge(o5_mm, 4)
            act.wait_ge(ot_t, 4)

            def wo_high(j):
                act.wait_ge(wo_ld[j % 2], 16 * (2 * (j // 2 + 1) if j < 8 else 8 + (j - 8) // 2 + 1))
                act.activation(woh[:, j, :], wor[j % 2][:, :], ACT.Copy).then_inc(wo_hi, 1)

            def mix_high(tt):
                n = rows_of(tt)
                act.wait_ge(mr_ld[tt % 2], 16 * (tt // 2 + 1))
                if tt:
                    act.wait_ge(y_mm, tt)
                act.activation(mh[:, :, 0:n], mr[tt % 2][:, :, 0:n], ACT.Copy).then_inc(m_hi, 1)

            def squares(tt):
                n = rows_of(tt)
                act.wait_ge(y_sum, tt + 1)
                if tt:
                    act.wait_ge(y_st, 16 * tt)
                act.activation(yo[0:n, :], yf[0:n, :], ACT.Square, accum_out=s6[0:n, 0:1]).then_inc(y_sq, 1)
                act.wait_ge(y_ms, tt + 1)
                act.activation(s6[0:n, 2:3], s6[0:n, 1:2], ACT.Sqrt).then_inc(y_rms, 1)

            mix_high(0)
            for j in range(16):
                wo_high(j)
            for tt in range(NTT):
                if tt + 1 < NTT:
                    mix_high(tt + 1)
                squares(tt)

        @block.vector
        def _(dve):
            chain = Chain(dve, dch)
            link = chain.link
            dve.wait_ge(rel_ld, 64)
            dve.wait_ge(idx_ld, 16 * (2 + NB))
            dve.wait_ge(idx_a, 1)
            link(dve.tensor_scalar(pidx[:, 1:2], pidx[:, 0:1], 7, None, ALU.bitwise_and))
            link(dve.tensor_scalar(pidx[:, 0:1], pidx[:, 0:1], 1, None, ALU.bitwise_and))
            dve.scalar_tensor_tensor(idxc[:, :], pgc[:, :], 2, ext(bass.AP(pidx[:, 0:1].tensor, pidx[:, 0:1].offset, [list(pidx[:, 0:1].ap[0])]), (0, 2)), ALU.mult, ALU.add).then_inc(idx_b, 1)
            dve.scalar_tensor_tensor(idxs[:, :], pgs[:, :], 8, ext(bass.AP(pidx[:, 1:2].tensor, pidx[:, 1:2].offset, [list(pidx[:, 1:2].ap[0])]), (0, NB)), ALU.mult, ALU.add).then_inc(idx_b, 1)
            dve.wait_ge(ct_pe, 1)
            dve.tensor_copy(vcol[:, :, :], PS[:, 7, 0:232].rearrange("p (k c) -> p k c", c=29)).then_inc(ct_dve, 1)
            dve.wait_ge(ct_dve, 1)
            dve.tensor_tensor(relx[0:32, :], relx[0:32, :], rel31[:, :], ALU.subtract).then_inc(tb_rel, 1)
            for ch in range(6):
                dve.wait_ge(ada_mm, ch + 1)
                out = adar[:, 512 * ch:512 * ch + 512] if ch < 4 else gate[:, 512 * (ch - 4):512 * (ch - 3)]
                dve.tensor_tensor(out, PS[0:9, 1 + ch % 2, :], adab[:, 512 * ch:512 * ch + 512], ALU.add).then_inc(ada_ev, 1)
            dve.wait_ge(ada_t, 1)
            both = PS[:, 0, 0:144].rearrange("p (k c) -> p k c", c=9)
            link(dve.tensor_copy(scB[:, :, :], both[:, 0:8, :]))
            dve.scalar_tensor_tensor(scA[:, :, :], both[:, 8:16, :], 1.0, ext(vcol[:, :, 9], (0, 9)), ALU.add, ALU.mult).then_inc(ada_col, 1)
            dve.wait_ge(ada_col, 1)
            dve.wait_ge(tb_mm, 1)
            dve.tensor_copy(rows[:, :], PS[0:NH, 7, 0:XW]).then_inc(tb_ev, 1)
            dve.tensor_copy(tcmp[:, :, :], PS[:, 7, XW:XW + 64].rearrange("p (m h) -> p m h", m=4)).then_inc(tb_ev, 1)
            for tt in range(NTT):
                n = rows_of(tt)
                one = slice(tt, tt + 1)
                dve.wait_ge(x_sq, tt + 1)
                dve.tensor_scalar(ms[0:n, one], ssq[0:n, one], 1.0 / D, EPS, ALU.mult, ALU.add).then_inc(x_ms, 1)
                dve.wait_ge(x_rms, tt + 1)
                link(dve.reciprocal(rstd[0:n, one], rms[0:n, one]))
                dve.tensor_scalar(xb[tt % 2][0:n, :], xb[tt % 2][0:n, :], rstd[0:n, one], None, ALU.mult).then_inc(x_n, 1)
                if tt == 0:
                    for c in range(2):
                        dve.wait_ge(wk_hi, c + 1)
                        dve.tensor_tensor(wkl[c][:, :, :], wkr[c][:, :, :], f32(wkh[c][:, :, :]), ALU.subtract).then_inc(wk_lo, 1)
                dve.wait_ge(x_t, tt + 1)
                bank = 3 + 2 * (tt % 2)
                for k in range(KC):
                    src = PS[:, bank + k // 4, P * (k % 4):P * (k % 4) + n]
                    if tt < NTT - 1:
                        ins = dve.tensor_scalar(h32[:, k, 0:n], src, scA[:, k, 0:1], scB[:, k, 0:1], ALU.mult, ALU.add)
                    else:
                        v = lambda t: t.rearrange("p (b t) -> p b t", t=TS)
                        link(dve.tensor_tensor(v(h32[:, k, 0:n]), v(src), ext(scA[:, k, 1:9], (0, TS)), ALU.mult))
                        ins = dve.tensor_tensor(v(h32[:, k, 0:n]), v(h32[:, k, 0:n]), ext(scB[:, k, 1:9], (0, TS)), ALU.add)
                    if k < KC - 1:
                        link(ins) if tt == NTT - 1 else ins.then_inc(dch, 1)
                        if tt < NTT - 1:
                            chain.n += 1
                dve.wait_ge(dch, chain.n)
                ins.then_inc(h_ev, 1)
                dve.wait_ge(h_ev, tt + 1)
                dve.wait_ge(h_hi, tt + 1)
                dve.tensor_tensor(hlo[:, :, tt * P:tt * P + n], h32[:, :, 0:n], f32(hhi[:, :, tt * P:tt * P + n]), ALU.subtract).then_inc(h_lo, 1)
            dve.wait_ge(kv_mm, 2 * NTT)
            dve.wait_ge(h_lo, NTT)
            link(dve.memset(uu[:, 0:2], 0.0))

            def split(j, kind, first):
                n = NK * j + kind
                dve.wait_ge(w_hi, n + 1)
                if not first:
                    dve.wait_ge(p2_mm, n - 1)
                dve.tensor_tensor(wl[kind % 2][:, :, :], wr[kind % 2][:, :, :], f32(wh[kind % 2][:, :, :]), ALU.subtract).then_inc(w_lo, 1)

            def ev(j, kind):
                n = NK * j + kind
                src = PS[:, 3 * (kind % 2):3 * (kind % 2) + 3, 0:CH]
                v = lambda t: t[:, 0:TOK].rearrange("p (a b) -> p a b", a=3)
                if kind == HC:
                    dve.wait_ge(p2_mm, n + 1)
                    dve.wait_ge(p2_ev[0], 3 * j + 1)
                    if j:
                        dve.wait_ge(tail_t, j)
                    dve.tensor_tensor(v(uu[:, 2:2 + TOK]), src, v(cct), ALU.mult).then_inc(p2_ev[1], 1)
                    dve.wait_ge(p2_ev[1], 3 * j + 1)
                    us_new = uu[:, 2 + S:2 + TOK].rearrange("p (b t) -> p b t", t=TS)
                    link(dve.tensor_copy(us[:, :, 0:2], vcol[:, j, 13:29].rearrange("p (b r) -> p b r", r=2)))
                    link(dve.tensor_copy(us[:, :, 2:6], us_new))
                    link(dve.tensor_copy(tail[:, 0:2], uu[:, S:2 + S]))
                    dve.tensor_copy(tail[:, 2:18].rearrange("p (b r) -> p b r", r=2), us_new[:, :, 2:4]).then_inc(tail_rdy, 1)
                    ys = yy[:, S:TOK].rearrange("p (b t) -> p b t", t=TS)
                    link(dve.tensor_scalar(yy[:, 0:S], uu[:, 2:2 + S], vcol[:, j, 12:13], None, ALU.mult))
                    link(dve.tensor_scalar(ys, us[:, :, 2:6], vcol[:, j, 12:13], None, ALU.mult))
                    for r in (1, 0):
                        link(dve.scalar_tensor_tensor(yy[:, 0:S], uu[:, r:r + S], vcol[:, j, 10 + r:11 + r], yy[:, 0:S], ALU.mult, ALU.add))
                        link(dve.scalar_tensor_tensor(ys, us[:, :, r:r + TS], vcol[:, j, 10 + r:11 + r], ys, ALU.mult, ALU.add))
                elif kind == BC:
                    dve.wait_ge(p2_mm, n + 1)
                    dve.tensor_tensor(v(yy), src, v(yy), ALU.mult).then_inc(p2_ev[0], 1)
                    dve.wait_ge(p2_ev[0], 3 * j + 2)
                elif kind == ZC:
                    dve.wait_ge(p2_ev[1], 3 * j + 2)
                    if j:
                        dve.wait_ge(ych_st, 16 * j)
                    dve.tensor_tensor(ych[:, :], yy[:, :], zt[:, :], ALU.mult).then_inc(y_rdy, 1)
                    dve.wait_ge(tail_t, j + 1)
                    dve.tensor_copy(tailr[:, j * P:(j + 1) * P], PS[0:18, 6, 0:P]).then_inc(tail_ev, 1)
                elif kind == QQ:
                    dve.wait_ge(q_hi, j + 1)
                    if j:
                        dve.wait_ge(q_st, 64 * j)
                    link(dve.tensor_scalar(qs[:, j, :], PS[:, 5, CH - SAMP:CH], 0.125, None, ALU.mult))
                    dve.scalar_tensor_tensor(v(qlo), src, 0.125, f32(v(qhi)), ALU.mult, ALU.subtract).then_inc(p2_ev[1], 1)

            split(0, 0, True)
            for j in range(8):
                for kind in range(NK):
                    if not (j == 7 and kind == NK - 1):
                        jn, kn = (j, kind + 1) if kind + 1 < NK else (j + 1, 0)
                        split(jn, kn, j == 0 and kind == 0)
                    ev(j, kind)
            for c in range(2):
                for m in range(32):
                    dve.wait_ge(x3_t, 64 * c + 2 * m + 1)
                    if 32 * c + m >= 2:
                        dve.wait_ge(x3_mm, 32 * c + m - 1)
                    bank = (2 * m) % 4
                    for g in range(NG):
                        ins = dve.tensor_copy(xt[m % 2][0:64, g, :], PS[64 * g:64 * g + 64, bank, 0:CB])
                    ins.then_inc(xe[0], 1)
                dve.wait_ge(x3_mm, 32 * (c + 1))
                dve.tensor_copy(pebias[:, c:c + 1], PS[:, 4, CB - 1:CB]).then_inc(pe_rdy, 1)
                if c == 0:
                    dve.wait_ge(k3_mm, 1)
                    dve.wait_ge(k3_hi, 1)
                    dve.tensor_copy(kcs[:, :], PS[:, 6, 0:2 * P]).then_inc(k3_ev, 1)
                    dve.tensor_tensor(kcp[:, :, NPB:2 * NPB], PS[:, 7, 0:2 * NPB].rearrange("p (g n) -> p g n", g=NG), f32(kcp[:, :, 0:NPB]), ALU.subtract).then_inc(k3_ev, 1)
                else:
                    dve.wait_ge(v3_mm, 1)
                    dve.wait_ge(v3_hi, 1)
                    for q in range(2):
                        dve.tensor_copy(vcs[:, 4 * q:4 * q + 4, :], PS[0:NSB, 6 + q, :].rearrange("p (b c) -> p b c", c=DKV)).then_inc(v3_ev, 1)
                    dve.tensor_tensor(vcp[0:NPB, :, 64:128], PS[0:NPB, 4, 0:P].rearrange("p (g d) -> p g d", g=NG), f32(vcp[0:NPB, :, 0:64]), ALU.subtract).then_inc(v3_ev, 1)
            dve.wait_ge(v3_mm, 1)
            for a, (kh, kl) in enumerate(((ksh, ksl), (kwh, kwl))):
                for half in range(2):
                    dve.wait_ge(kt_hi, 2 * a + half + 1)
                    cols = slice(512 * half, 512 * half + 512)
                    for g in range(NG):
                        for r in range(2):
                            rr = slice(64 * r, 64 * r + 64)
                            ins = dve.tensor_tensor(kl[rr, g, cols], PS[64 * g:64 * g + 64, 2 * a + half, :], f32(kh[rr, g, cols]), ALU.subtract)
                    ins.then_inc(kt_lo, 1)
            for n, (v, col) in enumerate(((vsx, C_VS), (vwx, C_VW))):
                dve.wait_ge(vb_hi, n + 1)
                dve.tensor_tensor(v[:, :, :, 64:128], kvt[:, 0:8, col:col + DKV].rearrange("p t (g d) -> p t g d", g=NG), f32(v[:, :, :, 0:64]), ALU.subtract).then_inc(vb_lo, 1)
            dve.wait_ge(c4_ld, 64)
            dve.wait_ge(pad0, 2)
            dve.wait_ge(sg_rdy, 2)

            dve.wait_ge(vb_hi, 5)
            dve.wait_ge(vb_lo, 2)
            dve.tensor_tensor(nearl[:, :, :], nearr, f32(near[:, :, :]), ALU.subtract).then_inc(vb_lo, 1)

            def maxima(w, h):
                n, u = 4 * w + h, w // 2
                g, hs, i = unit(u)
                dve.wait_ge(s_mm, n + 1)
                if h == 0 and w >= 3 and ON_ACT[(w - 3) % 2]:
                    dve.wait_ge(n_act, (w - 2) if ACT_A and ACT_B else (w - 3) // 2 + 1)
                k, parts = keys_of(w)
                b0, r = 2 * (n % 2), w % 3
                if w % 2 and h == 0 and i < 3:
                    if w >= 3:
                        dve.wait_ge(t_mm, tile0[w - 2])
                    link(dve.memset(prc[r][:, :, 0:NPB], 0.0))
                both = w % 2 and h == 3
                if both:
                    if u:
                        dve.wait_ge(ec_done, u)
                    dve.tensor_reduce(cs[:, :, :], PS[:, b0 + 1, 384:512].rearrange("p (h a n) -> p h n a", h=4, a=2), AX.X, ALU.add).then_inc(dch, 1)
                    chain.n += 1
                dve.tensor_reduce(nm[:, r, h:h + 1], PS[:, b0:b0 + len(parts), 0:parts[0]], AX.XY, ALU.max, negate=True).then_inc(m_rdy, 1)
                if both:
                    dve.wait_ge(dch, chain.n)
                    m0, head = max(0, 2 * i - 2), HPG * g + 4 * hs
                    cb = 2 * i + 2 - m0
                    row = tcmp[:, 2 * i - m0 + 1, head:head + 1]
                    tab = bass.AP(row.tensor, row.offset, [list(row.ap[0]), [1, 4], [-NH, cb]])
                    link(dve.tensor_tensor(cs[:, :, m0:m0 + cb], cs[:, :, m0:m0 + cb], tab, ALU.add))
                    link(dve.tensor_reduce(nm[:, r, 4:8], cs[:, :, 0:2 * i + 2], AX.X, ALU.max, negate=True))
                    dve.tensor_tensor(cs[:, :, 0:2 * i + 2], cs[:, :, 0:2 * i + 2], ext(nm[:, r, 4:8], (0, 2 * i + 2)), ALU.add).then_inc(mc_rdy, 1)

            def factors(w):
                g, hs, i = unit(w // 2)
                c0_ = HPG * g + 4 * hs
                dve.wait_ge(e_done, 4 * w + 4)
                m, r = (8 if w % 2 else 4), w % 3
                if w % 2:
                    dve.wait_ge(ec_done, w // 2 + 1)
                    link(dve.tensor_reduce(rsum[:, r, 4:8], prc[r][:, :, 0:2 * i + 2], AX.X, ALU.add))
                link(dve.reciprocal(rrec[:, r, 0:m], rsum[:, r, 0:m]))
                if w % 2 == 0:
                    dve.tensor_tensor(rg[:, r, 0:4], rrec[:, r, 0:4], sg[:, i, NH + c0_:NH + c0_ + 4], ALU.mult).then_inc(r_rdy, 1)
                else:
                    if i == 0:
                        link(dve.tensor_scalar(rrec[:, r, 4:8], rrec[:, r, 4:8], anyc[:, :], None, ALU.mult))
                    link(dve.tensor_tensor(rg[:, r, 4:8], rrec[:, r, 4:8], sg[:, i, c0_:c0_ + 4], ALU.mult))
                    dve.tensor_tensor(rg[:, r, 0:4], rrec[:, r, 0:4], sg[:, i, 2 * NH + c0_:2 * NH + c0_ + 4], ALU.mult).then_inc(r_rdy, 1)
                    dve.tensor_tensor(prc[r][:, :, 0:2 * i + 2], prc[r][:, :, 0:2 * i + 2], ext(rg[:, r, 4:8], (0, 2 * i + 2)), ALU.mult)

            def scale(w, h):
                dve.wait_ge(r_rdy, w + 1)
                if h not in ON_ACT[w % 2]:
                    k, r = keys_of(w)[0], w % 3
                    ins = dve.tensor_scalar(pr[r][:, h, 0:k], pr[r][:, h, 0:k], rg[:, r, h:h + 1], None, ALU.mult)
                    if h == max(set(range(4)) - ON_ACT[w % 2]):
                        ins.then_inc(n_dve, 1)

            def low(w, t):
                tc = tile0[w] + t
                dve.wait_ge(pt_hi, tc + 1)
                if tc >= 2:
                    dve.wait_ge(pv_mm, tc - 1)
                dve.tensor_tensor(ptl[tc % 2][:, :], PS[:, 4 + tc % 2, :], f32(pth[tc % 2][:, :]), ALU.subtract).then_inc(pt_lo, 1)

            def gate_o(u):
                g, hs, i = unit(u)
                half = slice(64 * g, 64 * g + 64)
                dve.wait_ge(r_mm, u + 1)
                dve.wait_ge(za_ld[u % 2], 16 * (u // 2 + 1))
                if u >= 2:
                    dve.wait_ge(mix_st[u % 2], 16 * (u // 2))
                dve.tensor_tensor(mixs[u % 2][half, :, :], PS[half, 7, :].rearrange("p (j c) -> p j c", j=4), zau[u % 2][half, :, :], ALU.mult).then_inc(r_ev, 1)

            for w in range(2):
                for h in range(4):
                    maxima(w, h)
                if w == 0:
                    factors(0)
            for h in range(4):
                scale(0, h)
            behind = None
            for w in range(NI):
                for h, part in enumerate(slots(w)):
                    for t in part or [None]:
                        if t is not None:
                            if behind:
                                low(*behind)
                            behind = (w, t)
                        if t in (None, part.start) and w + 2 < NI:
                            maxima(w + 2, h)
                    if w + 1 < NI:
                        if h == 1:
                            factors(w + 1)
                        for hh in ((), (0, 1), (2,), (3,))[h]:
                            scale(w + 1, hh)
                    if h == 3 and w % 2 == 0 and w:
                        gate_o(w // 2 - 1)
            low(*behind)
            gate_o(NU - 1)
            dve.wait_ge(pv_mm, tile0[NI])
            dve.wait_ge(r_mm, NU)
            dve.wait_ge(mix_st[0], 16 * NU // 2)
            dve.wait_ge(mix_st[1], 16 * NU // 2)
            link(dve.memset(qbd[:, :, :], 0.0))
            for g in range(NG):
                half = slice(64 * g, 64 * g + 64)
                ins = dve.tensor_copy(qbd[half, :, 32 * g:32 * g + 32].rearrange("p b (j t) -> p b j t", t=TS),
                                      qs[half, :, :].rearrange("p j (b t) -> p b j t", t=TS))
            ins.then_inc(q5_rdy, 1)
            dve.wait_ge(c5_ld, 16 * 10)
            dve.wait_ge(gr_ld, 16 * 32)

            def choose(pq):
                dve.wait_ge(s5c_mm, pq + 1)
                link(dve.tensor_copy(cm[:, :], PS[:, 5, 64:96]))
                dve.sem_inc(b5_rd, 1)
                link(dve.tensor_tensor(cm[:, 30:32], cm[:, 30:32], nbc[:, :], ALU.add))
                dve.tensor_reduce(n5[:, 2:3], cm[:, :], AX.X, ALU.max, negate=True).then_inc(m5c, 1)
                dve.wait_ge(e5c, pq + 1)
                link(dve.reciprocal(i5[:, 2:3], r5[:, 2:3]))
                dve.tensor_scalar(pn[:, :], cm[:, :], i5[:, 2:3], None, ALU.mult).then_inc(pn_rdy, 1)
                dve.wait_ge(pn_rdy, pq + 1)
                dve.wait_ge(s5_mm, pq + 1)
                if pq >= 2:
                    dve.wait_ge(o5_mm, pq - 1)
                s = s5[pq % 2]
                dve.tensor_tensor(s[:, PAST:SEL], PS[:, 5, 0:SAMP], nbnew[:, pq, :], ALU.add)
                link(dve.tensor_tensor(s[:, SEL + WIN:SEL + WN], PS[:, 5, SAMP:2 * SAMP], nbnew[:, pq, :], ALU.add))
                dve.sem_inc(b5_rd, 1)
                dve.wait_ge(imp_mm, pq + 1)
                link(dve.tensor_copy(imp[:, :], PS[:, 5, 96:128]))
                dve.sem_inc(b5_rd, 1)
                v = imp[:, :]
                other = bass.AP(v.tensor, v.offset, [list(v.ap[0]), [0, NSB], [1, NSB]])
                own = ext(v, (0, NSB))
                link(dve.tensor_tensor(gt[:, :, :], other, own, ALU.is_gt))
                link(dve.tensor_tensor(eq[:, :, :], other, own, ALU.is_equal))
                link(dve.tensor_tensor(eq[:, :, :], eq[:, :, :], before[:, :, :], ALU.mult))
                link(dve.tensor_tensor(gt[:, :, :], gt[:, :, :], eq[:, :, :], ALU.add))
                link(dve.tensor_reduce(rank[:, :], gt[:, :, :], AX.X, ALU.add))
                link(dve.tensor_scalar(bmask[:, :], rank[:, :], 14.5, NEG, ALU.is_ge, ALU.mult))

            def pair_rows(pq):
                s = s5[pq % 2]
                m = bmask[:, :]
                sel = s[:, 0:PAST].rearrange("p (i a b) -> p i a b", i=NSEL, b=4)
                link(dve.tensor_tensor(sel, PS[:, 0:4, :].rearrange("p k (i a b) -> p (k i) a b", a=32, b=4),
                                       bass.AP(m.tensor, m.offset, [list(m.ap[0]), [0, NSEL], [1, NSB], [0, 4]]), ALU.add))
                n8 = s[:, 0:PAST].rearrange("p (i c) -> p i c", i=NSEL)[:, :, 120:128]
                link(dve.tensor_tensor(n8, n8, nb[:, :].rearrange("p (c i) -> p i c", i=NSEL), ALU.add))
                link(dve.tensor_copy(s[:, SEL:SEL + WIN], PS[:, 4, :]))
                n32 = s[:, SEL:SEL + WIN].rearrange("p (i c) -> p i c", i=NWIN)
                link(dve.tensor_tensor(n32[:, :, 96:128], n32[:, :, 96:128], nb[:, :].rearrange("p (c i) -> p i c", i=NWIN), ALU.add))
                dve.tensor_tensor(n32[:, :, 0], n32[:, :, 0], wedge[:, :], ALU.add).then_inc(s5_ev, 1)
                dve.wait_ge(s5_ev, pq + 1)
                dve.tensor_reduce(n5[:, 0:1], s[:, 0:SEL], AX.X, ALU.max, negate=True)
                dve.tensor_reduce(n5[:, 1:2], s[:, SEL:SEL + WN], AX.X, ALU.max, negate=True).then_inc(m5, 1)

            def scale_rows(pq):
                s = s5[pq % 2]
                dve.wait_ge(e5, pq + 1)
                link(dve.reciprocal(i5[:, 0:2], r5[:, 0:2]))
                link(dve.tensor_tensor(i5[:, 0:2], i5[:, 0:2], gr[:, pq, 1:3], ALU.mult))
                dve.tensor_scalar(s[:, 0:SEL], s[:, 0:SEL], i5[:, 0:1], None, ALU.mult)
                if pq:
                    dve.wait_ge(ev5, 16 * pq)
                dve.tensor_scalar(cmg[:, :], pn[:, :], gr[:, pq, 0:1], None, ALU.mult)
                dve.tensor_scalar(s[:, SEL:SEL + WN], s[:, SEL:SEL + WN], i5[:, 1:2], None, ALU.mult).then_inc(p5, 1)

            def gate_rows(pq):
                dve.wait_ge(ot_t, pq + 1)
                for g in range(NG):
                    half = slice(64 * g, 64 * g + 64)
                    for b2 in range(2):
                        b = 2 * pq + b2
                        c0_ = 256 + 64 * b2 + 32 * g
                        ins = dve.tensor_tensor(mix5[half, :, TS * b:TS * b + TS], PS[half, 5, c0_:c0_ + 32].rearrange("p (j t) -> p j t", t=TS),
                                                zas[half, :, TS * b:TS * b + TS], ALU.mult)
                ins.then_inc(mix5_rdy, 1)
                dve.wait_ge(mix5_rdy, pq + 1)
                dve.sem_inc(b5_rd, 1)

            choose(0)
            pair_rows(0)
            scale_rows(0)
            for pq in range(4):
                if pq < 3:
                    choose(pq + 1)
                    pair_rows(pq + 1)
                gate_rows(pq)
                if pq < 3:
                    scale_rows(pq + 1)
            dve.wait_ge(mix5_st, 16)
            dve.wait_ge(o5_mm, 4)

            def mix_low(tt):
                n = rows_of(tt)
                dve.wait_ge(m_hi, tt + 1)
                dve.tensor_tensor(ml[:, :, 0:n], mr[tt % 2][:, :, 0:n], f32(mh[:, :, 0:n]), ALU.subtract).then_inc(m_lo, 1)

            mix_low(0)
            for j in range(16):
                dve.wait_ge(wo_hi, j + 1)
                dve.tensor_tensor(wol[:, j, :], wor[j % 2][:, :], f32(woh[:, j, :]), ALU.subtract).then_inc(wo_lo, 1)
            dve.wait_ge(c6_ld, 32)
            for tt in range(NTT):
                n, b0 = rows_of(tt), 2 * (tt % 4)
                if tt + 1 < NTT:
                    mix_low(tt + 1)
                dve.wait_ge(y_mm, tt + 1)
                if tt:
                    dve.wait_ge(y_sq, tt)
                    dve.wait_ge(y_out, tt)
                out = PS[0:n, b0:b0 + 2, :].rearrange("p a b -> p (a b)")
                if tt == NTT - 1:
                    dve.wait_ge(c6_ld, 48)
                dve.tensor_tensor(yf[0:n, :], out, gbc[0:n, :], ALU.mult).then_inc(y_ev, 1)
                dve.wait_ge(y_ev, tt + 1)
                dve.wait_ge(xf_ld[tt % 2], 16 * (tt // 2 + 1))
                dve.tensor_tensor(yf[0:n, :], yf[0:n, :], xf[tt % 2][0:n, :], ALU.add).then_inc(y_sum, 1)
                dve.wait_ge(y_sq, tt + 1)
                dve.tensor_scalar(s6[0:n, 1:2], s6[0:n, 0:1], 1.0 / D, EPS, ALU.mult, ALU.add).then_inc(y_ms, 1)
                dve.wait_ge(y_rms, tt + 1)
                link(dve.reciprocal(s6[0:n, 3:4], s6[0:n, 2:3]))
                dve.scalar_tensor_tensor(yo[0:n, :], yf[0:n, :], s6[0:n, 3:4], fgb[0:n, :], ALU.mult, ALU.mult).then_inc(y_out, 1)


_INS = ['x_prompt', 'x_sample', 'cache_k_cmp', 'cache_v_cmp', 'cache_k_slc', 'cache_v_slc',
        'cache_k_win', 'cache_v_win', 'state_conv', 'page_table', 'c_prompt', 'c_sample', 'ada_w',
        'ada_b', 'norm_g', 'w_in', 'cmp_pe_k', 'cmp_w1_k', 'cmp_w2_k', 'cmp_pe_v', 'cmp_w1_v',
        'cmp_w2_v', 'conv_w', 'w_out', 'rel_bias', 'final_g']
_KV = (1, 1, 1024, 2, 64)
_OUTS = {
    'y_prompt': (1, 1024, 1024), 'y_sample': (8, 4, 1024),
    'p_kc': _KV, 'p_vc': _KV, 'p_ks': _KV, 'p_vs': _KV, 'p_kw': (1, 1, 512, 2, 64), 'p_vw': (1, 1, 512, 2, 64),
    'p_cv': (1, 1, 2, 1024),
    's_kc': (1, 8, 4, 2, 64), 's_vc': (1, 8, 4, 2, 64), 's_ks': (1, 8, 4, 2, 64), 's_vs': (1, 8, 4, 2, 64),
    's_kw': (1, 8, 512, 2, 64), 's_vw': (1, 8, 512, 2, 64), 's_cv': (1, 8, 2, 1024),
}


def constants():
    import math

    import numpy as np

    def bucket(n):
        n = np.asarray(n)
        m = np.maximum(n, 0)
        f = np.maximum(m, 16).astype(np.float32)
        large = 16 + (np.log(f / np.float32(16)) / np.float32(math.log(8.0)) * np.float32(16)).astype(np.int32)
        b = np.where(m < 16, m, np.minimum(large, 31))
        one = np.zeros((33, *n.shape), np.float32)
        np.put_along_axis(one, np.where(n < 0, 32, b)[None], 1.0, axis=0)
        return one

    i = np.arange(128)
    return {
        'k_ident': np.eye(128, dtype=np.float32),
        'k_stack2': np.concatenate([np.eye(64, dtype=np.float32)] * 2),
        'k_group': ((i[:, None] // 32 == i[None] // 32) & (i[:, None] % 4 == i[None] % 4)).astype(np.float32),
        'k_before': np.tril(np.ones((32, 32), np.float32), -1).reshape(1, 1024),
        'k_row': bucket(255 - np.arange(384)),
        'k_cmpd': bucket(64 * np.arange(-1, 3)[:, None] + i[None] - 63),
        'k_edge': np.where(i[None] >= i[:, None], 0.0, NEG).astype(np.float32),
        'k_wedge': np.where(np.arange(4)[None] >= i[:, None] % 4, 0.0, NEG).astype(np.float32),
        'k_any': (i[:, None] >= 63).astype(np.float32),
    }


def kernel(**inputs):
    import numpy as _np
    import concourse.bacc as _bacc
    from concourse import mybir as _mybir
    from concourse.bass_utils import run_bass_kernel_spmd as _run

    nc = _bacc.Bacc("TRN2", target_bir_lowering=False, num_devices=1)
    arrays, args = {}, {}
    for name, a in [*((n, inputs[n]) for n in _INS), *constants().items()]:
        a = _np.ascontiguousarray(a)
        arrays[f"in_{name}"] = a
        args[name] = nc.dram_tensor(f"in_{name}", a.shape, _mybir.dt.from_np(a.dtype), kind="ExternalInput").ap()
    for name, shape in _OUTS.items():
        args[name] = nc.dram_tensor(f"out_{name}", shape, F32, kind="ExternalOutput").ap()
    build(nc, **args)
    r = _run(nc, [arrays], core_ids=[0])
    return tuple(r.results[0][f"out_{name}"] for name in _OUTS)
```

```python
from contextlib import ExitStack

import concourse.bass as bass
from concourse import mybir

ALU = mybir.AluOpType
ACT = mybir.ActivationFunctionType
AX = mybir.AxisListType
F32 = mybir.dt.float32
F32R = mybir.dt.float32r
I32 = mybir.dt.int32

P = 128
D = 1024
S = 1024
NB, TS = 8, 4
SAMP = NB * TS
TOK = S + SAMP
KC = D // P
NTT = S // P + 1
CH = TOK // 3
PAST, PAGE, WIN, BLK = 2048, 128, 512, 64
NH, NG, HD = 16, 2, 64
HPG = NH // NG
DKV = NG * HD
NPT = 16
NPB = S // BLK
NSB = PAST // BLK
EPS = 1e-6
NEG = -1e30
O_KV = 1024
KV0, KV1 = 3 * DKV, 3 * DKV + 3 * NH
KVW = KV0 + KV1
O_H = O_KV + KVW
O_B, O_C, O_Z = O_H + D, O_H + 2 * D, O_H + 3 * D
C_KC, C_VC, C_KS, C_VS, C_KW, C_VW, C_G = (i * DKV for i in range(7))
CC, HC, BC, ZC, ZA, QQ = range(6)
NK = 6
XR, XW = 255, 384
CB = 2 * P + NPB + 1


ACT_A, ACT_B = {0, 1}, {0, 1}
TILE_ORDER = (0, 2, 4, 6, 7, 5, 3, 1)
NWE = 6


def build(nc: "bass.Bass", x_prompt, x_sample, cache_k_cmp, cache_v_cmp, cache_k_slc, cache_v_slc, cache_k_win,
          cache_v_win, state_conv, page_table, c_prompt, c_sample, ada_w, ada_b, norm_g, w_in,
          cmp_pe_k, cmp_w1_k, cmp_w2_k, cmp_pe_v, cmp_w1_v, cmp_w2_v, conv_w, w_out, rel_bias,
          final_g, k_ident, k_stack2, k_group, k_before, k_row, k_cmpd, k_edge, k_wedge, k_any,
          y_prompt, y_sample, p_kc, p_vc, p_ks, p_vs, p_kw, p_vw, p_cv,
          s_kc, s_vc, s_ks, s_vs, s_kw, s_vw, s_cv):
    ctx = ExitStack()

    def scope():
        return ctx.enter_context(ExitStack())

    def sb(name, shape, dt=F32, cx=None):
        return (cx or ctx).enter_context(nc.sbuf_tensor(name, shape, dt))

    def sem(name):
        return ctx.enter_context(nc.semaphore(name))

    def ext(ap, *dims):
        return bass.AP(ap.tensor, ap.offset, [*[list(x) for x in ap.ap], *[list(x) for x in dims]])

    def flat(ap, off, dims):
        return bass.AP(ap.tensor, off, [list(x) for x in dims])

    def f32(ap):
        return ap.bitcast(F32)

    with ctx:
        PS = ctx.enter_context(nc.psum_tensor("PS", [P, 8, 512], F32))
        qst = nc.dram_tensor("q_stacked", [NH, P, S], F32R, kind="Internal").ap()
        zad = nc.dram_tensor("z_attn_silu", [8, P, TOK], F32, kind="Internal").ap()
        mixd = nc.dram_tensor("mixed", [16, P, TOK], F32, kind="Internal").ap()
        rowd = nc.dram_tensor("bias_rows", [NH, P, XW], F32, kind="Internal").ap()
        gbd = nc.dram_tensor("gate_rows", [9, D], F32, kind="Internal").ap()
        gated = nc.dram_tensor("gates_sample", [SAMP, 3 * NH], F32, kind="Internal").ap()

        ident = sb("ident", [P, P])
        gate = sb("gate", [9, D])
        qs = sb("qs", [P, 8, SAMP])
        vcol = sb("vcol", [P, 8, 29])
        tcmp = sb("tcmp", [P, 4, NH])

        idxc = sb("idxc", [P, 2], I32)
        idxq = sb("idxq", [P, 2, 4], I32)
        idxs = sb("idxs", [P, NB], I32)
        pidx = sb("pidx", [P, 2], I32)
        pgc = sb("pgc", [P, 2], I32)
        pgs = sb("pgs", [P, NB], I32)
        sg = sb("sg", [P, NTT, 3 * NH])
        kcs = sb("kcs", [P, NB * NSB])
        vcs = sb("vcs", [NSB, NB, DKV])
        kcp = sb("kcp", [P, NG, 2 * NPB], F32R)
        vcp = sb("vcp", [P, NG, P], F32R)
        pebias = sb("pebias", [P, 2])

        kvs = sb("kvs", [P, KVW])
        cN = ExitStack()
        nearl = sb("nearl", [P, NH, 2 * P], F32R, cN)
        cN.close()
        cV = ExitStack()
        kvt = sb("kvt", [P, NTT - 1, KVW], cx=cV)
        krow = kvt[0:33, 7, 0:XW]
        kcmpd = kvs[0:33, 0:4 * P].rearrange("p (m q) -> p m q", m=4)

        cA = ExitStack()
        hhi = sb("hhi", [P, KC, TOK], F32R, cA)
        hlo = sb("hlo", [P, KC, TOK], F32R, cA)
        c0 = ExitStack()
        vrow = sb("vrow", [29, D], cx=c0)
        relx = sb("relx", [33, NH], cx=c0)
        rel31 = sb("rel31", [32, NH], cx=c0)
        rows = sb("rows", [NH, XW], cx=c0)
        wkr = [sb(f"wkr{i}", [P, KC, w], cx=c0) for i, w in enumerate((KV0, KV1))]
        xb = [sb(f"xb{i}", [P, D], cx=c0) for i in range(2)]
        h32 = sb("h32", [P, KC, P], cx=c0)
        scA = sb("scA", [P, KC, 9], cx=c0)
        scB = sb("scB", [P, KC, 9], cx=c0)
        ssq = sb("ssq", [P, NTT], cx=c0)
        ms = sb("ms", [P, NTT], cx=c0)
        rms = sb("rms", [P, NTT], cx=c0)
        rstd = sb("rstd", [P, NTT], cx=c0)
        cS = ExitStack()
        adaw = [sb(f"adaw{i}", [P, KC, 512], cx=cS) for i in range(2)]
        adar = sb("adar", [9, 2 * D], cx=cS)
        adab = sb("adab", [9, 3 * D], cx=cS)
        cS.close()
        wkh = [sb(f"wkh{i}", [P, KC, w], F32R, c0) for i, w in enumerate((KV0, KV1))]
        wkl = [sb(f"wkl{i}", [P, KC, w], F32R, c0) for i, w in enumerate((KV0, KV1))]
        c0.close()
        c2 = ExitStack()
        wr = [sb(f"wr{i}", [P, KC, P], cx=c2) for i in range(2)]
        wh = [sb(f"wh{i}", [P, KC, P], F32R, c2) for i in range(2)]
        wl = [sb(f"wl{i}", [P, KC, P], F32R, c2) for i in range(2)]
        cct = sb("cct", [P, TOK], cx=c2)
        uu = sb("uu", [P, 2 + TOK], cx=c2)
        us = sb("us", [P, NB, 6], cx=c2)
        yy = sb("yy", [P, TOK], cx=c2)
        zt = sb("zt", [P, TOK], cx=c2)
        ych = sb("ych", [P, TOK], cx=c2)
        zab = sb("zab", [P, TOK], cx=c2)
        qhi = sb("qhi", [P, TOK], F32R, c2)
        qlo = sb("qlo", [P, TOK], F32R, c2)
        tail = sb("tail", [P, 18], cx=c2)
        tailr = sb("tailr", [18, D], cx=c2)
        c2.close()
        cA.close()
        c3 = ExitStack()
        QT = BLK // 4 * DKV
        w1 = [sb(f"w1{i}", [P, 32, P], cx=c3) for i in range(2)]
        w2 = [sb(f"w2{i}", [P, P], cx=c3) for i in range(2)]
        xpq = [sb(f"xpq{i}", [NPB + 1, QT], cx=c3) for i in range(4)]
        xt = [sb(f"xt{i}", [P, NG, CB], cx=c3) for i in range(2)]
        hs3 = sb("hs3", [P, NG, CB], cx=c3)
        xq = [None] + [sb(f"xq{i}", [P, 2, QT], cx=c3) for i in (1, 2, 3)]
        c3.close()
        c4 = ExitStack()
        ksh, ksl, kwh, kwl = (sb(n, [P, NG, S], F32R, c4) for n in ("ksh", "ksl", "kwh", "kwl"))
        vsx, vwx = (sb(n, [P, 8, NG, P], F32R, c4) for n in ("vsx", "vwx"))
        near = sb("near", [P, NH, 2 * P], F32R, c4)
        edge = sb("edge", [P, P], cx=c4)
        edger = sb("edger", [P, P], F32R, c4)
        identr = sb("identr", [P, P], F32R, c4)
        stack2 = sb("stack2", [P, 64], cx=c4)
        anyc = sb("anyc", [P, 1], cx=c4)
        pr = [sb(f"pr{i}", [P, 4, S], cx=c4) for i in range(2)]
        prc = [sb(f"prc{i}", [P, 4, P], cx=c4) for i in range(3)]
        cs = sb("cs", [P, 4, NPB], cx=c4)
        nm = sb("nm", [P, 3, 8], cx=c4)
        rsum = sb("rsum", [P, 3, 8], cx=c4)
        rrec = sb("rrec", [P, 3, 8], cx=c4)
        rg = sb("rg", [P, 3, 8], cx=c4)
        qb = [sb(f"qb{i}", [P, 4, P], F32R, c4) for i in range(4)]
        pth = [sb(f"pth{i}", [P, 512], F32R, c4) for i in range(2)]
        ptl = [sb(f"ptl{i}", [P, 512], F32R, c4) for i in range(2)]
        osb = sb("osb", [P, 512], cx=c4)
        zau = [sb(f"zau{i}", [P, 4, P], cx=c4) for i in range(2)]
        mixs = [sb(f"mixs{i}", [P, 4, P], cx=c4) for i in range(2)]
        pr.append(sb("pr2", [P, 4, S], cx=c4))
        nearr = pr[2][:, :, :].rearrange("p a (b c) -> p (a b) c", c=2 * P)
        xq[0] = pr[2][:, :, :].rearrange("p (a b) c -> p a (b c)", a=2)
        NSEL, NWIN = PAST // P, WIN // P
        grp = sb("grp", [P, P], cx=c4)
        before = sb("before", [P, NSB, NSB], cx=c4)
        wedge = sb("wedge", [P, TS], cx=c4)
        nb = sb("nb", [P, P], cx=c4)
        nbnew = sb("nbnew", [P, 4, SAMP], cx=c4)
        nbc = sb("nbc", [P, 2], cx=c4)
        gr = sb("gr", [P, 4, 3], cx=c4)
        zas = sb("zas", [P, 8, SAMP], cx=c4)
        qbd = sb("qbd", [P, NB, 64], cx=c4)
        kb0 = sb("kb0", [P, NSEL, DKV], cx=c4)
        c4.close()
        cV.close()
        mix5 = sb("mix5", [P, 8, SAMP])
        wor = [sb(f"wor{i}", [P, D]) for i in range(2)]
        woh = [sb(f"woh{j}", [P, D], F32R) for j in range(NWE)]
        wol = [sb(f"wol{j}", [P, D], F32R) for j in range(NWE)]
        c5 = ExitStack()
        kb = [kb0, sb("kb1", [P, NSEL, DKV], cx=c5)]
        kwb = [sb(f"kwb{i}", [P, NWIN, DKV], cx=c5) for i in range(2)]
        gt = sb("gt", [P, NSB, NSB], cx=c5)
        kt5 = [sb(f"kt5{i}", [P, NSEL + NWIN, P], cx=c5) for i in range(2)]
        vb = [sb(f"vb{i}", [P, NSEL, DKV], cx=c5) for i in range(4)]
        vwb = [sb(f"vwb{i}", [P, NWIN, DKV], cx=c5) for i in range(4)]
        knt = sb("knt", [P, 2, SAMP], cx=c5)
        SEL, WN = PAST + SAMP, WIN + SAMP
        s5 = [sb(f"s5{i}", [P, SEL + WN], cx=c5) for i in range(2)]
        cm = sb("cm", [P, NSB], cx=c5)
        pn = sb("pn", [P, NSB], cx=c5)
        cmg = sb("cmg", [P, NSB], cx=c5)
        imp = sb("imp", [P, NSB], cx=c5)
        eq = sb("eq", [P, NSB, NSB], cx=c5)
        rank = sb("rank", [P, NSB], cx=c5)
        bmask = sb("bmask", [P, NSB], cx=c5)
        n5 = sb("n5", [P, 4], cx=c5)
        r5 = sb("r5", [P, 4], cx=c5)
        i5 = sb("i5", [P, 4], cx=c5)
        pt5 = sb("pt5", [P, NSEL + NWIN + 3, P], cx=c5)
        o5 = sb("o5", [P, P], cx=c5)
        c5.close()
        c6 = ExitStack()
        for j in range(NWE, 16):
            if j == 8:
                mr = sb("mr", [P, 16, P], cx=c6)
                gbc = sb("gbc", [P, D], cx=c6)
                fgb = sb("fgb", [P, D], cx=c6)
                xf = [sb(f"xf{i}", [P, D], cx=c6) for i in range(2)]
            woh.append(sb(f"woh{j}", [P, D], F32R, c6))
            wol.append(sb(f"wol{j}", [P, D], F32R, c6))
        mh = sb("mh", [P, 16, P], F32R, c6)
        ml = sb("ml", [P, 16, P], F32R, c6)
        yf = sb("yf", [P, D], cx=c6)
        yo = sb("yo", [P, D], cx=c6)
        s6 = sb("s6", [P, 4], cx=c6)
        c6.close()

        const_ld, c_ld, row_st, rel_ld = sem("const_ld"), sem("c_ld"), sem("row_st"), sem("rel_ld")
        adaw_ld = [sem(f"adaw_ld{i}") for i in range(2)]
        ct_pe, ct_dve, ada_mm, ada_ev, ada_t, ada_col = (sem(n) for n in
            ("ct_pe", "ct_dve", "ada_mm", "ada_ev", "ada_t", "ada_col"))
        x_ld = [sem(f"x_ld{i}") for i in range(2)]
        x_ms, x_act, x_n, x_t, h_ev, h_hi, h_lo = (sem(n) for n in ("x_ms", "x_act", "x_n", "x_t", "h_ev", "h_hi", "h_lo"))
        wk_ld, wk_hi, wk_lo, kv_mm, kv_ev = (sem(n) for n in ("wk_ld", "wk_hi", "wk_lo", "kv_mm", "kv_ev"))
        dch, pch = sem("dch"), sem("pch")
        wr_ld = [sem(f"wr_ld{i}") for i in range(2)]
        w_hi, w_lo, p2_mm = sem("w_hi"), sem("w_lo"), sem("p2_mm")
        p2_ev = [sem(f"p2_ev{i}") for i in range(2)]
        q_hi, y_rdy, tail_rdy, tail_t, tail_ev = (sem(n) for n in
            ("q_hi", "y_rdy", "tail_rdy", "tail_t", "tail_ev"))
        ych_st, zab_st, q_st = sem("ych_st"), sem("zab_st"), sem("q_st")
        tb_mm, tb_ev, tb_rel = sem("tb_mm"), sem("tb_ev"), sem("tb_rel")
        out_st, tail_st = sem("out_st"), sem("tail_st")
        nout = [0]
        idx_ld, idx_a, idx_b, kc_st = sem("idx_ld"), sem("idx_a"), sem("idx_b"), sem("kc_st")
        xq_ld = [sem(f"xq_ld{i}") for i in range(4)]
        xp_ld = [sem(f"xp_ld{i}") for i in range(4)]
        w2_ld, x3_t, x3_mm, pe_rdy, hs_rdy, c3_mm, c3_hi, c3_ev = (sem(n) for n in
            ("w2_ld", "x3_t", "x3_mm", "pe_rdy", "hs_rdy", "c3_mm", "c3_hi", "c3_ev"))
        xe = [sem(f"xe{i}") for i in range(2)]
        c4_ld, kt_t, kt_hi, kt_lo, vb_hi, vb_lo, sg_rdy, pad0 = (sem(n) for n in
            ("c4_ld", "kt_t", "kt_hi", "kt_lo", "vb_hi", "vb_lo", "sg_rdy", "pad0"))
        s_mm, m_rdy, mc_rdy, e_done, ec_done, r_rdy, n_act, n_dve, t_mm, pt_hi, pt_lo, pv_mm, o_ev, r_mm, r_ev = (sem(n) for n in
            ("s_mm", "m_rdy", "mc_rdy", "e_done", "ec_done", "r_rdy", "n_act", "n_dve", "t_mm", "pt_hi", "pt_lo", "pv_mm", "o_ev", "r_mm", "r_ev"))
        q_ld = [sem(f"q_ld{i}") for i in range(4)]
        za_ld = [sem(f"za_ld{i}") for i in range(2)]
        mix_st = [sem(f"mix_st{i}") for i in range(2)]

        c5_ld, g_st, gr_ld = sem("c5_ld"), sem("g_st"), sem("gr_ld")
        kg_ld = [sem(f"kg_ld{i}") for i in range(2)]
        vg_ld = [sem(f"vg_ld{i}") for i in range(4)]
        kw_ld = [sem(f"kw_ld{i}") for i in range(2)]
        vw_ld = [sem(f"vw_ld{i}") for i in range(4)]
        q5_rdy, nbn_rdy, t5, ev5, ev5d, s5c_mm, m5c, e5c, pn_rdy, imp_mm, s5_mm, s5_ev, m5, e5, p5, b5_rd, o5_mm, o5_cp, ot_t, mix5_rdy, mix5_st, kn_t, kn_ev = (
            sem(n) for n in ("q5_rdy nbn_rdy t5 ev5 ev5d s5c_mm m5c e5c pn_rdy imp_mm s5_mm s5_ev m5 e5 p5 b5_rd o5_mm o5_cp ot_t mix5_rdy mix5_st kn_t kn_ev".split()))
        wo_ld = [sem(f"wo_ld{i}") for i in range(2)]
        mr_ld = [sem(f"mr_ld{i}") for i in range(2)]
        xf_ld = [sem(f"xf_ld{i}") for i in range(2)]
        c6_ld, wo_hi, wo_lo, m_hi, m_lo, y_mm, y_ev, y_sum, y_act, y_ms, y_out, y_st = (
            sem(n) for n in "c6_ld wo_hi wo_lo m_hi m_lo y_mm y_ev y_sum y_act y_ms y_out y_st".split())

        def early(pq):
            return range(2 * pq, 2 * pq + 2)

        NU = 32
        NI = 2 * NU

        def unit(u):
            return u // 16, u // 8 % 2, TILE_ORDER[u % 8]

        def tiles_of(w):
            i = unit(w // 2)[2]
            return i + 1 if w % 2 == 0 else min(i + 1, 5) + 1

        def keys_of(w):
            k = (tiles_of(w) - w % 2) * P
            return k, ([k] if k <= 512 else [k // 2, k // 2])

        ON_ACT = {0: ACT_A, 1: ACT_B}

        tile0 = [0]
        for w in range(NI):
            tile0.append(tile0[-1] + tiles_of(w))

        def slots(w):
            n = tiles_of(w)
            cuts = [(n * q + 2) // 4 for q in range(5)]
            return [range(cuts[q], cuts[q + 1]) for q in range(4)]

        keys_by_dve = [False] * 5 + [True, False] * 2 + [True]
        by_dve = keys_by_dve * 2 + ([False] * 6 + keys_by_dve) * 2 + [False] * 12

        def keys_turned(b, win):
            return 10 * (b // 2) + 6 * max(0, b // 2 - 1) + 5 * (b % 2) + (5 if win else 4)

        def copied(n):
            return (ev5d if by_dve[n] else ev5), sum(x == by_dve[n] for x in by_dve[:n + 1])

        class Chain:
            def __init__(self, eng, s):
                self.eng, self.s, self.n = eng, s, 0

            def link(self, ins):
                self.n += 1
                ins.then_inc(self.s, 1)
                self.eng.wait_ge(self.s, self.n)

        w3 = w_in.rearrange("l (k p) c -> p (l k) c", p=P)
        ada3 = ada_w.rearrange("l (k p) c -> p (l k) c", p=P)
        xp = x_prompt.rearrange("b (t p) c -> p (b t) c", p=P)
        xs = x_sample.rearrange("b t c -> (b t) c")

        def wcol(j, kind):
            if kind == QQ:
                return [(64 * j, 64), (512 + 64 * j, 64)]
            if kind == ZA:
                return [(O_Z + 64 * j, 64), (O_Z + 512 + 64 * j, 64)]
            return [({CC: O_C, HC: O_H, BC: O_B, ZC: O_Z + D}[kind] + P * j, P)]

        def rows_of(tt):
            return P if tt < NTT - 1 else SAMP

        KVB = [0, 7, 1, 2]

        block = ctx.enter_context(nc.Block())

        @block.sync
        def _(sp):
            sp.dma_start(vrow[0:1, :], c_prompt).then_inc(c_ld, 16)
            sp.dma_start(vrow[1:9, :], c_sample).then_inc(c_ld, 16)
            sp.dma_start(ident[:, :], k_ident).then_inc(const_ld, 16)
            sp.dma_start(vrow[9:10, :], norm_g).then_inc(const_ld, 16)
            sp.dma_start(vrow[10:13, :], conv_w.rearrange("l r c -> (l r) c")).then_inc(const_ld, 16)
            sp.dma_start(vrow[13:29, :], state_conv.rearrange("l b r c -> (l b r) c")).then_inc(const_ld, 16)
            sp.dma_start(adab[:, :], flat(ada_b, 0, [(0, 9), (1, 3 * D)])).then_inc(c_ld, 16)
            for ch in range(6):
                if ch >= 2:
                    sp.wait_ge(ada_mm, ch - 1)
                sp.dma_start(adaw[ch % 2][:, :, :], ada3[:, :, 512 * ch:512 * ch + 512]).then_inc(adaw_ld[ch % 2], 16)
                if ch == 1:
                    sp.dma_start(wkr[0][:, :, :], w3[:, :, O_KV:O_KV + KV0]).then_inc(wk_ld, 16)
            sp.dma_start(wkr[1][:, :, :], w3[:, :, O_KV + KV0:O_H]).then_inc(wk_ld, 16)
            sp.wait_ge(h_lo, NTT)
            sp.wait_ge(h_hi, NTT)
            sp.wait_ge(kv_mm, 2 * NTT)
            sp.wait_ge(row_st, 16)
            sp.wait_ge(tb_ev, 2)

            def load_w(j, kind, first):
                n = NK * j + kind
                if not first:
                    sp.wait_ge(w_lo, n - 1)
                for at, (c0_, w) in zip((0, 64), wcol(j, kind)):
                    sp.dma_start(wr[kind % 2][:, :, at:at + w], w3[:, :, c0_:c0_ + w]).then_inc(wr_ld[kind % 2], 16 if kind in (QQ, ZA) else 16)

            for j in range(8):
                for kind in range(NK):
                    load_w(j, kind, j == 0 and kind < 2)
            sp.wait_ge(p2_mm, 8 * NK)
            sp.wait_ge(kc_st, 32)
            for c, (pe_, w1_, rows_) in enumerate(((cmp_pe_k, cmp_w1_k, p_kc), (cmp_pe_v, cmp_w1_v, p_vc))):
                for q in range(4):
                    n, toks = 4 * c + q, slice(16 * q, 16 * q + 16)
                    if n >= 4:
                        sp.wait_ge(x3_t, 16 * (n - 3))
                    sp.dma_start(w1[c][:, 8 * q:8 * q + 8, :], w1_.rearrange("l (t p) c -> p (l t) c", p=P)[:, 8 * q:8 * q + 8, :]).then_inc(xp_ld[q], 16)
                    sp.dma_start(xpq[q][0:NPB, :], rows_.rearrange("l b (n t) g d -> (l b n) t (g d)", t=BLK)[:, toks, :]).then_inc(xp_ld[q], 16)
                    for g in range(NG):
                        sp.dma_start(xpq[q][NPB:NPB + 1, :].rearrange("p (t c) -> p t c", c=DKV)[:, :, 64 * g:64 * g + 64], pe_[:, toks, :]).then_inc(xp_ld[q], 16)
                if c == 0:
                    for a in range(2):
                        for t, src in zip(w2, (cmp_w2_k, cmp_w2_v)):
                            sp.dma_start(t[:, 64 * a:64 * a + 64], src.rearrange("l p c -> (l p) c")).then_inc(w2_ld, 16)
            sp.wait_ge(x3_t, 80)
            sp.dma_start(nearr, flat(rowd, P - 1, [(XW - 1, P), (P * XW, NH), (1, 2 * P)])).then_inc(c4_ld, 16)
            sp.wait_ge(c3_mm, 2)
            sp.dma_start(edge[:, :], k_edge).then_inc(c4_ld, 16)
            sp.dma_start(stack2[:, :], k_stack2).then_inc(c4_ld, 16)
            sp.dma_start(anyc[:, :], k_any).then_inc(c4_ld, 16)

            def load_q(u):
                g, hs, i = unit(u)
                if u >= 4:
                    sp.wait_ge(s_mm, 8 * (u - 3))
                h0 = HPG * g + 4 * hs
                sp.dma_start(f32(qb[u % 4][:, :, :]), f32(qst[h0:h0 + 4, :, i * P:(i + 1) * P]).rearrange("h p c -> p h c")).then_inc(q_ld[u % 4], 16)

            def load_za(u):
                g, hs, i = unit(u)
                half = slice(64 * g, 64 * g + 64)
                if u >= 2:
                    sp.wait_ge(r_ev, u - 1)
                sp.dma_start(zau[u % 2][half, :, :], zad[4 * hs:4 * hs + 4, half, i * P:(i + 1) * P].rearrange("j p c -> p j c")).then_inc(za_ld[u % 2], 16)

            def load_tables():
                sp.wait_ge(g_st, 32)
                sp.dma_start(grp[:, :], k_group).then_inc(c5_ld, 16)
                sp.dma_start(before[:, :, :], flat(k_before, 0, [(0, P), (1, NSB * NSB)])).then_inc(c5_ld, 16)
                sp.dma_start(wedge[:, :], k_wedge).then_inc(c5_ld, 16)
                sp.dma_start(zas[:, :, :], zad[:, :, S:TOK].rearrange("j p c -> p j c")).then_inc(c5_ld, 16)
                for b2 in range(2):
                    half = slice(64 * b2, 64 * b2 + 64)
                    sp.dma_start(nb[half, :], flat(rowd, P - 1, [(P * XW, NH), (XW - 1, TS), (1, P)])).then_inc(c5_ld, 16)
                    for a in range(2):
                        sp.dma_start(nbc[half, a:a + 1], flat(rowd, XR - 65 + 64 * a, [(P * XW, NH), (XW - 1, TS), (1, 1)]), allow_slow_non_contiguous=True).then_inc(c5_ld, 16)
                for b in range(NB):
                    half = slice(64 * (b % 2), 64 * (b % 2) + 64)
                    for a in range(3):
                        sp.dma_start(gr[half, b // 2, a:a + 1], flat(gated, TS * b * 3 * NH + NH * a, [(1, NH), (3 * NH, TS), (1, 1)]), allow_slow_non_contiguous=True).then_inc(gr_ld, 16)
                sp.wait_ge(nbn_rdy, 1)
                for b in range(NB):
                    half = slice(64 * (b % 2), 64 * (b % 2) + 64)
                    sp.dma_start(nbnew[half, b // 2, TS * b:TS * b + TS], flat(rowd, XR, [(P * XW, NH), (XW - 1, TS), (1, TS)])).then_inc(gr_ld, 16)

            for u in range(3):
                load_q(u)
            load_za(0)
            for u in range(NU):
                g, hs, i = unit(u)
                half = slice(64 * g, 64 * g + 64)
                if u + 3 < NU:
                    load_q(u + 3)
                if u + 1 < NU:
                    load_za(u + 1)
                if u == 4:
                    load_tables()
                sp.wait_ge(r_ev, u + 1)
                sp.dma_start(mixd[4 * hs:4 * hs + 4, half, i * P:(i + 1) * P].rearrange("j p c -> p j c"), mixs[u % 2][half, :, :]).then_inc(mix_st[u % 2], 16)
            sp.wait_ge(mix_st[0], 16 * NU // 2)
            sp.wait_ge(mix_st[1], 16 * NU // 2)
            sp.wait_ge(r_ev, NU)
            sp.wait_ge(pv_mm, tile0[NI])
            wo = w_out.rearrange("l r c -> (l r) c")

            def load_wo(j):
                if j >= 2:
                    sp.wait_ge(wo_lo, j - 1)
                if j < 8:
                    sp.dma_start(wor[j % 2][0:64, :], wo[64 * j:64 * j + 64, :]).then_inc(wo_ld[j % 2], 16)
                    sp.dma_start(wor[j % 2][64:128, :], wo[512 + 64 * j:576 + 64 * j, :]).then_inc(wo_ld[j % 2], 16)
                else:
                    sp.dma_start(wor[j % 2][:, :], wo[P * j:P * j + P, :]).then_inc(wo_ld[j % 2], 16)

            for b in range(NB):
                if b >= 2:
                    sp.wait_ge(t5, keys_turned(b - 2, True))
                sp.dma_start(kwb[b % 2][:, :, :], cache_k_win[0, b].rearrange("(p i) g d -> p (i g d)", i=NWIN)).then_inc(kw_ld[b % 2], 16)
                if b >= 4:
                    sp.wait_ge(o5_mm, b // 2 - 1)
                sp.dma_start(vwb[b % 4][:, :, :], cache_v_win[0, b].rearrange("(p i) g d -> p (i g d)", i=NWIN)).then_inc(vw_ld[b % 4], 16)
                for j in early(b // 2) if b % 2 else ():
                    load_wo(j)
            sp.wait_ge(s5_mm, 4)
            sp.dma_start(gbc[:, :], flat(gbd, 0, [(0, P), (1, D)])).then_inc(c6_ld, 16)
            sp.dma_start(fgb[:, :], flat(final_g, 0, [(0, P), (1, D)])).then_inc(c6_ld, 16)
            def load_mix(tt):
                n = rows_of(tt)
                for a in range(2):
                    if tt:
                        sp.wait_ge(m_lo, 2 * tt - 1 + a)
                    ks = slice(8 * a, 8 * a + 8)
                    sp.dma_start(mr[:, ks, 0:n], mixd[ks, :, tt * P:tt * P + n].rearrange("j p c -> p j c")).then_inc(mr_ld[a], 16)
                if tt >= 2:
                    sp.wait_ge(y_sum, tt - 1)
                sp.dma_start(xf[tt % 2][0:n, :], xp[:, tt, :] if tt < NTT - 1 else xs).then_inc(xf_ld[tt % 2], 16)

            load_mix(0)
            for j in (8, 9):
                load_wo(j)
            sp.wait_ge(mix5_rdy, 4)
            sp.dma_start(mixd[0:8, :, S:TOK].rearrange("j p c -> p j c"), mix5[:, :, :]).then_inc(mix5_st, 16)
            for j in range(10, 16):
                load_wo(j)
            sp.wait_ge(mix5_st, 16)
            for tt in range(1, NTT):
                load_mix(tt)
            sp.wait_ge(y_ev, NTT - 1)
            sp.dma_start(gbc[0:SAMP, :], flat(gbd, D, [(D, NB), (0, TS), (1, D)])).then_inc(c6_ld, 16)

        def wr_count(j, kind):
            return 16 * (4 * j + (1, 1, 2, 2, 4, 4)[kind])

        @block.gpsimd
        def _(po):
            chain = Chain(po, pch)
            chain.link(po.memset(relx[32:33, :], NEG))
            po.dma_start(relx[0:32, :], rel_bias).then_inc(rel_ld, 16)
            po.dma_start(rel31[:, :], flat(rel_bias, 31 * NH, [(0, 32), (1, NH)])).then_inc(rel_ld, 16)
            po.dma_start(krow, k_row).then_inc(rel_ld, 16)
            po.dma_start(kcmpd, k_cmpd).then_inc(rel_ld, 16)
            for tt in range(NTT):
                if tt == 2:
                    for T in range(2):
                        po.dma_start(pgc[:, T:T + 1], flat(page_table, 64 * T, [(1, 64), (0, 2), (1, 1)])).then_inc(idx_ld, 16)
                    for b in range(NB):
                        po.dma_start(pgs[:, b:b + 1], flat(page_table, NPT * b, [(1, NPT), (0, 8), (1, 1)])).then_inc(idx_ld, 16)
                    po.iota(pidx[:, :], [[0, 2]], base=0, channel_multiplier=1).then_inc(idx_a, 1)
                if tt >= 2:
                    po.wait_ge(x_t, tt - 1)
                src = xp[:, tt, :] if tt < NTT - 1 else xs
                po.dma_start(xb[tt % 2][0:rows_of(tt), :], src).then_inc(x_ld[tt % 2], 16)
            po.wait_ge(tb_ev, 1)
            rv = rows[:, :]
            po.dma_start(rowd, bass.AP(rv.tensor, rv.offset, [list(rv.ap[0]), [0, P], [1, XW]])).then_inc(row_st, 16)
            po.wait_ge(kv_ev, 2 * NTT)
            for which, (dst, col, t0) in enumerate(((p_kc, C_KC, 0), (p_vc, C_VC, 0), (p_ks, C_KS, 0), (p_vs, C_VS, 0),
                                 (p_kw, C_KW, 4), (p_vw, C_VW, 4))):
                po.dma_start(dst.rearrange("l b (t p) g d -> p (l b t) (g d)", p=P), kvt[:, t0:8, col:col + DKV]).then_inc(kc_st if which < 2 else out_st, 16)
                nout[0] += 0 if which < 2 else 16
            for dst, col in ((s_kc, C_KC), (s_vc, C_VC), (s_ks, C_KS), (s_vs, C_VS)):
                po.dma_start(dst.rearrange("l b t g d -> (l b t) (g d)"), kvs[0:SAMP, col:col + DKV]).then_inc(out_st, 16)
                nout[0] += 16
            for dst, buf, col in ((s_kw, cache_k_win, C_KW), (s_vw, cache_v_win, C_VW)):
                po.dma_start(dst[0, :, 0:WIN - TS, :, :].rearrange("b t g d -> b (t g d)"),
                             buf[0, :, TS:WIN, :, :].rearrange("b t g d -> b (t g d)")).then_inc(out_st, 16)
                for b in range(NB):
                    po.dma_start(dst[0, b, WIN - TS:WIN, :, :].rearrange("t g d -> t (g d)"),
                                 kvs[TS * b:TS * b + TS, col:col + DKV]).then_inc(out_st, 16)
                nout[0] += 16 * 9
            def gather_quarter(c, q):
                cache = (cache_k_cmp, cache_v_cmp)[c]
                src = cache.rearrange("l n (e t) g d -> (l n e) (t g d)", e=8)
                for T in range(2):
                    po.indirect_dma_start(xq[q][:, T, :], None, src, bass.IndirectOffsetOnAxis(idxq[:, T, q:q + 1], 0)).then_inc(xq_ld[q], 16)

            po.wait_ge(idx_b, 3)
            po.wait_ge(kv_mm, 2 * NTT)
            po.wait_ge(h_lo, NTT)
            gather_quarter(0, 0)
            for j in range(8):
                po.wait_ge(y_rdy, j + 1)
                po.dma_start(mixd[8 + j], ych[:, :]).then_inc(ych_st, 16)
                po.wait_ge(p2_ev[0], 3 * j + 3)
                po.dma_start(zad[j], zab[:, :]).then_inc(zab_st, 16)
                po.wait_ge(p2_ev[1], 3 * j + 3)
                for g in range(2):
                    half = slice(64 * g, 64 * g + 64)
                    po.dma_start(f32(qst[8 * g + j, 0:64, :]), f32(qhi[half, 0:S])).then_inc(q_st, 16)
                    po.dma_start(f32(qst[8 * g + j, 64:128, :]), f32(qlo[half, 0:S])).then_inc(q_st, 16)
            po.wait_ge(tail_ev, 8)
            po.dma_start(p_cv.rearrange("l b r c -> (l b r) c"), tailr[0:2, :]).then_inc(tail_st, 16)
            po.dma_start(s_cv.rearrange("l b r c -> (l b r) c"), tailr[2:18, :]).then_inc(tail_st, 16)
            po.wait_ge(p2_mm, 8 * NK)
            po.wait_ge(w_lo, 8 * NK)
            gather_quarter(0, 1)
            po.wait_ge(out_st, nout[0])
            po.wait_ge(ych_st, 16 * 8)
            po.wait_ge(zab_st, 16 * 8)
            po.wait_ge(q_st, 16 * 32)
            po.wait_ge(row_st, 16)
            po.wait_ge(tail_st, 32)
            for e in (0, 1):
                po.wait_ge(p2_ev[e], 24)
            for c in range(2):
                for q in range(4):
                    if 4 * c + q >= 4:
                        po.wait_ge(x3_t, 16 * (4 * c + q - 3))
                    if 4 * c + q >= 2:
                        gather_quarter(c, q)
            for q in range(4):
                po.wait_ge(xq_ld[q], 2 * 32)
            po.memset(f32(vcp[:, :, :]), 0.0).then_inc(pad0, 1)
            po.wait_ge(c3_mm, 2)
            for r in range(3):
                ins = po.memset(prc[r][:, :, :], 0.0)
            ins.then_inc(pad0, 1)
            po.wait_ge(sg_rdy, 2)
            po.dma_start(gated, sg[0:SAMP, 8, :]).then_inc(g_st, 16)
            po.dma_start(gbd, gate[:, :]).then_inc(g_st, 16)
            po.wait_ge(g_st, 32)
            po.memset(nbnew[:, :, :], NEG).then_inc(nbn_rdy, 1)
            ksrc = cache_k_slc.rearrange("l n (e t) g d -> (l n e) (t g d)", e=8)
            vsrc = cache_v_slc.rearrange("l n (e t) g d -> (l n e) (t g d)", e=8)
            flat2 = lambda t: t[:, :, :].rearrange("p i c -> p (i c)")
            for b in range(NB):
                if b == 1:
                    po.wait_ge(r_ev, NU)
                    po.wait_ge(pv_mm, tile0[NI])
                if b >= 2:
                    po.wait_ge(t5, keys_turned(b - 2, False))
                po.indirect_dma_start(flat2(kb[b % 2]), None, ksrc, bass.IndirectOffsetOnAxis(idxs[:, b:b + 1], 0)).then_inc(kg_ld[b % 2], 16)
                for bv in (b - 1, b) if b % 2 else ():
                    if bv >= 4:
                        po.wait_ge(o5_mm, bv // 2 - 1)
                    po.indirect_dma_start(flat2(vb[bv % 4]), None, vsrc, bass.IndirectOffsetOnAxis(idxs[:, bv:bv + 1], 0)).then_inc(vg_ld[bv % 4], 16)
            for q in range(4):
                po.wait_ge(vg_ld[q], 32)
            for q in range(2):
                po.wait_ge(kg_ld[q], 64)
            for tt in range(NTT):
                n = rows_of(tt)
                po.wait_ge(y_out, tt + 1)
                dst = y_prompt[0, tt * P:tt * P + n, :] if tt < NTT - 1 else y_sample.rearrange("b t c -> (b t) c")
                po.dma_start(dst, yo[0:n, :]).then_inc(y_st, 16)
            po.wait_ge(y_st, 16 * NTT)

        @block.tensor
        def _(pe):
            pe.wait_ge(const_ld, 16 * 4)
            pe.wait_ge(c_ld, 48)
            for k in range(KC):
                ins = pe.transpose(PS[:, 7, 29 * k:29 * k + 29], vrow[:, k * P:(k + 1) * P], ident[0:29, 0:29])
            ins.then_inc(ct_pe, 1)
            pe.wait_ge(ct_dve, 1)
            for ch in range(6):
                pe.wait_ge(adaw_ld[ch % 2], 16 * (ch // 2 + 1))
                if ch >= 2:
                    pe.wait_ge(ada_ev, ch - 1)
                for k in range(KC):
                    ins = pe.matmul(PS[0:9, 1 + ch % 2, :], vcol[:, k, 0:9], adaw[ch % 2][:, k, :], start=(k == 0), stop=(k == KC - 1))
                ins.then_inc(ada_mm, 1)
            pe.wait_ge(ada_ev, 4)
            for c in range(16):
                ins = pe.transpose(PS[:, 0, 9 * c:9 * c + 9], adar[:, c * P:(c + 1) * P], ident[0:9, 0:9])
            ins.then_inc(ada_t, 1)
            pe.wait_ge(rel_ld, 64)
            pe.wait_ge(tb_rel, 1)
            pe.wait_ge(pch, 1)
            pe.matmul(PS[0:NH, 7, 0:XW], relx[:, :], krow, start=True, stop=True)
            for m in range(4):
                ins = pe.matmul(PS[:, 7, XW + NH * m:XW + NH * m + NH], kcmpd[:, m, :], relx[:, :], start=True, stop=True)
            ins.then_inc(tb_mm, 1)

            def transpose_x(tt):
                n, bank = rows_of(tt), 3 + 2 * (tt % 2)
                pe.wait_ge(x_n, tt + 1)
                if tt >= 2:
                    pe.wait_ge(h_ev, tt - 1)
                for k in range(KC):
                    ins = pe.transpose(PS[:, bank + k // 4, P * (k % 4):P * (k % 4) + n], xb[tt % 2][0:n, k * P:(k + 1) * P], ident[0:n, 0:n])
                ins.then_inc(x_t, 1)

            def kv(tt):
                n = rows_of(tt)
                pe.wait_ge(h_hi, tt + 1)
                pe.wait_ge(h_lo, tt + 1)
                for c in range(2):
                    m = 2 * tt + c
                    pe.wait_ge(wk_hi, c + 1)
                    pe.wait_ge(wk_lo, c + 1)
                    if m >= 4:
                        pe.wait_ge(kv_ev, m - 3)
                    out = PS[0:n, KVB[m % 4], 0:(KV0, KV1)[c]]
                    for k in range(KC):
                        a, b = hhi[:, k, tt * P:tt * P + n], hlo[:, k, tt * P:tt * P + n]
                        pe.matmul(out, a, wkh[c][:, k, :], start=(k == 0), stop=False)
                        pe.matmul(out, a, wkl[c][:, k, :], start=False, stop=False)
                        ins = pe.matmul(out, b, wkh[c][:, k, :], start=False, stop=(k == KC - 1))
                    ins.then_inc(kv_mm, 1)
                    if c == 0 and tt + 1 < NTT:
                        transpose_x(tt + 1)

            transpose_x(0)
            pe.wait_ge(ada_col, 1)
            pe.wait_ge(ada_ev, 6)
            pe.wait_ge(tb_ev, 2)
            for tt in range(NTT):
                kv(tt)
            pe.wait_ge(kv_ev, 2 * NTT)
            pe.wait_ge(h_ev, NTT)

            def project(j, kind, first):
                n = NK * j + kind
                pe.wait_ge(w_hi, n + 1)
                pe.wait_ge(w_lo, n + 1)
                if not first:
                    pe.wait_ge(p2_ev[kind % 2], NK // 2 * j + kind // 2)
                bank = 3 * (kind % 2)
                for k in range(KC):
                    for a, b in ((wh, hhi), (wh, hlo), (wl, hhi)):
                        for c in range(3):
                            ins = pe.matmul(PS[:, bank + c, 0:CH], a[kind % 2][:, k, :], b[:, k, c * CH:(c + 1) * CH],
                                            start=(k == 0 and b is hhi and a is wh), stop=(k == KC - 1 and a is wl))
                ins.then_inc(p2_mm, 1)

            def tails(j):
                pe.wait_ge(tail_rdy, j + 1)
                if j >= 1:
                    pe.wait_ge(tail_ev, j)
                pe.transpose(PS[0:18, 6, 0:P], tail[:, :], ident[:, :]).then_inc(tail_t, 1)

            for j in range(8):
                for kind in range(NK):
                    project(j, kind, j == 0 and kind < 2)
                    if kind == ZC:
                        tails(j)
            for e in (0, 1):
                pe.wait_ge(p2_ev[e], 24)
            pe.wait_ge(tail_ev, 8)
            for c in range(2):
                def turn(t):
                    q = t // 16
                    if t % 16 == 0:
                        pe.wait_ge(xq_ld[q], 32 * (c + 1))
                        pe.wait_ge(xp_ld[q], 64 * (c + 1))
                    n = 64 * c + t
                    if n >= 4:
                        pe.wait_ge(xe[t % 2], n // 2 - 1)
                    col = slice(t % 16 * DKV, (t % 16 + 1) * DKV)
                    pe.transpose(PS[:, t % 4, 0:P], xq[q][:, 0, col], ident[:, :])
                    pe.transpose(PS[:, t % 4, P:2 * P], xq[q][:, 1, col], ident[:, :])
                    pe.transpose(PS[:, t % 4, 2 * P:CB], xpq[q][:, col], ident[0:NPB + 1, 0:NPB + 1]).then_inc(x3_t, 1)

                def pair(m):
                    for e in (0, 1):
                        pe.wait_ge(xe[e], 32 * c + m + 1)
                    for g in range(NG):
                        ins = pe.matmul(PS[:, 4 + g, 0:CB], w1[c][:, m, :], xt[m % 2][:, g, :], start=(m == 0), stop=(m == 31))
                    ins.then_inc(x3_mm, 1)

                turn(0)
                turn(1)
                for m in range(32):
                    if m < 31:
                        turn(2 * m + 2)
                        turn(2 * m + 3)
                    pair(m)
                pe.wait_ge(w2_ld, 64)
                pe.wait_ge(hs_rdy, c + 1)
                if c == 0:
                    for g in range(NG):
                        pe.matmul(PS[64 * g:64 * g + 64, 6, 0:2 * P], w2[c][:, 0:64], hs3[:, g, 0:2 * P], start=True, stop=True)
                    for g in range(NG):
                        ins = pe.matmul(PS[:, 7, NPB * g:NPB * g + NPB], w2[c][:, :], hs3[:, g, 2 * P:2 * P + NPB], start=True, stop=True)
                    ins.then_inc(c3_mm, 1)
                else:
                    pe.wait_ge(c3_ev, 2)
                    for b in range(NB):
                        for g in range(NG):
                            pe.matmul(PS[0:NSB, 6 + b // 4, (b % 4) * P + 64 * g:(b % 4) * P + 64 * g + 64], hs3[:, g, NSB * b:NSB * b + NSB], w2[c][:, 0:64], start=True, stop=True)
                    for g in range(NG):
                        ins = pe.matmul(PS[0:NPB, 4, 64 * g:64 * g + 64], hs3[:, g, 2 * P:2 * P + NPB], w2[c][:, 0:64], start=True, stop=True)
                    ins.then_inc(c3_mm, 1)
            pe.wait_ge(xe[0], 64)
            pe.wait_ge(xe[1], 64)
            for a, col in enumerate((C_KS, C_KW)):
                if a:
                    pe.wait_ge(c3_ev, 5)
                for half in range(2):
                    for q in range(4):
                        ins = pe.transpose(PS[:, 4 * a + half, q * P:(q + 1) * P], kvt[:, 4 * half + q, col:col + DKV], ident[:, :])
                    ins.then_inc(kt_t, 1)

            def scores(w, h):
                u, n = w // 2, 4 * w + h
                g, hs, i = unit(u)
                if h == 0:
                    pe.wait_ge(q_ld[u % 4], 16 * (u // 4 + 1))
                if n >= 2:
                    pe.wait_ge(e_done, n - 1)
                b0 = 2 * (n % 2)
                q = qb[u % 4][:, h, :]
                kh, kl = (ksh, ksl) if w % 2 == 0 else (kwh, kwl)
                k, parts = keys_of(w)
                a = (i + 1) * P - k
                for c, m in enumerate(parts):
                    last, masked = c == len(parts) - 1, w % 2 and i >= 4 and c == 0
                    pe.matmul(PS[:, b0 + c, 0:m], q, kh[:, g, a:a + m], start=True, stop=False)
                    ins = pe.matmul(PS[:, b0 + c, 0:m], q, kl[:, g, a:a + m], start=False, stop=not (last or masked))
                    if masked:
                        ins = pe.matmul(PS[:, b0 + c, 0:P], identr[:, :], edger[:, :], start=False, stop=not last)
                    if last:
                        r = min(2 * P, k)
                        head = HPG * g + 4 * hs + h
                        pe.matmul(PS[:, b0 + c, m - r:m], identr[:, :], near[:, head, 2 * P - r:2 * P], start=False, stop=False)
                        ins = pe.matmul(PS[:, b0 + c, m - r:m], identr[:, :], nearl[:, head, 2 * P - r:2 * P], start=False, stop=True)
                    a += m
                if w % 2 and h == 3:
                    for hh in range(4):
                        c0_ = 384 + 2 * NPB * hh
                        ins = pe.matmul(PS[:, b0 + 1, c0_:c0_ + 2 * NPB], qb[u % 4][:, hh, :], kcp[:, g, :], start=True, stop=True)
                ins.then_inc(s_mm, 1)

            def turn_p(w, t):
                tc = tile0[w] + t
                if t == 0:
                    if ON_ACT[w % 2]:
                        pe.wait_ge(n_act, (w + 1) if ACT_A and ACT_B else w // 2 + 1)
                    pe.wait_ge(n_dve, w + 1)
                if tc >= 2:
                    pe.wait_ge(pt_hi, tc - 1)
                    pe.wait_ge(pt_lo, tc - 1)
                for h in range(4):
                    cmp_ = w % 2 and t == tiles_of(w) - 1
                    src = prc[w % 3][:, h, :] if cmp_ else pr[w % 3][:, h, t * P:(t + 1) * P]
                    ins = pe.transpose(PS[:, 4 + tc % 2, h * P:(h + 1) * P], src, ident[:, :])
                ins.then_inc(t_mm, 1)

            def values(w, t):
                tc, u = tile0[w] + t, w // 2
                g, hs, i = unit(u)
                pe.wait_ge(pt_hi, tc + 1)
                pe.wait_ge(pt_lo, tc + 1)
                first, last = w % 2 == 0 and t == 0, w % 2 == 1 and t == tiles_of(w) - 1
                if first and u:
                    pe.wait_ge(o_ev, u)
                v = vsx[:, t, g, :] if w % 2 == 0 else vcp[:, g, :] if last else vwx[:, max(0, i - 4) + t, g, :]
                pe.matmul(PS[:, 6, :], v, pth[tc % 2][:, :], start=first, stop=False)
                pe.matmul(PS[:, 6, :], v, ptl[tc % 2][:, :], start=False, stop=last).then_inc(pv_mm, 1)

            def reduce_o(u):
                g = unit(u)[0]
                pe.wait_ge(o_ev, u + 1)
                if u:
                    pe.wait_ge(r_ev, u)
                pe.matmul(PS[64 * g:64 * g + 64, 7, :], stack2[:, :], osb[:, :], start=True, stop=True).then_inc(r_mm, 1)

            pe.wait_ge(vb_hi, 5)
            pe.wait_ge(vb_lo, 3)
            for w in range(2):
                pe.wait_ge(kt_hi, 2 * w + 2)
                pe.wait_ge(kt_lo, 2 * w + 2)
                for h in range(4):
                    scores(w, h)
            pe.wait_ge(vb_hi, 6)
            pe.wait_ge(vb_lo, 4)
            behind = None
            for w in range(NI):
                for h, part in enumerate(slots(w)):
                    for t in part or [None]:
                        if t in (None, part.start) and w + 2 < NI:
                            scores(w + 2, h)
                        if t is not None:
                            turn_p(w, t)
                        if t is not None:
                            if behind:
                                values(*behind)
                            behind = (w, t)
                    if h == 2 and w % 2 == 0 and w:
                        reduce_o(w // 2 - 1)
            values(*behind)
            reduce_o(NU - 1)
            pe.wait_ge(r_ev, NU)
            pe.wait_ge(pt_lo, tile0[NI])
            pe.wait_ge(c5_ld, 16 * 10)
            gi = [0]

            def group(ops):
                n = gi[0]
                if n >= 2:
                    pe.wait_ge(*copied(n - 2))
                for q, (k, src) in enumerate(ops):
                    ins = pe.transpose(PS[0:k, 6 + n % 2, q * P:(q + 1) * P], src, ident[:, :])
                ins.then_inc(t5, 1)
                gi[0] += 1

            for a, col in enumerate((C_KS, C_KW)):
                ins = pe.transpose(PS[:, 5, 256 + SAMP * a:256 + SAMP * a + SAMP], kvs[0:SAMP, col:col + DKV], ident[0:SAMP, 0:SAMP])
            ins.then_inc(kn_t, 1)
            pe.wait_ge(kn_ev, 1)
            pe.wait_ge(q5_rdy, 1)

            turns5 = [0]

            def bank5():
                if turns5[0]:
                    pe.wait_ge(b5_rd, turns5[0])
                turns5[0] += 1

            def first_scores(pq):
                bank5()
                for b2 in range(2):
                    ins = pe.matmul(PS[64 * b2:64 * b2 + 64, 5, 64:96], qbd[:, 2 * pq + b2, :], kcs[:, NSB * (2 * pq + b2):NSB * (2 * pq + b2 + 1)], start=True, stop=True)
                ins.then_inc(s5c_mm, 1)

            def key_turns(pq):
                for b2 in range(2):
                    pe.wait_ge(kg_ld[b2], 16 * (pq + 1))
                    for q in range(NSEL // 4):
                        group([(P, kb[b2][:, 4 * q + r, :]) for r in range(4)])
                    pe.wait_ge(kw_ld[b2], 16 * (pq + 1))
                    group([(P, kwb[b2][:, r, :]) for r in range(4)])

            def pair_scores(pq):
                for n in (2, 1):
                    pe.wait_ge(*copied(gi[0] - n))
                if pq:
                    pe.wait_ge(s5_ev, pq)
                for b2 in range(2):
                    q = qbd[:, 2 * pq + b2, :]
                    half = slice(64 * b2, 64 * b2 + 64)
                    kt = kt5[b2][:, :, :].rearrange("p i c -> p (i c)")
                    for c in range(5):
                        pe.matmul(PS[half, c, :], q, kt[:, 512 * c:512 * c + 512], start=True, stop=True)
                bank5()
                for b2 in range(2):
                    q = qbd[:, 2 * pq + b2, :]
                    half = slice(64 * b2, 64 * b2 + 64)
                    for a in range(2):
                        ins = pe.matmul(PS[half, 5, SAMP * a:SAMP * a + SAMP], q, knt[:, a, :], start=True, stop=True)
                ins.then_inc(s5_mm, 1)

            def importance(pq):
                pe.wait_ge(pn_rdy, pq + 1)
                bank5()
                pe.matmul(PS[:, 5, 96:128], grp[:, :], pn[:, :], start=True, stop=True).then_inc(imp_mm, 1)

            def pair_values(pq):
                pe.wait_ge(p5, pq + 1)
                s = s5[pq % 2]
                pos = [P * r for r in range(NSEL)] + [SEL + P * r for r in range(NWIN)]
                for q in range(5):
                    group([(P, s[:, a:a + P]) for a in pos[4 * q:4 * q + 4]])
                group([(SAMP, s[:, PAST:SEL]), (SAMP, s[:, SEL + WIN:SEL + WN]), (NSB, cmg[:, :])])
                pe.wait_ge(*copied(gi[0] - 1))
                bank5()
                for b2 in range(2):
                    b = 2 * pq + b2
                    pe.wait_ge(vg_ld[b % 4], 16 * (b // 4 + 1))
                    pe.wait_ge(vw_ld[b % 4], 16 * (b // 4 + 1))
                    half = slice(64 * b2, 64 * b2 + 64)
                    ops = [(pt5[:, r, half], vb[b % 4][:, r, :]) for r in range(NSEL)]
                    ops += [(pt5[:, NSEL + r, half], vwb[b % 4][:, r, :]) for r in range(NWIN)]
                    ops += [(pt5[0:SAMP, 20, half], kvs[0:SAMP, C_VS:C_VS + DKV]), (pt5[0:SAMP, 21, half], kvs[0:SAMP, C_VW:C_VW + DKV]),
                            (pt5[0:NSB, 22, half], vcs[:, b, :])]
                    for n, (a, v) in enumerate(ops):
                        ins = pe.matmul(PS[half, 5, P:2 * P], a, v, start=(n == 0), stop=(n == len(ops) - 1))
                ins.then_inc(o5_mm, 1)
                bank5()
                pe.wait_ge(o5_cp, pq + 1)
                pe.transpose(PS[:, 5, 256:384], o5[:, :], ident[:, :]).then_inc(ot_t, 1)

            key_turns(0)
            first_scores(0)
            pair_scores(0)
            importance(0)
            for pq in range(4):
                if pq < 3:
                    key_turns(pq + 1)
                    first_scores(pq + 1)
                    pair_scores(pq + 1)
                    importance(pq + 1)
                pair_values(pq)
            pe.wait_ge(mix5_rdy, 4)
            pe.wait_ge(s5_ev, 4)
            pe.wait_ge(*copied(gi[0] - 1))
            for tt in range(NTT):
                n, b0 = rows_of(tt), 2 * (tt % 4)
                if tt >= 4:
                    pe.wait_ge(y_ev, tt - 3)
                for k in range(16):
                    if k % 8 == 0:
                        pe.wait_ge(m_hi, 2 * tt + k // 8 + 1)
                        pe.wait_ge(m_lo, 2 * tt + k // 8 + 1)
                    if tt == 0:
                        pe.wait_ge(wo_hi, k + 1)
                        pe.wait_ge(wo_lo, k + 1)
                    for a, b in ((mh, woh), (mh, wol), (ml, woh)):
                        for c in range(2):
                            ins = pe.matmul(PS[0:n, b0 + c, :], a[:, k, 0:n], b[k][:, 512 * c:512 * c + 512],
                                            start=(k == 0 and a is mh and b is woh), stop=(k == 15 and a is ml))
                    if k % 8 == 7:
                        ins.then_inc(y_mm, 1)

        @block.scalar
        def _(act):
            def hi(tt):
                n = rows_of(tt)
                act.wait_ge(h_ev, tt + 1)
                act.activation(hhi[:, :, tt * P:tt * P + n], h32[:, :, 0:n], ACT.Copy).then_inc(h_hi, 1)

            def kv_evac(tt, c):
                m, n = 2 * tt + c, rows_of(tt)
                act.wait_ge(kv_mm, m + 1)
                cols = slice(c * KV0, c * KV0 + (KV0, KV1)[c])
                act.activation(kvt[:, tt, cols] if tt < NTT - 1 else kvs[0:n, cols], PS[0:n, KVB[m % 4], 0:(KV0, KV1)[c]], ACT.Copy).then_inc(kv_ev, 1)

            for tt in range(NTT):
                n = rows_of(tt)
                act.wait_ge(x_ld[tt % 2], 16 * (tt // 2 + 1))
                if tt:
                    act.wait_ge(h_lo, tt)
                    act.wait_ge(h_hi, tt)
                act.activation(h32[0:n, :, :].rearrange("p a b -> p (a b)"), xb[tt % 2][0:n, :], ACT.Square,
                               accum_out=ssq[0:n, tt:tt + 1]).then_inc(x_act, 1)
                act.wait_ge(x_ms, tt + 1)
                act.activation(rms[0:n, tt:tt + 1], ms[0:n, tt:tt + 1], ACT.Sqrt).then_inc(x_act, 1)
                if tt == 0:
                    act.wait_ge(ada_t, 1)
                    act.wait_ge(ada_mm, 6)
                    act.wait_ge(ada_ev, 6)
                    act.wait_ge(wk_ld, 32)
                    for c in range(2):
                        act.activation(wkh[c][:, :, :], wkr[c][:, :, :], ACT.Copy).then_inc(wk_hi, 1)
                        if c == 0:
                            hi(tt)
                else:
                    hi(tt)
                if tt:
                    kv_evac(tt - 1, 0)
                    kv_evac(tt - 1, 1)
            kv_evac(NTT - 1, 0)
            kv_evac(NTT - 1, 1)

            act.wait_ge(kv_mm, 2 * NTT)
            act.wait_ge(h_lo, NTT)

            def split(j, kind, first):
                n = NK * j + kind
                act.wait_ge(wr_ld[kind % 2], wr_count(j, kind))
                if not first:
                    act.wait_ge(p2_mm, n - 1)
                act.activation(wh[kind % 2][:, :, :], wr[kind % 2][:, :, :], ACT.Copy).then_inc(w_hi, 1)

            def ev(j, kind):
                n = NK * j + kind
                src = PS[:, 3 * (kind % 2):3 * (kind % 2) + 3, 0:CH]
                act.wait_ge(p2_mm, n + 1)
                v = lambda t: t[:, 0:TOK].rearrange("p (a b) -> p a b", a=3)
                if kind == CC:
                    if j:
                        act.wait_ge(p2_ev[1], 3 * j - 2)
                    act.activation(v(cct), src, ACT.Copy).then_inc(p2_ev[0], 1)
                elif kind == ZC:
                    if j:
                        act.wait_ge(y_rdy, j)
                    act.activation(v(zt), src, ACT.Silu).then_inc(p2_ev[1], 1)
                elif kind == ZA:
                    if j:
                        act.wait_ge(zab_st, 16 * j)
                    act.activation(v(zab), src, ACT.Silu).then_inc(p2_ev[0], 1)
                elif kind == QQ:
                    if j:
                        act.wait_ge(q_st, 64 * j)
                    act.activation(v(qhi), src, ACT.Copy, scale=0.125).then_inc(q_hi, 1)

            split(0, 0, True)
            for j in range(8):
                for kind in range(NK):
                    if not (j == 7 and kind == NK - 1):
                        jn, kn = (j, kind + 1) if kind + 1 < NK else (j + 1, 0)
                        split(jn, kn, j == 0 and kind == 0)
                    ev(j, kind)
            act.activation(sg[:, 0:8, :], kvt[:, 0:8, C_G:C_G + 3 * NH], ACT.Sigmoid).then_inc(sg_rdy, 1)
            act.activation(sg[0:SAMP, 8, :], kvs[0:SAMP, C_G:C_G + 3 * NH], ACT.Sigmoid).then_inc(sg_rdy, 1)
            for c in range(2):
                for m in range(32):
                    act.wait_ge(x3_t, 64 * c + 2 * m + 2)
                    if 32 * c + m >= 2:
                        act.wait_ge(x3_mm, 32 * c + m - 1)
                    bank = (2 * m + 1) % 4
                    for g in range(NG):
                        ins = act.activation(xt[m % 2][64:128, g, :], PS[64 * g:64 * g + 64, bank, 0:CB], ACT.Copy)
                    ins.then_inc(xe[1], 1)
                act.wait_ge(pe_rdy, c + 1)
                act.wait_ge(x3_mm, 32 * (c + 1))
                if c:
                    act.wait_ge(c3_mm, 1)
                for g in range(NG):
                    ins = act.activation(hs3[:, g, :], PS[:, 4 + g, 0:CB], ACT.Silu, bias=pebias[:, c:c + 1])
                ins.then_inc(hs_rdy, 1)
                if c == 0:
                    act.wait_ge(c3_mm, 1)
                    act.activation(kcp[:, :, 0:NPB], PS[:, 7, 0:2 * NPB].rearrange("p (g n) -> p g n", g=NG), ACT.Copy).then_inc(c3_hi, 1)
                else:
                    act.wait_ge(c3_mm, 2)
                    act.wait_ge(pad0, 1)
                    act.activation(vcp[0:NPB, :, 0:64], PS[0:NPB, 4, 0:P].rearrange("p (g d) -> p g d", g=NG), ACT.Copy).then_inc(c3_hi, 1)
            act.wait_ge(c3_mm, 2)
            for v, col in ((vsx, C_VS), (vwx, C_VW)):
                act.activation(v[:, :, :, 0:64], kvt[:, 0:8, col:col + DKV].rearrange("p t (g d) -> p t g d", g=NG), ACT.Copy).then_inc(vb_hi, 1)
            act.wait_ge(c4_ld, 64)
            act.activation(identr[:, :], ident[:, :], ACT.Copy).then_inc(vb_hi, 1)
            act.activation(edger[:, :], edge[:, :], ACT.Copy).then_inc(vb_hi, 1)
            act.activation(near[:, 0:4, :], nearr[:, 0:4, :], ACT.Copy).then_inc(vb_hi, 1)

            def keys_high(a):
                kh = (ksh, kwh)[a]
                for half in range(2):
                    act.wait_ge(kt_t, 2 * a + half + 1)
                    for g in range(NG):
                        for r in range(2):
                            ins = act.activation(kh[64 * r:64 * r + 64, g, 512 * half:512 * half + 512], PS[64 * g:64 * g + 64, 4 * a + half, :], ACT.Copy)
                    ins.then_inc(kt_hi, 1)

            def exps(w, h):
                n, u = 4 * w + h, w // 2
                g, hs, i = unit(u)
                act.wait_ge(m_rdy, n + 1)
                if h == 0 and w >= 3:
                    act.wait_ge(t_mm, tile0[w - 2])
                k, parts = keys_of(w)
                b0, r = 2 * (n % 2), w % 3
                out = pr[r][:, h, 0:k].rearrange("p (a b) -> p a b", a=len(parts))
                act.activation(out, PS[:, b0:b0 + len(parts), 0:parts[0]], ACT.Exp, bias=nm[:, r, h:h + 1], accum_out=rsum[:, r, h:h + 1]).then_inc(e_done, 1)
                if w % 2 and h == 3:
                    act.wait_ge(mc_rdy, u + 1)
                    act.activation(prc[r][:, :, 0:2 * i + 2], cs[:, :, 0:2 * i + 2], ACT.Exp).then_inc(ec_done, 1)

            def scale(w):
                act.wait_ge(r_rdy, w + 1)
                for h in sorted(ON_ACT[w % 2]):
                    k, r = keys_of(w)[0], w % 3
                    ins = act.activation(pr[r][:, h, 0:k], pr[r][:, h, 0:k], ACT.Copy, scale=rg[:, r, h:h + 1])
                ins.then_inc(n_act, 1)

            def high(w, t):
                tc = tile0[w] + t
                act.wait_ge(t_mm, tc + 1)
                if tc >= 2:
                    act.wait_ge(pv_mm, tc - 1)
                act.activation(pth[tc % 2][:, :], PS[:, 4 + tc % 2, :], ACT.Copy).then_inc(pt_hi, 1)

            def sums(u):
                act.wait_ge(pv_mm, tile0[2 * u + 2])
                if u:
                    act.wait_ge(r_mm, u)
                act.activation(osb[:, :], PS[:, 6, :], ACT.Copy).then_inc(o_ev, 1)

            keys_high(0)
            for w in range(2):
                for h in range(4):
                    exps(w, h)
                if w == 0:
                    keys_high(1)
                    act.activation(near[:, 4:NH, :], nearr[:, 4:NH, :], ACT.Copy).then_inc(vb_hi, 1)
            act.wait_ge(vb_lo, 4)
            scale(0)
            behind, ahead = None, None
            for w in range(NI):
                for h, part in enumerate(slots(w)):
                    for t in part or [None]:
                        if t in (None, part.start):
                            if ahead:
                                exps(*ahead)
                            ahead = (w + 2, h) if w + 2 < NI else None
                        if t is not None:
                            high(w, t)
                            if behind is not None:
                                sums(behind)
                                behind = None
                    if w + 1 < NI and h == 2:
                        scale(w + 1)
                if w % 2:
                    behind = w // 2
            sums(NU - 1)
            act.wait_ge(r_mm, NU)
            act.wait_ge(kn_t, 1)
            act.activation(knt[:, :, :], PS[:, 5, 256:256 + 2 * SAMP].rearrange("p (a c) -> p a c", a=2), ACT.Copy).then_inc(kn_ev, 1)
            gi = [0]

            def copy_group(dst, k=P, m=4):
                n = gi[0]
                act.wait_ge(t5, n + 1)
                act.activation(dst, PS[0:k, 6 + n % 2, 0:m * P].rearrange("p (a c) -> p a c", a=m), ACT.Copy).then_inc(ev5, 1)
                gi[0] += 1

            def wo_high(j):
                act.wait_ge(wo_ld[j % 2], 16 * (2 * (j // 2 + 1) if j < 8 else 8 + (j - 8) // 2 + 1))
                act.activation(woh[j][:, :], wor[j % 2][:, :], ACT.Copy).then_inc(wo_hi, 1)

            def key_copies(pq, part):
                if pq:
                    act.wait_ge(s5_mm, pq)
                for m in part:
                    if by_dve[gi[0]]:
                        gi[0] += 1
                    else:
                        copy_group(kt5[m // 5][:, m % 5 * 4:m % 5 * 4 + 4, :])

            def exp_cmp(pq):
                act.wait_ge(m5c, pq + 1)
                act.activation(cm[:, :], cm[:, :], ACT.Exp, bias=n5[:, 2:3], accum_out=r5[:, 2:3]).then_inc(e5c, 1)

            def exp_rest(pq):
                act.wait_ge(m5, pq + 1)
                s = s5[pq % 2]
                act.activation(s[:, 0:SEL], s[:, 0:SEL], ACT.Exp, bias=n5[:, 0:1], accum_out=r5[:, 0:1])
                act.activation(s[:, SEL:SEL + WN], s[:, SEL:SEL + WN], ACT.Exp, bias=n5[:, 1:2], accum_out=r5[:, 1:2]).then_inc(e5, 1)

            key_copies(0, range(10))
            exp_cmp(0)
            key_copies(1, range(4))
            exp_rest(0)
            for pq in range(4):
                if pq < 3:
                    key_copies(pq + 1, range(4, 10))
                    exp_cmp(pq + 1)
                    for j in early(pq):
                        wo_high(j)
                if pq:
                    act.wait_ge(o5_mm, pq)
                for q in range(5):
                    copy_group(pt5[:, 4 * q:4 * q + 4, :])
                copy_group(pt5[0:SAMP, 20:23, :], SAMP, 3)
                act.wait_ge(o5_mm, pq + 1)
                act.activation(o5[:, :], PS[:, 5, P:2 * P], ACT.Copy).then_inc(o5_cp, 1)
                act.wait_ge(o5_cp, pq + 1)
                act.sem_inc(b5_rd, 1)
                if pq == 3:
                    act.wait_ge(t5, keys_turned(NB - 1, True))
                    for j in early(3):
                        wo_high(j)
                if pq < 2:
                    key_copies(pq + 2, range(4))
                if pq < 3:
                    exp_rest(pq + 1)
            act.wait_ge(o5_mm, 4)
            act.wait_ge(ot_t, 4)

            def mix_high(tt):
                n = rows_of(tt)
                for a in range(2):
                    act.wait_ge(mr_ld[a], 16 * (tt + 1))
                    if tt:
                        act.wait_ge(y_mm, 2 * tt - 1 + a)
                    ks = slice(8 * a, 8 * a + 8)
                    act.activation(mh[:, ks, 0:n], mr[:, ks, 0:n], ACT.Copy).then_inc(m_hi, 1)

            def squares(tt):
                n = rows_of(tt)
                act.wait_ge(y_sum, tt + 1)
                if tt:
                    act.wait_ge(y_st, 16 * tt)
                act.activation(yo[0:n, :], yf[0:n, :], ACT.Square, accum_out=s6[0:n, 0:1]).then_inc(y_act, 1)
                act.wait_ge(y_ms, tt + 1)
                act.activation(s6[0:n, 2:3], s6[0:n, 1:2], ACT.Sqrt).then_inc(y_act, 1)

            mix_high(0)
            for j in range(8, 16):
                wo_high(j)
            for tt in range(NTT):
                if tt + 1 < NTT:
                    mix_high(tt + 1)
                squares(tt)

        @block.vector
        def _(dve):
            chain = Chain(dve, dch)
            link = chain.link
            dve.wait_ge(rel_ld, 64)
            dve.wait_ge(ct_pe, 1)
            dve.tensor_copy(vcol[:, :, :], PS[:, 7, 0:232].rearrange("p (k c) -> p k c", c=29)).then_inc(ct_dve, 1)
            dve.wait_ge(ct_dve, 1)
            dve.tensor_tensor(relx[0:32, :], relx[0:32, :], rel31[:, :], ALU.subtract).then_inc(tb_rel, 1)
            for ch in range(6):
                dve.wait_ge(ada_mm, ch + 1)
                out = adar[:, 512 * ch:512 * ch + 512] if ch < 4 else gate[:, 512 * (ch - 4):512 * (ch - 3)]
                dve.tensor_tensor(out, PS[0:9, 1 + ch % 2, :], adab[:, 512 * ch:512 * ch + 512], ALU.add).then_inc(ada_ev, 1)
            dve.wait_ge(ada_t, 1)
            both = PS[:, 0, 0:144].rearrange("p (k c) -> p k c", c=9)
            link(dve.tensor_copy(scB[:, :, :], both[:, 0:8, :]))
            dve.scalar_tensor_tensor(scA[:, :, :], both[:, 8:16, :], 1.0, ext(vcol[:, :, 9], (0, 9)), ALU.add, ALU.mult).then_inc(ada_col, 1)
            dve.wait_ge(ada_col, 1)
            dve.wait_ge(tb_mm, 1)
            dve.tensor_copy(rows[:, :], PS[0:NH, 7, 0:XW]).then_inc(tb_ev, 1)
            dve.tensor_copy(tcmp[:, :, :], PS[:, 7, XW:XW + 64].rearrange("p (m h) -> p m h", m=4)).then_inc(tb_ev, 1)
            for tt in range(NTT):
                if tt == 1:
                    dve.wait_ge(idx_ld, 16 * (2 + NB))
                    dve.wait_ge(idx_a, 1)
                    link(dve.tensor_scalar(pidx[:, 1:2], pidx[:, 0:1], 7, None, ALU.bitwise_and))
                    link(dve.tensor_scalar(pidx[:, 0:1], pidx[:, 0:1], 1, None, ALU.bitwise_and))
                    dve.scalar_tensor_tensor(idxc[:, :], pgc[:, :], 2, ext(bass.AP(pidx[:, 0:1].tensor, pidx[:, 0:1].offset, [list(pidx[:, 0:1].ap[0])]), (0, 2)), ALU.mult, ALU.add).then_inc(idx_b, 1)
                    dve.wait_ge(idx_b, 1)
                    for q in range(4):
                        ins = dve.tensor_scalar(idxq[:, :, q], idxc[:, :], 4, q, ALU.mult, ALU.add)
                    ins.then_inc(idx_b, 1)
                    dve.scalar_tensor_tensor(idxs[:, :], pgs[:, :], 8, ext(bass.AP(pidx[:, 1:2].tensor, pidx[:, 1:2].offset, [list(pidx[:, 1:2].ap[0])]), (0, NB)), ALU.mult, ALU.add).then_inc(idx_b, 1)
                n = rows_of(tt)
                one = slice(tt, tt + 1)
                dve.wait_ge(x_act, 2 * tt + 1)
                dve.tensor_scalar(ms[0:n, one], ssq[0:n, one], 1.0 / D, EPS, ALU.mult, ALU.add).then_inc(x_ms, 1)
                dve.wait_ge(x_act, 2 * tt + 2)
                link(dve.reciprocal(rstd[0:n, one], rms[0:n, one]))
                dve.tensor_scalar(xb[tt % 2][0:n, :], xb[tt % 2][0:n, :], rstd[0:n, one], None, ALU.mult).then_inc(x_n, 1)
                dve.wait_ge(x_t, tt + 1)
                bank = 3 + 2 * (tt % 2)
                for k in range(KC):
                    src = PS[:, bank + k // 4, P * (k % 4):P * (k % 4) + n]
                    if tt < NTT - 1:
                        ins = dve.tensor_scalar(h32[:, k, 0:n], src, scA[:, k, 0:1], scB[:, k, 0:1], ALU.mult, ALU.add)
                    else:
                        v = lambda t: t.rearrange("p (b t) -> p b t", t=TS)
                        link(dve.tensor_tensor(v(h32[:, k, 0:n]), v(src), ext(scA[:, k, 1:9], (0, TS)), ALU.mult))
                        ins = dve.tensor_tensor(v(h32[:, k, 0:n]), v(h32[:, k, 0:n]), ext(scB[:, k, 1:9], (0, TS)), ALU.add)
                    if k < KC - 1:
                        link(ins) if tt == NTT - 1 else ins.then_inc(dch, 1)
                        if tt < NTT - 1:
                            chain.n += 1
                dve.wait_ge(dch, chain.n)
                ins.then_inc(h_ev, 1)
                dve.wait_ge(h_ev, tt + 1)
                dve.wait_ge(h_hi, tt + 1)
                dve.tensor_tensor(hlo[:, :, tt * P:tt * P + n], h32[:, :, 0:n], f32(hhi[:, :, tt * P:tt * P + n]), ALU.subtract).then_inc(h_lo, 1)
                if tt == 0:
                    for c in range(2):
                        dve.wait_ge(wk_hi, c + 1)
                        dve.tensor_tensor(wkl[c][:, :, :], wkr[c][:, :, :], f32(wkh[c][:, :, :]), ALU.subtract).then_inc(wk_lo, 1)
            dve.wait_ge(kv_mm, 2 * NTT)
            dve.wait_ge(h_lo, NTT)
            link(dve.memset(uu[:, 0:2], 0.0))

            def split(j, kind, first):
                n = NK * j + kind
                dve.wait_ge(w_hi, n + 1)
                if not first:
                    dve.wait_ge(p2_mm, n - 1)
                dve.tensor_tensor(wl[kind % 2][:, :, :], wr[kind % 2][:, :, :], f32(wh[kind % 2][:, :, :]), ALU.subtract).then_inc(w_lo, 1)

            def ev(j, kind):
                n = NK * j + kind
                src = PS[:, 3 * (kind % 2):3 * (kind % 2) + 3, 0:CH]
                v = lambda t: t[:, 0:TOK].rearrange("p (a b) -> p a b", a=3)
                if kind == HC:
                    dve.wait_ge(p2_mm, n + 1)
                    dve.wait_ge(p2_ev[0], 3 * j + 1)
                    if j:
                        dve.wait_ge(tail_t, j)
                    dve.tensor_tensor(v(uu[:, 2:2 + TOK]), src, v(cct), ALU.mult).then_inc(p2_ev[1], 1)
                    dve.wait_ge(p2_ev[1], 3 * j + 1)
                    us_new = uu[:, 2 + S:2 + TOK].rearrange("p (b t) -> p b t", t=TS)
                    link(dve.tensor_copy(us[:, :, 0:2], vcol[:, j, 13:29].rearrange("p (b r) -> p b r", r=2)))
                    link(dve.tensor_copy(us[:, :, 2:6], us_new))
                    link(dve.tensor_copy(tail[:, 0:2], uu[:, S:2 + S]))
                    dve.tensor_copy(tail[:, 2:18].rearrange("p (b r) -> p b r", r=2), us_new[:, :, 2:4]).then_inc(tail_rdy, 1)
                    ys = yy[:, S:TOK].rearrange("p (b t) -> p b t", t=TS)
                    link(dve.tensor_scalar(yy[:, 0:S], uu[:, 2:2 + S], vcol[:, j, 12:13], None, ALU.mult))
                    link(dve.tensor_scalar(ys, us[:, :, 2:6], vcol[:, j, 12:13], None, ALU.mult))
                    for r in (1, 0):
                        link(dve.scalar_tensor_tensor(yy[:, 0:S], uu[:, r:r + S], vcol[:, j, 10 + r:11 + r], yy[:, 0:S], ALU.mult, ALU.add))
                        link(dve.scalar_tensor_tensor(ys, us[:, :, r:r + TS], vcol[:, j, 10 + r:11 + r], ys, ALU.mult, ALU.add))
                elif kind == BC:
                    dve.wait_ge(p2_mm, n + 1)
                    dve.tensor_tensor(v(yy), src, v(yy), ALU.mult).then_inc(p2_ev[0], 1)
                    dve.wait_ge(p2_ev[0], 3 * j + 2)
                elif kind == ZC:
                    dve.wait_ge(p2_ev[1], 3 * j + 2)
                    if j:
                        dve.wait_ge(ych_st, 16 * j)
                    dve.tensor_tensor(ych[:, :], yy[:, :], zt[:, :], ALU.mult).then_inc(y_rdy, 1)
                    dve.wait_ge(tail_t, j + 1)
                    dve.tensor_copy(tailr[:, j * P:(j + 1) * P], PS[0:18, 6, 0:P]).then_inc(tail_ev, 1)
                elif kind == QQ:
                    dve.wait_ge(q_hi, j + 1)
                    if j:
                        dve.wait_ge(q_st, 64 * j)
                    link(dve.tensor_scalar(qs[:, j, :], PS[:, 5, CH - SAMP:CH], 0.125, None, ALU.mult))
                    dve.scalar_tensor_tensor(v(qlo), src, 0.125, f32(v(qhi)), ALU.mult, ALU.subtract).then_inc(p2_ev[1], 1)

            split(0, 0, True)
            for j in range(8):
                for kind in range(NK):
                    if not (j == 7 and kind == NK - 1):
                        jn, kn = (j, kind + 1) if kind + 1 < NK else (j + 1, 0)
                        split(jn, kn, j == 0 and kind == 0)
                    ev(j, kind)
            for c in range(2):
                for m in range(32):
                    dve.wait_ge(x3_t, 64 * c + 2 * m + 1)
                    if 32 * c + m >= 2:
                        dve.wait_ge(x3_mm, 32 * c + m - 1)
                    bank = (2 * m) % 4
                    for g in range(NG):
                        ins = dve.tensor_copy(xt[m % 2][0:64, g, :], PS[64 * g:64 * g + 64, bank, 0:CB])
                    ins.then_inc(xe[0], 1)
                dve.wait_ge(x3_mm, 32 * (c + 1))
                dve.tensor_copy(pebias[:, c:c + 1], PS[:, 4, CB - 1:CB]).then_inc(pe_rdy, 1)
                if c == 0:
                    dve.wait_ge(c3_mm, 1)
                    dve.wait_ge(c3_hi, 1)
                    dve.tensor_copy(kcs[:, :], PS[:, 6, 0:2 * P]).then_inc(c3_ev, 1)
                    dve.tensor_tensor(kcp[:, :, NPB:2 * NPB], PS[:, 7, 0:2 * NPB].rearrange("p (g n) -> p g n", g=NG), f32(kcp[:, :, 0:NPB]), ALU.subtract).then_inc(c3_ev, 1)
                else:
                    dve.wait_ge(c3_mm, 2)
                    dve.wait_ge(c3_hi, 2)
                    for q in range(2):
                        dve.tensor_copy(vcs[:, 4 * q:4 * q + 4, :], PS[0:NSB, 6 + q, :].rearrange("p (b c) -> p b c", c=DKV)).then_inc(c3_ev, 1)
                    dve.tensor_tensor(vcp[0:NPB, :, 64:128], PS[0:NPB, 4, 0:P].rearrange("p (g d) -> p g d", g=NG), f32(vcp[0:NPB, :, 0:64]), ALU.subtract).then_inc(c3_ev, 1)
            dve.wait_ge(c3_mm, 2)
            for n, (v, col) in enumerate(((vsx, C_VS), (vwx, C_VW))):
                dve.wait_ge(vb_hi, n + 1)
                dve.tensor_tensor(v[:, :, :, 64:128], kvt[:, 0:8, col:col + DKV].rearrange("p t (g d) -> p t g d", g=NG), f32(v[:, :, :, 0:64]), ALU.subtract).then_inc(vb_lo, 1)
            dve.wait_ge(c4_ld, 64)
            dve.wait_ge(pad0, 2)
            dve.wait_ge(sg_rdy, 2)

            dve.wait_ge(kt_t, 4)
            dve.wait_ge(vb_lo, 2)

            def near_low(h0, h1):
                dve.tensor_tensor(nearl[:, h0:h1, :], nearr[:, h0:h1, :], f32(near[:, h0:h1, :]), ALU.subtract).then_inc(vb_lo, 1)

            def keys_low(a):
                kh, kl = ((ksh, ksl), (kwh, kwl))[a]
                for half in range(2):
                    dve.wait_ge(kt_hi, 2 * a + half + 1)
                    cols = slice(512 * half, 512 * half + 512)
                    for g in range(NG):
                        for r in range(2):
                            rr = slice(64 * r, 64 * r + 64)
                            ins = dve.tensor_tensor(kl[rr, g, cols], PS[64 * g:64 * g + 64, 4 * a + half, :], f32(kh[rr, g, cols]), ALU.subtract)
                    ins.then_inc(kt_lo, 1)

            dve.wait_ge(vb_hi, 5)
            near_low(0, 4)
            keys_low(0)
            link(dve.memset(qbd[:, :, :], 0.0))
            for g in range(NG):
                half = slice(64 * g, 64 * g + 64)
                ins = dve.tensor_copy(qbd[half, :, 32 * g:32 * g + 32].rearrange("p b (j t) -> p b j t", t=TS),
                                      qs[half, :, :].rearrange("p j (b t) -> p b j t", t=TS))
            ins.then_inc(q5_rdy, 1)

            def maxima(w, h):
                n, u = 4 * w + h, w // 2
                g, hs, i = unit(u)
                dve.wait_ge(s_mm, n + 1)
                if h == 0 and w >= 3 and ON_ACT[(w - 3) % 2]:
                    dve.wait_ge(n_act, (w - 2) if ACT_A and ACT_B else (w - 3) // 2 + 1)
                k, parts = keys_of(w)
                b0, r = 2 * (n % 2), w % 3
                if w % 2 and h == 0:
                    if w >= 3:
                        dve.wait_ge(t_mm, tile0[w - 2])
                    link(dve.memset(prc[r][:, :, 0:NPB], 0.0))
                both = w % 2 and h == 3
                if both:
                    if u:
                        dve.wait_ge(ec_done, u)
                    dve.tensor_reduce(cs[:, :, :], PS[:, b0 + 1, 384:512].rearrange("p (h a n) -> p h n a", h=4, a=2), AX.X, ALU.add).then_inc(dch, 1)
                    chain.n += 1
                dve.tensor_reduce(nm[:, r, h:h + 1], PS[:, b0:b0 + len(parts), 0:parts[0]], AX.XY, ALU.max, negate=True).then_inc(m_rdy, 1)
                if both:
                    dve.wait_ge(dch, chain.n)
                    m0, head = max(0, 2 * i - 2), HPG * g + 4 * hs
                    cb = 2 * i + 2 - m0
                    row = tcmp[:, 2 * i - m0 + 1, head:head + 1]
                    tab = bass.AP(row.tensor, row.offset, [list(row.ap[0]), [1, 4], [-NH, cb]])
                    link(dve.tensor_tensor(cs[:, :, m0:m0 + cb], cs[:, :, m0:m0 + cb], tab, ALU.add))
                    link(dve.tensor_reduce(nm[:, r, 4:8], cs[:, :, 0:2 * i + 2], AX.X, ALU.max, negate=True))
                    dve.tensor_tensor(cs[:, :, 0:2 * i + 2], cs[:, :, 0:2 * i + 2], ext(nm[:, r, 4:8], (0, 2 * i + 2)), ALU.add).then_inc(mc_rdy, 1)

            def factors(w):
                g, hs, i = unit(w // 2)
                c0_ = HPG * g + 4 * hs
                dve.wait_ge(e_done, 4 * w + 4)
                m, r = (8 if w % 2 else 4), w % 3
                if w % 2:
                    dve.wait_ge(ec_done, w // 2 + 1)
                    link(dve.tensor_reduce(rsum[:, r, 4:8], prc[r][:, :, 0:2 * i + 2], AX.X, ALU.add))
                link(dve.reciprocal(rrec[:, r, 0:m], rsum[:, r, 0:m]))
                if w % 2 == 0:
                    dve.tensor_tensor(rg[:, r, 0:4], rrec[:, r, 0:4], sg[:, i, NH + c0_:NH + c0_ + 4], ALU.mult).then_inc(r_rdy, 1)
                else:
                    if i == 0:
                        link(dve.tensor_scalar(rrec[:, r, 4:8], rrec[:, r, 4:8], anyc[:, :], None, ALU.mult))
                    link(dve.tensor_tensor(rg[:, r, 4:8], rrec[:, r, 4:8], sg[:, i, c0_:c0_ + 4], ALU.mult))
                    dve.tensor_tensor(rg[:, r, 0:4], rrec[:, r, 0:4], sg[:, i, 2 * NH + c0_:2 * NH + c0_ + 4], ALU.mult).then_inc(r_rdy, 1)
                    dve.tensor_tensor(prc[r][:, :, 0:2 * i + 2], prc[r][:, :, 0:2 * i + 2], ext(rg[:, r, 4:8], (0, 2 * i + 2)), ALU.mult)

            def scale(w, h):
                dve.wait_ge(r_rdy, w + 1)
                if h not in ON_ACT[w % 2]:
                    k, r = keys_of(w)[0], w % 3
                    ins = dve.tensor_scalar(pr[r][:, h, 0:k], pr[r][:, h, 0:k], rg[:, r, h:h + 1], None, ALU.mult)
                    if h == max(set(range(4)) - ON_ACT[w % 2]):
                        ins.then_inc(n_dve, 1)

            def low(w, t):
                tc = tile0[w] + t
                dve.wait_ge(pt_hi, tc + 1)
                if tc >= 2:
                    dve.wait_ge(pv_mm, tc - 1)
                dve.tensor_tensor(ptl[tc % 2][:, :], PS[:, 4 + tc % 2, :], f32(pth[tc % 2][:, :]), ALU.subtract).then_inc(pt_lo, 1)

            def gate_o(u):
                g, hs, i = unit(u)
                half = slice(64 * g, 64 * g + 64)
                dve.wait_ge(r_mm, u + 1)
                dve.wait_ge(za_ld[u % 2], 16 * (u // 2 + 1))
                if u >= 2:
                    dve.wait_ge(mix_st[u % 2], 16 * (u // 2))
                dve.tensor_tensor(mixs[u % 2][half, :, :], PS[half, 7, :].rearrange("p (j c) -> p j c", j=4), zau[u % 2][half, :, :], ALU.mult).then_inc(r_ev, 1)

            for w in range(2):
                for h in range(4):
                    maxima(w, h)
                if w == 0:
                    keys_low(1)
                    factors(0)
                    dve.wait_ge(vb_hi, 6)
                    near_low(4, NH)
            for h in range(4):
                scale(0, h)
            behind = None
            for w in range(NI):
                for h, part in enumerate(slots(w)):
                    for t in part or [None]:
                        if t is not None:
                            if behind:
                                low(*behind)
                            behind = (w, t)
                        if t in (None, part.start) and w + 2 < NI:
                            maxima(w + 2, h)
                    if w + 1 < NI:
                        if h == 1:
                            factors(w + 1)
                        for hh in ((), (0, 1), (2, 3), ())[h]:
                            scale(w + 1, hh)
                    if h == 3 and w % 2 == 0 and w:
                        gate_o(w // 2 - 1)
            low(*behind)
            gate_o(NU - 1)
            dve.wait_ge(pv_mm, tile0[NI])
            dve.wait_ge(r_mm, NU)
            dve.wait_ge(mix_st[0], 16 * NU // 2)
            dve.wait_ge(mix_st[1], 16 * NU // 2)
            dve.wait_ge(c5_ld, 16 * 10)
            dve.wait_ge(gr_ld, 16 * 32)

            def wo_low(j):
                dve.wait_ge(wo_hi, j + 1)
                dve.tensor_tensor(wol[j][:, :], wor[j % 2][:, :], f32(woh[j][:, :]), ALU.subtract).then_inc(wo_lo, 1)

            def choose(pq):
                dve.wait_ge(s5c_mm, pq + 1)
                link(dve.tensor_copy(cm[:, :], PS[:, 5, 64:96]))
                dve.sem_inc(b5_rd, 1)
                link(dve.tensor_tensor(cm[:, 30:32], cm[:, 30:32], nbc[:, :], ALU.add))
                dve.tensor_reduce(n5[:, 2:3], cm[:, :], AX.X, ALU.max, negate=True).then_inc(m5c, 1)
                dve.wait_ge(e5c, pq + 1)
                link(dve.reciprocal(i5[:, 2:3], r5[:, 2:3]))
                dve.tensor_scalar(pn[:, :], cm[:, :], i5[:, 2:3], None, ALU.mult).then_inc(pn_rdy, 1)
                dve.wait_ge(pn_rdy, pq + 1)
                for j in early(pq - 1) if pq else ():
                    wo_low(j)
                dve.wait_ge(s5_mm, pq + 1)
                if pq >= 2:
                    dve.wait_ge(o5_mm, pq - 1)
                s = s5[pq % 2]
                dve.tensor_tensor(s[:, PAST:SEL], PS[:, 5, 0:SAMP], nbnew[:, pq, :], ALU.add)
                link(dve.tensor_tensor(s[:, SEL + WIN:SEL + WN], PS[:, 5, SAMP:2 * SAMP], nbnew[:, pq, :], ALU.add))
                dve.sem_inc(b5_rd, 1)
                dve.wait_ge(imp_mm, pq + 1)
                link(dve.tensor_copy(imp[:, :], PS[:, 5, 96:128]))
                dve.sem_inc(b5_rd, 1)
                v = imp[:, :]
                other = bass.AP(v.tensor, v.offset, [list(v.ap[0]), [0, NSB], [1, NSB]])
                own = ext(v, (0, NSB))
                link(dve.tensor_tensor(gt[:, :, :], other, own, ALU.is_gt))
                link(dve.tensor_tensor(eq[:, :, :], other, own, ALU.is_equal))
                link(dve.tensor_tensor(eq[:, :, :], eq[:, :, :], before[:, :, :], ALU.mult))
                link(dve.tensor_tensor(gt[:, :, :], gt[:, :, :], eq[:, :, :], ALU.add))
                link(dve.tensor_reduce(rank[:, :], gt[:, :, :], AX.X, ALU.add))
                link(dve.tensor_scalar(bmask[:, :], rank[:, :], 14.5, NEG, ALU.is_ge, ALU.mult))

            def pair_rows(pq):
                s = s5[pq % 2]
                m = bmask[:, :]
                sel = s[:, 0:PAST].rearrange("p (i a b) -> p i a b", i=NSEL, b=4)
                link(dve.tensor_tensor(sel, PS[:, 0:4, :].rearrange("p k (i a b) -> p (k i) a b", a=32, b=4),
                                       bass.AP(m.tensor, m.offset, [list(m.ap[0]), [0, NSEL], [1, NSB], [0, 4]]), ALU.add))
                n8 = s[:, 0:PAST].rearrange("p (i c) -> p i c", i=NSEL)[:, :, 120:128]
                link(dve.tensor_tensor(n8, n8, nb[:, :].rearrange("p (c i) -> p i c", i=NSEL), ALU.add))
                link(dve.tensor_copy(s[:, SEL:SEL + WIN], PS[:, 4, :]))
                n32 = s[:, SEL:SEL + WIN].rearrange("p (i c) -> p i c", i=NWIN)
                link(dve.tensor_tensor(n32[:, :, 96:128], n32[:, :, 96:128], nb[:, :].rearrange("p (c i) -> p i c", i=NWIN), ALU.add))
                dve.tensor_tensor(n32[:, :, 0], n32[:, :, 0], wedge[:, :], ALU.add).then_inc(s5_ev, 1)
                dve.wait_ge(s5_ev, pq + 1)
                dve.tensor_reduce(n5[:, 0:1], s[:, 0:SEL], AX.X, ALU.max, negate=True)
                dve.tensor_reduce(n5[:, 1:2], s[:, SEL:SEL + WN], AX.X, ALU.max, negate=True).then_inc(m5, 1)

            def scale_rows(pq):
                s = s5[pq % 2]
                dve.wait_ge(e5, pq + 1)
                link(dve.reciprocal(i5[:, 0:2], r5[:, 0:2]))
                link(dve.tensor_tensor(i5[:, 0:2], i5[:, 0:2], gr[:, pq, 1:3], ALU.mult))
                dve.tensor_scalar(s[:, 0:SEL], s[:, 0:SEL], i5[:, 0:1], None, ALU.mult)
                dve.tensor_scalar(cmg[:, :], pn[:, :], gr[:, pq, 0:1], None, ALU.mult)
                dve.tensor_scalar(s[:, SEL:SEL + WN], s[:, SEL:SEL + WN], i5[:, 1:2], None, ALU.mult).then_inc(p5, 1)

            def gate_rows(pq):
                dve.wait_ge(ot_t, pq + 1)
                for g in range(NG):
                    half = slice(64 * g, 64 * g + 64)
                    for b2 in range(2):
                        b = 2 * pq + b2
                        c0_ = 256 + 64 * b2 + 32 * g
                        ins = dve.tensor_tensor(mix5[half, :, TS * b:TS * b + TS], PS[half, 5, c0_:c0_ + 32].rearrange("p (j t) -> p j t", t=TS),
                                                zas[half, :, TS * b:TS * b + TS], ALU.mult)
                ins.then_inc(mix5_rdy, 1)
                dve.wait_ge(mix5_rdy, pq + 1)
                dve.sem_inc(b5_rd, 1)

            def key_copies(pq):
                if pq:
                    dve.wait_ge(s5_mm, pq)
                n0 = 10 * pq + 6 * max(0, pq - 1)
                for m in (5, 7, 9):
                    n = n0 + m
                    dve.wait_ge(t5, n + 1)
                    dve.tensor_copy(kt5[m // 5][:, m % 5 * 4:m % 5 * 4 + 4, :], PS[:, 6 + n % 2, :].rearrange("p (a c) -> p a c", a=4)).then_inc(ev5d, 1)

            key_copies(0)
            choose(0)
            pair_rows(0)
            scale_rows(0)
            for pq in range(4):
                if pq < 3:
                    key_copies(pq + 1)
                    choose(pq + 1)
                    pair_rows(pq + 1)
                if pq == 3:
                    dve.wait_ge(t5, keys_turned(NB - 1, True))
                    for j in early(3):
                        wo_low(j)
                gate_rows(pq)
                if pq < 3:
                    scale_rows(pq + 1)
            dve.wait_ge(o5_mm, 4)

            def mix_low(tt):
                n = rows_of(tt)
                for a in range(2):
                    dve.wait_ge(m_hi, 2 * tt + a + 1)
                    ks = slice(8 * a, 8 * a + 8)
                    dve.tensor_tensor(ml[:, ks, 0:n], mr[:, ks, 0:n], f32(mh[:, ks, 0:n]), ALU.subtract).then_inc(m_lo, 1)

            mix_low(0)
            for j in range(8, 16):
                wo_low(j)
            dve.wait_ge(c6_ld, 32)
            for tt in range(NTT):
                n, b0 = rows_of(tt), 2 * (tt % 4)
                if tt + 1 < NTT:
                    mix_low(tt + 1)
                dve.wait_ge(y_mm, 2 * tt + 2)
                if tt:
                    dve.wait_ge(y_act, 2 * tt)
                    dve.wait_ge(y_out, tt)
                out = PS[0:n, b0:b0 + 2, :].rearrange("p a b -> p (a b)")
                if tt == NTT - 1:
                    dve.wait_ge(c6_ld, 48)
                dve.tensor_tensor(yf[0:n, :], out, gbc[0:n, :], ALU.mult).then_inc(y_ev, 1)
                dve.wait_ge(y_ev, tt + 1)
                dve.wait_ge(xf_ld[tt % 2], 16 * (tt // 2 + 1))
                dve.tensor_tensor(yf[0:n, :], yf[0:n, :], xf[tt % 2][0:n, :], ALU.add).then_inc(y_sum, 1)
                dve.wait_ge(y_act, 2 * tt + 1)
                dve.tensor_scalar(s6[0:n, 1:2], s6[0:n, 0:1], 1.0 / D, EPS, ALU.mult, ALU.add).then_inc(y_ms, 1)
                dve.wait_ge(y_act, 2 * tt + 2)
                link(dve.reciprocal(s6[0:n, 3:4], s6[0:n, 2:3]))
                dve.scalar_tensor_tensor(yo[0:n, :], yf[0:n, :], s6[0:n, 3:4], fgb[0:n, :], ALU.mult, ALU.mult).then_inc(y_out, 1)


_INS = ['x_prompt', 'x_sample', 'cache_k_cmp', 'cache_v_cmp', 'cache_k_slc', 'cache_v_slc',
        'cache_k_win', 'cache_v_win', 'state_conv', 'page_table', 'c_prompt', 'c_sample', 'ada_w',
        'ada_b', 'norm_g', 'w_in', 'cmp_pe_k', 'cmp_w1_k', 'cmp_w2_k', 'cmp_pe_v', 'cmp_w1_v',
        'cmp_w2_v', 'conv_w', 'w_out', 'rel_bias', 'final_g']
_KV = (1, 1, 1024, 2, 64)
_OUTS = {
    'y_prompt': (1, 1024, 1024), 'y_sample': (8, 4, 1024),
    'p_kc': _KV, 'p_vc': _KV, 'p_ks': _KV, 'p_vs': _KV, 'p_kw': (1, 1, 512, 2, 64), 'p_vw': (1, 1, 512, 2, 64),
    'p_cv': (1, 1, 2, 1024),
    's_kc': (1, 8, 4, 2, 64), 's_vc': (1, 8, 4, 2, 64), 's_ks': (1, 8, 4, 2, 64), 's_vs': (1, 8, 4, 2, 64),
    's_kw': (1, 8, 512, 2, 64), 's_vw': (1, 8, 512, 2, 64), 's_cv': (1, 8, 2, 1024),
}


def constants():
    import math

    import numpy as np

    def bucket(n):
        n = np.asarray(n)
        m = np.maximum(n, 0)
        f = np.maximum(m, 16).astype(np.float32)
        large = 16 + (np.log(f / np.float32(16)) / np.float32(math.log(8.0)) * np.float32(16)).astype(np.int32)
        b = np.where(m < 16, m, np.minimum(large, 31))
        one = np.zeros((33, *n.shape), np.float32)
        np.put_along_axis(one, np.where(n < 0, 32, b)[None], 1.0, axis=0)
        return one

    i = np.arange(128)
    return {
        'k_ident': np.eye(128, dtype=np.float32),
        'k_stack2': np.concatenate([np.eye(64, dtype=np.float32)] * 2),
        'k_group': ((i[:, None] // 32 == i[None] // 32) & (i[:, None] % 4 == i[None] % 4)).astype(np.float32),
        'k_before': np.tril(np.ones((32, 32), np.float32), -1).reshape(1, 1024),
        'k_row': bucket(255 - np.arange(384)),
        'k_cmpd': bucket(64 * np.arange(-1, 3)[:, None] + i[None] - 63),
        'k_edge': np.where(i[None] >= i[:, None], 0.0, NEG).astype(np.float32),
        'k_wedge': np.where(np.arange(4)[None] >= i[:, None] % 4, 0.0, NEG).astype(np.float32),
        'k_any': (i[:, None] >= 63).astype(np.float32),
    }


def kernel(**inputs):
    import numpy as _np
    import concourse.bacc as _bacc
    from concourse import mybir as _mybir
    from concourse.bass_utils import run_bass_kernel_spmd as _run

    nc = _bacc.Bacc("TRN2", target_bir_lowering=False, num_devices=1)
    arrays, args = {}, {}
    for name, a in [*((n, inputs[n]) for n in _INS), *constants().items()]:
        a = _np.ascontiguousarray(a)
        arrays[f"in_{name}"] = a
        args[name] = nc.dram_tensor(f"in_{name}", a.shape, _mybir.dt.from_np(a.dtype), kind="ExternalInput").ap()
    for name, shape in _OUTS.items():
        args[name] = nc.dram_tensor(f"out_{name}", shape, F32, kind="ExternalOutput").ap()
    build(nc, **args)
    r = _run(nc, [arrays], core_ids=[0])
    return tuple(r.results[0][f"out_{name}"] for name in _OUTS)
```
